# Optimizing a Trainium2 kernel written in Bass

```python
import math
import jax
import jax.numpy as jnp
from jax import lax
import numpy as np
import jax, jax.numpy as jnp

D_MODEL = 1024
BATCH = 1
SEQ = 512
DEPTH = 1

CTX_LEN = 256
GRID_W = 64

ATTN_HEADS = 8
ATTN_KV_HEADS = 2
ATTN_GROUP = ATTN_HEADS // ATTN_KV_HEADS
HEAD_DIM = 128
ROPE_AXIS_DIM = HEAD_DIM // 2
ROPE_THETA = 10000.0
Q_BLOCK = 128

GDN_HEADS = 8
GDN_DK = 128
GDN_DV = 128
GDN_CHUNK = 64
SHORT_CONV = 3

D_FF = 2816
FFN_CONV = 3

NORM_EPS = 1e-6

ATTN_Q_W = ATTN_HEADS * HEAD_DIM
ATTN_KV_W = ATTN_KV_HEADS * HEAD_DIM
GDN_QK_W = GDN_HEADS * GDN_DK
GDN_V_W = GDN_HEADS * GDN_DV
GDN_CONV_W = 2 * GDN_QK_W + GDN_V_W
IN_SPLITS = (ATTN_KV_W, ATTN_KV_W, GDN_CONV_W, 2 * GDN_HEADS, 2 * GDN_HEADS, ATTN_Q_W, GDN_V_W, 2 * D_MODEL)
CTX_COLS = 2 * ATTN_KV_W + GDN_CONV_W + 4 * GDN_HEADS
IN_COLS = CTX_COLS + ATTN_Q_W + GDN_V_W + 2 * D_MODEL


def rms_norm(x, gain=None):
    x32 = x.astype(jnp.float32)
    y = x32 * lax.rsqrt(jnp.mean(x32 * x32, axis=-1, keepdims=True) + NORM_EPS)
    if gain is not None:
        y = y * gain.astype(jnp.float32)
    return y.astype(x.dtype)

def l2_normalize(x):
    return x * lax.rsqrt(jnp.sum(x * x, axis=-1, keepdims=True) + NORM_EPS)

def modulate(h, shift, scale):
    return h * (1.0 + scale) + shift

def split_cols(p):
    parts, off = [], 0
    for size in IN_SPLITS:
        if off >= p.shape[-1]:
            break
        parts.append(p[..., off:off + size])
        off += size
    return parts

def dwconv_centred(x, w, b=None):
    width = w.shape[0]
    pad = width // 2
    n = x.shape[1]
    xp = jnp.pad(x, ((0, 0), (pad, pad), (0, 0)))
    y = xp[:, 0:n] * w[0]
    for j in range(1, width):
        y = y + xp[:, j:j + n] * w[j]
    return y if b is None else y + b

def axial_rope_tables(n):
    rows = n // GRID_W
    row_ids = jnp.broadcast_to(jnp.arange(rows, dtype=jnp.float32)[:, None], (rows, GRID_W)).reshape(n)
    col_ids = jnp.broadcast_to(jnp.arange(GRID_W, dtype=jnp.float32)[None, :], (rows, GRID_W)).reshape(n)
    inv_freq = ROPE_THETA ** (-jnp.arange(0, ROPE_AXIS_DIM, 2, dtype=jnp.float32) / ROPE_AXIS_DIM)
    ang = jnp.concatenate([row_ids[:, None] * inv_freq, col_ids[:, None] * inv_freq], axis=-1)
    ang = ang.reshape(n, 2, ROPE_AXIS_DIM // 2)
    return jnp.cos(ang), jnp.sin(ang)

def apply_axial_rope(x, cos, sin):
    x32 = x.astype(jnp.float32).reshape(*x.shape[:-1], 2, 2, ROPE_AXIS_DIM // 2)
    x1, x2 = x32[..., 0, :], x32[..., 1, :]
    cos = cos[None, :, None]
    sin = sin[None, :, None]
    out = jnp.stack([x1 * cos - x2 * sin, x2 * cos + x1 * sin], axis=-2)
    return out.reshape(x.shape).astype(x.dtype)

def sdpa_block(q, k, v):
    s = jnp.einsum('bqhgd,bkhd->bhgqk', q, k).astype(jnp.float32) * (HEAD_DIM ** -0.5)
    p = jax.nn.softmax(s, axis=-1).astype(v.dtype)
    return jnp.einsum('bhgqk,bkhd->bqhgd', p, v)

def latent_attention(q, k_all, v_all):
    b, n = q.shape[:2]
    nb = n // Q_BLOCK
    qb = jnp.moveaxis(q.reshape(b, nb, Q_BLOCK, *q.shape[2:]), 1, 0)
    o = lax.map(lambda q_blk: sdpa_block(q_blk, k_all, v_all), qb)
    return jnp.moveaxis(o, 0, 1).reshape(b, n, ATTN_Q_W)

def gdn_chunked(q, k, v, log_a, beta, s0, with_output):
    b, h, n, dk = q.shape
    dv = v.shape[-1]
    nc = n // GDN_CHUNK
    q = q.reshape(b, h, nc, GDN_CHUNK, dk)
    k = k.reshape(b, h, nc, GDN_CHUNK, dk)
    v = v.reshape(b, h, nc, GDN_CHUNK, dv)
    log_a = log_a.reshape(b, h, nc, GDN_CHUNK)
    beta = beta.reshape(b, h, nc, GDN_CHUNK)
    gam = jnp.cumsum(log_a, axis=-1)
    idx = jnp.arange(GDN_CHUNK)
    strict = idx[:, None] > idx[None, :]
    incl = idx[:, None] >= idx[None, :]
    dec = jnp.exp(jnp.where(incl, gam[..., :, None] - gam[..., None, :], -jnp.inf))
    kk = jnp.einsum('bhncd,bhnsd->bhncs', k, k)
    a_mat = jnp.where(strict, beta[..., :, None] * dec * kk, 0.0) + jnp.eye(GDN_CHUNK, dtype=jnp.float32)
    rhs = jnp.concatenate([beta[..., None] * v, (beta * jnp.exp(gam))[..., None] * k], axis=-1)
    uw = lax.linalg.triangular_solve(a_mat, rhs, left_side=True, lower=True, unit_diagonal=True)
    u, w = uw[..., :dv], uw[..., dv:]
    k_dec = k * jnp.exp(gam[..., -1:] - gam)[..., None]
    g_last = jnp.exp(gam[..., -1])
    xs = [u, w, k_dec, g_last]
    if with_output:
        q_dec = q * jnp.exp(gam)[..., None]
        p = dec * jnp.einsum('bhncd,bhnsd->bhncs', q, k)
        xs = xs + [q_dec, p]
    xs = tuple(jnp.moveaxis(t, 2, 0) for t in xs)

    def step(s, inp):
        u_c, w_c, kd_c, gl_c = inp[:4]
        delta = u_c - jnp.einsum('bhcd,bhde->bhce', w_c, s)
        s_new = gl_c[..., None, None] * s + jnp.einsum('bhcd,bhce->bhde', kd_c, delta)
        if with_output:
            qd_c, p_c = inp[4], inp[5]
            o = jnp.einsum('bhcd,bhde->bhce', qd_c, s) + jnp.einsum('bhcs,bhse->bhce', p_c, delta)
            return s_new, o
        return s_new, None

    s_fin, o = lax.scan(step, s0, xs)
    if with_output:
        o = jnp.moveaxis(o, 0, 2).reshape(b, h, n, dv)
    return o, s_fin

def gdn_prepare(qkv, db, da, conv_w, a_log, dt_bias):
    b, n, _ = qkv.shape
    qkv = jax.nn.silu(dwconv_centred(qkv, conv_w)).astype(jnp.float32)
    q, k, v = jnp.split(qkv, [GDN_QK_W, 2 * GDN_QK_W], axis=-1)
    q = l2_normalize(q.reshape(b, n, GDN_HEADS, GDN_DK)) * (GDN_DK ** -0.5)
    k = l2_normalize(k.reshape(b, n, GDN_HEADS, GDN_DK))
    v = v.reshape(b, n, GDN_HEADS, GDN_DV)
    q, k, v = (t.transpose(0, 2, 1, 3) for t in (q, k, v))
    beta = jax.nn.sigmoid(db.astype(jnp.float32)).reshape(b, n, 2, GDN_HEADS).transpose(2, 0, 3, 1)
    da = da.astype(jnp.float32).reshape(b, n, 2, GDN_HEADS).transpose(2, 0, 3, 1)
    log_a = -jnp.exp(a_log.astype(jnp.float32))[:, None, :, None] * jax.nn.softplus(
        da + dt_bias.astype(jnp.float32)[:, None, :, None])
    return q, k, v, log_a, beta

def gdn_bidirectional(ctx_in, lat_in, with_ctx_output):
    qc, kc, vc, lac, bc = ctx_in
    ql, kl, vl, lal, bl = lat_in
    s0 = jnp.zeros((ql.shape[0], GDN_HEADS, GDN_DK, GDN_DV), jnp.float32)
    o_lat, o_ctx = None, None
    for d in range(2):
        rev = (lambda t: jnp.flip(t, axis=2)) if d == 1 else (lambda t: t)
        oc, sc = gdn_chunked(rev(qc), rev(kc), rev(vc), rev(lac[d]), rev(bc[d]), s0, with_ctx_output)
        ol, _ = gdn_chunked(rev(ql), rev(kl), rev(vl), rev(lal[d]), rev(bl[d]), sc, True)
        o_lat = rev(ol) if o_lat is None else o_lat + rev(ol)
        if with_ctx_output:
            o_ctx = rev(oc) if o_ctx is None else o_ctx + rev(oc)
    return o_lat, o_ctx

def gdn_output(o, z, norm_w):
    b, n = z.shape[:2]
    o = rms_norm(o.transpose(0, 2, 1, 3), norm_w)
    y = o * jax.nn.silu(z.astype(jnp.float32).reshape(b, n, GDN_HEADS, GDN_DV))
    return y.reshape(b, n, GDN_V_W).astype(z.dtype)

def merge_branches(attn, gdn, gates, w_pa, w_pd, w_out):
    g_a, g_d = jnp.split(gates, 2, axis=-1)
    y = jax.nn.sigmoid(g_a) * (attn @ w_pa) + jax.nn.sigmoid(g_d) * (gdn @ w_pd)
    return y @ w_out

def conv_ffn(h, w_up, conv_w, conv_b, w_down):
    u = dwconv_centred(h @ w_up, conv_w, conv_b)
    g, val = jnp.split(u, 2, axis=-1)
    return (jax.nn.silu(g) * val) @ w_down

def hybrid_layer(x, ctx, c, c_ctx, w_mod, b_mod, w_in, q_norm_w, k_norm_w, conv_qkv_w, a_log, dt_bias,
                 gdn_norm_w, w_pa, w_pd, w_out, w_up, ffn_conv_w, ffn_conv_b, w_down, update_ctx):
    b, n, _ = x.shape
    cl = ctx.shape[1]
    mod_lat = jax.nn.silu(c) @ w_mod + b_mod
    mod_ctx = jax.nn.silu(c_ctx) @ w_mod + b_mod
    sh1, sc1, g1, sh2, sc2, g2 = [m[:, None, :] for m in jnp.split(mod_lat, 6, axis=-1)]
    csh1, csc1, cg1, csh2, csc2, cg2 = jnp.split(mod_ctx, 6, axis=-1)

    hx = modulate(rms_norm(x), sh1, sc1)
    hc = modulate(rms_norm(ctx), csh1, csc1)
    ak_x, av_x, qkv_x, db_x, da_x, aq_x, z_x, gate_x = split_cols(hx @ w_in)
    ak_c, av_c, qkv_c, db_c, da_c, *rest_c = split_cols(hc @ (w_in if update_ctx else w_in[:, :CTX_COLS]))

    cos, sin = axial_rope_tables(n)
    q_x = apply_axial_rope(rms_norm(aq_x.reshape(b, n, ATTN_HEADS, HEAD_DIM), q_norm_w), cos, sin)
    q_x = q_x.reshape(b, n, ATTN_KV_HEADS, ATTN_GROUP, HEAD_DIM)
    k_x = apply_axial_rope(rms_norm(ak_x.reshape(b, n, ATTN_KV_HEADS, HEAD_DIM), k_norm_w), cos, sin)
    v_x = av_x.reshape(b, n, ATTN_KV_HEADS, HEAD_DIM)
    k_c = rms_norm(ak_c.reshape(b, cl, ATTN_KV_HEADS, HEAD_DIM), k_norm_w)
    v_c = av_c.reshape(b, cl, ATTN_KV_HEADS, HEAD_DIM)
    attn_x = latent_attention(q_x, jnp.concatenate([k_c, k_x], axis=1), jnp.concatenate([v_c, v_x], axis=1))

    gdn_x_in = gdn_prepare(qkv_x, db_x, da_x, conv_qkv_w, a_log, dt_bias)
    gdn_c_in = gdn_prepare(qkv_c, db_c, da_c, conv_qkv_w, a_log, dt_bias)
    o_x, o_c = gdn_bidirectional(gdn_c_in, gdn_x_in, update_ctx)
    gdn_x = gdn_output(o_x, z_x, gdn_norm_w)

    x = x + g1 * merge_branches(attn_x, gdn_x, gate_x, w_pa, w_pd, w_out)
    x = x + g2 * conv_ffn(modulate(rms_norm(x), sh2, sc2), w_up, ffn_conv_w, ffn_conv_b, w_down)

    if update_ctx:
        aq_c, z_c, gate_c = rest_c
        q_c = rms_norm(aq_c.reshape(b, cl, ATTN_HEADS, HEAD_DIM), q_norm_w)
        q_c = q_c.reshape(b, cl, ATTN_KV_HEADS, ATTN_GROUP, HEAD_DIM)
        attn_c = sdpa_block(q_c, k_c, v_c).reshape(b, cl, ATTN_Q_W)
        gdn_c = gdn_output(o_c, z_c, gdn_norm_w)
        ctx = ctx + cg1 * merge_branches(attn_c, gdn_c, gate_c, w_pa, w_pd, w_out)
        ctx = ctx + cg2 * conv_ffn(modulate(rms_norm(ctx), csh2, csc2), w_up, ffn_conv_w, ffn_conv_b, w_down)
    return x, ctx

def first_inputs(seed: int = 0) -> dict:
    key = jax.random.key(seed)
    ks = jax.random.split(key, 22)
    f32 = jnp.float32

    def dense(k, shape, fan_in, s=1.0):
        return s * (fan_in ** -0.5) * jax.random.normal(k, shape, f32)

    dt = jnp.exp(jax.random.uniform(ks[10], (DEPTH, 2, GDN_HEADS), f32,
                                    minval=math.log(1e-3), maxval=math.log(1e-1)))
    return {
        'x': jax.random.normal(ks[0], (BATCH, SEQ, D_MODEL), f32),
        'c': jax.random.normal(ks[1], (BATCH, D_MODEL), f32),
        'ctx': jax.random.normal(ks[2], (BATCH, CTX_LEN, D_MODEL), f32),
        'c_ctx': jax.random.normal(ks[3], (D_MODEL,), f32),
        'w_mod': dense(ks[4], (DEPTH, D_MODEL, 6 * D_MODEL), D_MODEL, 0.5),
        'b_mod': 0.02 * jax.random.normal(ks[5], (DEPTH, 6 * D_MODEL), f32),
        'w_in': dense(ks[6], (DEPTH, D_MODEL, IN_COLS), D_MODEL),
        'q_norm_w': 1.0 + 0.05 * jax.random.normal(ks[7], (DEPTH, HEAD_DIM), f32),
        'k_norm_w': 1.0 + 0.05 * jax.random.normal(ks[8], (DEPTH, HEAD_DIM), f32),
        'conv_qkv_w': dense(ks[9], (DEPTH, SHORT_CONV, GDN_CONV_W), SHORT_CONV),
        'a_log': jnp.log(jax.random.uniform(ks[11], (DEPTH, 2, GDN_HEADS), f32, minval=1.0, maxval=16.0)),
        'dt_bias': dt + jnp.log(-jnp.expm1(-dt)),
        'gdn_norm_w': 1.0 + 0.05 * jax.random.normal(ks[12], (DEPTH, GDN_DV), f32),
        'w_pa': dense(ks[13], (DEPTH, ATTN_Q_W, D_MODEL), ATTN_Q_W),
        'w_pd': dense(ks[14], (DEPTH, GDN_V_W, D_MODEL), GDN_V_W),
        'w_out': dense(ks[15], (DEPTH, D_MODEL, D_MODEL), D_MODEL),
        'w_up': dense(ks[16], (DEPTH, D_MODEL, 2 * D_FF), D_MODEL),
        'ffn_conv_w': dense(ks[17], (DEPTH, FFN_CONV, 2 * D_FF), FFN_CONV),
        'ffn_conv_b': 0.02 * jax.random.normal(ks[18], (DEPTH, 2 * D_FF), f32),
        'w_down': dense(ks[19], (DEPTH, D_FF, D_MODEL), D_FF),
        'final_norm_w': 1.0 + 0.05 * jax.random.normal(ks[20], (D_MODEL,), f32),
    }

def first_block(x, c, ctx, c_ctx, w_mod, b_mod, w_in, q_norm_w, k_norm_w, conv_qkv_w, a_log, dt_bias,
              gdn_norm_w, w_pa, w_pd, w_out, w_up, ffn_conv_w, ffn_conv_b, w_down, final_norm_w):
    for layer in range(DEPTH):
        x, ctx = hybrid_layer(
            x, ctx, c, c_ctx, w_mod[layer], b_mod[layer], w_in[layer], q_norm_w[layer], k_norm_w[layer],
            conv_qkv_w[layer], a_log[layer], dt_bias[layer], gdn_norm_w[layer], w_pa[layer], w_pd[layer],
            w_out[layer], w_up[layer], ffn_conv_w[layer], ffn_conv_b[layer], w_down[layer],
            update_ctx=layer < DEPTH - 1)
    return rms_norm(x, final_norm_w)


DEPTH_2 = 2

CHUNK = 64
D_MIX = D_MODEL
POOL_WIDTH = D_MIX // 4
DIFF_WIDTH = D_MIX // 2
GLA_WIDTH = D_MIX // 4
POOL_WINDOWS = (2, 4, 8, 16)
POOL_GROUPS = len(POOL_WINDOWS)
POOL_GDIM = POOL_WIDTH // POOL_GROUPS
DIFF_HEADS = 4
DIFF_VDIM = DIFF_WIDTH // DIFF_HEADS
DIFF_QKDIM = DIFF_VDIM // 2
GLA_HEADS = 4
GLA_VDIM = GLA_WIDTH // GLA_HEADS
GLA_KDIM = GLA_VDIM // 2
GLA_GATE_RANK = 16
GLA_GATE_TAU = 16.0
D_FF_2 = 4 * D_MODEL
EPS = 1e-6

SIZES = (
    POOL_WIDTH,
    DIFF_HEADS * 2 * DIFF_QKDIM,
    DIFF_HEADS * 2 * DIFF_QKDIM,
    DIFF_HEADS * DIFF_VDIM,
    GLA_HEADS * GLA_KDIM,
    GLA_HEADS * GLA_KDIM,
    GLA_WIDTH,
    GLA_WIDTH,
    GLA_GATE_RANK,
)
D_IN_PROJ = sum(SIZES)
SPLIT_POINTS = tuple(sum(SIZES[:i + 1]) for i in range(len(SIZES) - 1))


def rms_norm_2(x, g):
    xf = x.astype(jnp.float32)
    y = xf * lax.rsqrt(jnp.mean(xf * xf, axis=-1, keepdims=True) + EPS)
    return (y * g.astype(jnp.float32)).astype(x.dtype)

def pool_mixer(u, w_pool, pool_scale):
    B, S, _ = u.shape
    uf = u.astype(jnp.float32).reshape(B, S, POOL_GROUPS, POOL_GDIM)
    csum = jnp.cumsum(uf, axis=1)
    t = jnp.arange(S)
    means = []
    for g, win in enumerate(POOL_WINDOWS):
        c = csum[:, :, g]
        c_prev = jnp.pad(c, ((0, 0), (win, 0), (0, 0)))[:, :S]
        cnt = jnp.minimum(t + 1, win).astype(jnp.float32)[None, :, None]
        means.append((c - c_prev) / cnt)
    pooled = jnp.stack(means, axis=2) - uf
    mixed = jnp.einsum('bsgc,gcd->bsgd', pooled, w_pool.astype(jnp.float32))
    return (mixed.reshape(B, S, POOL_WIDTH) * pool_scale.astype(jnp.float32)).astype(u.dtype)

def diff_attention(q, k, v, lq1, lk1, lq2, lk2, norm_g, lambda_init):
    B, S = q.shape[:2]
    nqb = S // Q_BLOCK
    f32 = jnp.float32
    lam = (jnp.exp(jnp.sum(lq1.astype(f32) * lk1.astype(f32)))
           - jnp.exp(jnp.sum(lq2.astype(f32) * lk2.astype(f32))) + lambda_init)
    scale = DIFF_QKDIM ** -0.5
    k_chunk = jnp.arange(S) // CHUNK
    qb = q.reshape(B, nqb, Q_BLOCK, DIFF_HEADS, 2, DIFF_QKDIM).transpose(1, 0, 2, 3, 4, 5)

    def one_block(args):
        q_blk, blk = args
        s = jnp.einsum('bqhmd,bkhmd->bhmqk', q_blk, k).astype(f32) * scale
        q_chunk = (blk * Q_BLOCK + jnp.arange(Q_BLOCK)) // CHUNK
        mask = k_chunk[None, :] <= q_chunk[:, None]
        s = jnp.where(mask, s, -jnp.inf)
        p = jax.nn.softmax(s, axis=-1)
        a = p[:, :, 0] - lam * p[:, :, 1]
        return jnp.einsum('bhqk,bkhd->bqhd', a.astype(v.dtype), v)

    o = lax.map(one_block, (qb, jnp.arange(nqb)))
    o = o.transpose(1, 0, 2, 3, 4).reshape(B, S, DIFF_HEADS, DIFF_VDIM)
    o = rms_norm_2(o, norm_g.reshape(DIFF_HEADS, DIFF_VDIM)) * (1.0 - lambda_init)
    return o.reshape(B, S, DIFF_WIDTH)

def gla_mixer(q, k, v, r, g_lr, w_gate2, b_gate, norm_g):
    B, S = q.shape[:2]
    nc = S // CHUNK
    f32 = jnp.float32
    log_a = jax.nn.log_sigmoid((g_lr @ w_gate2 + b_gate).astype(f32)) / GLA_GATE_TAU
    log_a = log_a.reshape(B, S, GLA_HEADS, GLA_KDIM)

    def to_chunks(t):
        return t.astype(f32).reshape(B, nc, CHUNK, GLA_HEADS, t.shape[-1]).transpose(1, 0, 3, 2, 4)

    qc = to_chunks(q) * (GLA_KDIM ** -0.5)
    kc, vc, lc = to_chunks(k), to_chunks(v), to_chunks(log_a)
    bcum = jnp.cumsum(lc, axis=3)
    b_last = bcum[:, :, :, -1, :]
    q_dec = qc * jnp.exp(bcum)
    k_inv = kc * jnp.exp(-bcum)
    k_end = kc * jnp.exp(b_last[:, :, :, None, :] - bcum)
    causal = jnp.tril(jnp.ones((CHUNK, CHUNK), dtype=bool))
    att = jnp.where(causal, jnp.einsum('nbhid,nbhjd->nbhij', q_dec, k_inv), 0.0)
    o_intra = jnp.einsum('nbhij,nbhje->nbhie', att, vc)

    def step(state, xs):
        q_d, k_e, v_c, decay = xs
        o_inter = jnp.einsum('bhid,bhde->bhie', q_d, state)
        state = state * jnp.exp(decay)[..., None] + jnp.einsum('bhjd,bhje->bhde', k_e, v_c)
        return state, o_inter

    state0 = jnp.zeros((B, GLA_HEADS, GLA_KDIM, GLA_VDIM), f32)
    _, o_inter = lax.scan(step, state0, (q_dec, k_end, vc, b_last))
    o = (o_intra + o_inter).transpose(1, 0, 3, 2, 4).reshape(B, S, GLA_HEADS, GLA_VDIM)
    o = rms_norm_2(o, norm_g.reshape(GLA_HEADS, GLA_VDIM)).reshape(B, S, GLA_WIDTH)
    return (o * jax.nn.silu(r.astype(f32))).astype(r.dtype)

def second_inputs(seed: int = 0) -> dict:
    key = jax.random.key(seed)
    ks = jax.random.split(key, 24)
    nrm = jax.random.normal
    f32 = jnp.float32
    L = DEPTH_2
    return {
        "x": nrm(ks[0], (BATCH, SEQ, D_MODEL), f32),
        "norm1_g": 1.0 + 0.05 * nrm(ks[1], (L, D_MODEL), f32),
        "w_in": nrm(ks[2], (L, D_MODEL, D_IN_PROJ), f32) * D_MODEL ** -0.5,
        "pool_w": nrm(ks[3], (L, POOL_GROUPS, POOL_GDIM, POOL_GDIM), f32) * POOL_GDIM ** -0.5,
        "pool_scale": 1.0 + 0.1 * nrm(ks[4], (L, POOL_WIDTH), f32),
        "diff_lq1": 0.1 * nrm(ks[5], (L, DIFF_QKDIM), f32),
        "diff_lk1": 0.1 * nrm(ks[6], (L, DIFF_QKDIM), f32),
        "diff_lq2": 0.1 * nrm(ks[7], (L, DIFF_QKDIM), f32),
        "diff_lk2": 0.1 * nrm(ks[8], (L, DIFF_QKDIM), f32),
        "diff_norm_g": 1.0 + 0.05 * nrm(ks[9], (L, DIFF_WIDTH), f32),
        "gla_w_gate2": nrm(ks[10], (L, GLA_GATE_RANK, GLA_HEADS * GLA_KDIM), f32) * GLA_GATE_RANK ** -0.5,
        "gla_b_gate": 0.1 * nrm(ks[11], (L, GLA_HEADS * GLA_KDIM), f32),
        "gla_norm_g": 1.0 + 0.05 * nrm(ks[12], (L, GLA_WIDTH), f32),
        "w_out": nrm(ks[13], (L, D_MIX, D_MODEL), f32) * D_MIX ** -0.5,
        "norm2_g": 1.0 + 0.05 * nrm(ks[14], (L, D_MODEL), f32),
        "w_mlp1": nrm(ks[15], (L, D_MODEL, D_FF_2), f32) * D_MODEL ** -0.5,
        "w_mlp2": nrm(ks[16], (L, D_FF_2, D_MODEL), f32) * D_FF_2 ** -0.5,
        "final_norm_g": 1.0 + 0.05 * nrm(ks[17], (D_MODEL,), f32),
    }

def second_block(x, norm1_g, w_in, pool_w, pool_scale, diff_lq1, diff_lk1, diff_lq2, diff_lk2,
              diff_norm_g, gla_w_gate2, gla_b_gate, gla_norm_g, w_out, norm2_g, w_mlp1,
              w_mlp2, final_norm_g):
    B, S, _ = x.shape
    h = x
    for l in range(DEPTH_2):
        u = rms_norm_2(h, norm1_g[l])
        proj = u @ w_in[l]
        p_in, dq, dk, dv, gq, gk, gv, gr, gg = jnp.split(proj, SPLIT_POINTS, axis=-1)
        y_pool = pool_mixer(p_in, pool_w[l], pool_scale[l])
        lambda_init = 0.8 - 0.6 * math.exp(-0.3 * l)
        y_diff = diff_attention(
            dq.reshape(B, S, DIFF_HEADS, 2, DIFF_QKDIM),
            dk.reshape(B, S, DIFF_HEADS, 2, DIFF_QKDIM),
            dv.reshape(B, S, DIFF_HEADS, DIFF_VDIM),
            diff_lq1[l], diff_lk1[l], diff_lq2[l], diff_lk2[l], diff_norm_g[l], lambda_init)
        y_gla = gla_mixer(
            gq.reshape(B, S, GLA_HEADS, GLA_KDIM),
            gk.reshape(B, S, GLA_HEADS, GLA_KDIM),
            gv.reshape(B, S, GLA_HEADS, GLA_VDIM),
            gr, gg, gla_w_gate2[l], gla_b_gate[l], gla_norm_g[l])
        mix = jnp.concatenate([y_pool, y_diff.astype(y_pool.dtype), y_gla.astype(y_pool.dtype)], axis=-1)
        h = h + (mix @ w_out[l]).astype(h.dtype)
        z = rms_norm_2(h, norm2_g[l])
        h = h + jnp.square(jax.nn.relu(z @ w_mlp1[l])) @ w_mlp2[l]
    return rms_norm_2(h, final_norm_g)


def setup_inputs(seed=0):
    out = dict(first_inputs(seed))
    for name, value in second_inputs(seed + 1).items():
        if name != "x":
            out[name + "_2"] = value
    return out


def reference(
    x, c, ctx, c_ctx, w_mod, b_mod, w_in, q_norm_w, k_norm_w, conv_qkv_w, a_log, dt_bias,
    gdn_norm_w, w_pa, w_pd, w_out, w_up, ffn_conv_w, ffn_conv_b, w_down, final_norm_w,
    norm1_g_2, w_in_2, pool_w_2, pool_scale_2, diff_lq1_2, diff_lk1_2, diff_lq2_2, diff_lk2_2,
    diff_norm_g_2, gla_w_gate2_2, gla_b_gate_2, gla_norm_g_2, w_out_2, norm2_g_2, w_mlp1_2,
    w_mlp2_2, final_norm_g_2,
):
    x = first_block(
        x, c, ctx, c_ctx, w_mod, b_mod, w_in, q_norm_w, k_norm_w, conv_qkv_w, a_log, dt_bias,
        gdn_norm_w, w_pa, w_pd, w_out, w_up, ffn_conv_w, ffn_conv_b, w_down, final_norm_w,
    )
    return second_block(
        x, norm1_g_2, w_in_2, pool_w_2, pool_scale_2, diff_lq1_2, diff_lk1_2, diff_lq2_2,
        diff_lk2_2, diff_norm_g_2, gla_w_gate2_2, gla_b_gate_2, gla_norm_g_2, w_out_2,
        norm2_g_2, w_mlp1_2, w_mlp2_2, final_norm_g_2,
    )


_drawn_inputs = setup_inputs


def setup_inputs(seed=0):
    import zlib

    import numpy as np

    out = dict(_drawn_inputs(seed))
    spreads = {}
    factors = {'q_norm_w': 8.0,
     'k_norm_w': 8.0,
     'gdn_norm_w': 5.855,
     'ffn_conv_b': 4.752,
     'diff_lq2_2': 5.708,
     'gla_b_gate_2': 3.51,
     'gla_norm_g_2': 3.23}
    for name, (base, spread) in spreads.items():
        noise = np.random.default_rng([zlib.crc32(name.encode()), seed]).standard_normal(out[name].shape)
        drawn = base * np.exp(spread * noise) if base else spread * noise
        out[name] = jnp.asarray(drawn.astype(out[name].dtype))
    for name, factor in factors.items():
        out[name] = (out[name] * factor).astype(out[name].dtype)
    return out
```

```python
from contextlib import ExitStack

import concourse.bass as bass
import numpy as np
from concourse import mybir

F32 = mybir.dt.float32
ALU = mybir.AluOpType
ACT = mybir.ActivationFunctionType
AX_X = mybir.AxisListType.X

P = 128
D = 1024
KD = D // P
LAT, CTX = 512, 256
TOK = LAT + CTX
TT, TL = TOK // P, LAT // P
EPS = 1e-6
HD = 128
HEADS, KV_HEADS = 8, 2
GROUP = HEADS // KV_HEADS
GH = 8
FF = 2816
KF = FF // P
GRID_W = 64
ROPE_THETA = 10000.0
QUAD = 4
LEVELS = 6
DEPTH2 = 2
FF2 = 4096
KF2 = FF2 // P
DH2 = 4
GLA_C = 64
NCH = LAT // GLA_C
RING = 6
UNIT = 8 * P
BIG = -1.0e30
POOL_WINDOWS = (2, 4, 8, 16)

VEC = {}


def _vec_columns():
    at = 0
    for name, n in (("c", 16), ("b_mod", 48), ("q_norm", 1), ("k_norm", 1), ("conv_qkv", 72),
                    ("gdn_norm", 1), ("ffn_w", 132), ("ffn_b", 44), ("final", 8), ("a_log", 16),
                    ("dt_bias", 16), ("norm1", 16), ("norm2", 16), ("final2", 8), ("diff_norm", 8),
                    ("gla_norm", 4), ("gla_b", 2), ("pool_scale", 4), ("lam", 8)):
        VEC[name] = at
        at += n
    return at


NVEC = _vec_columns()

TAB = {}


def _table_columns():
    at = 0
    for name, n in (("ident", P), ("ones", P), ("le", P), ("ge", P), ("lt", P), ("gt", P),
                    ("up", 7 * P), ("lo", 7 * P), ("rot", P), ("ones64", P), ("causal64", P),
                    ("blockdiag", 256), ("half", 2), ("keep", LAT), ("inv_count", 2 * LAT),
                    ("mask_q", P), ("mask_k", P), ("eps", 1)):
        TAB[name] = at
        at += n
    return at


NTAB = _table_columns()


def shape_tables():
    r, c = np.arange(P)[:, None], np.arange(P)[None, :]
    t = np.zeros((P, NTAB), np.float32)

    def put(name, a):
        t[:, TAB[name]:TAB[name] + a.shape[1]] = a

    put("ident", (r == c) * 1.0)
    put("ones", np.ones((P, P)))
    put("le", (r <= c) * 1.0)
    put("ge", (r >= c) * 1.0)
    put("lt", (r < c) * 1.0)
    put("gt", (r > c) * 1.0)
    up = [((r // b) % 2 == 0) & (c // b == r // b + 1) for b in (1, 2, 4, 8, 16, 32, 64)]
    put("up", np.concatenate(up, 1) * 1.0)
    put("lo", np.concatenate([u.T for u in up], 1) * 1.0)
    rot = np.zeros((P, P))
    for a in range(2):
        for i in range(32):
            rot[a * 64 + 32 + i, a * 64 + i] = -1.0
            rot[a * 64 + i, a * 64 + 32 + i] = 1.0
    put("rot", rot)
    put("ones64", (r // 64 == c // 64) * 1.0)
    put("causal64", ((r // 64 == c // 64) & (r <= c)) * 1.0)
    put("blockdiag", (np.arange(P)[:, None] // 32 == np.arange(256)[None, :] // 64) * 1.0)
    put("half", (r // 64 == np.arange(2)[None, :]) * 1.0)
    put("keep", np.broadcast_to((np.arange(LAT) % GLA_C != 0)[None, :] * 1.0, (P, LAT)))
    win = np.array([[POOL_WINDOWS[2 * tile + (p // 64)] for p in range(P)] for tile in range(2)])
    cnt = np.minimum(np.arange(LAT)[None, None, :] + 1, win[:, :, None])
    put("inv_count", (1.0 / cnt).transpose(1, 0, 2).reshape(P, 2 * LAT))
    put("mask_q", np.where(r == 0, (c < 64) * BIG, 0.0))
    put("mask_k", np.where(r == 0, (c >= 64) * 1.0, 0.0))
    put("eps", np.full((P, 1), EPS))
    tok = np.arange(LAT, dtype=np.float32)
    inv = np.float32(ROPE_THETA) ** (-np.arange(0, 64, 2, dtype=np.float32) / np.float32(64))
    row, col = np.floor(tok / GRID_W), tok % GRID_W
    ang = np.stack([(row[None, :] * inv[:, None]), (col[None, :] * inv[:, None])]).astype(np.float32)
    ang = np.repeat(ang[:, None], 2, 1).reshape(P, LAT)
    rope = np.concatenate([np.cos(ang), np.sin(ang)], 1).astype(np.float32)
    return t, rope


class Signal:

    def __init__(self, sem):
        self.sem, self.base, self.total = sem, 0, 0

    def one(self):
        self.total += 1
        return self.sem, 1

    def dma(self):
        self.total += 16
        return self.sem, 16

    def at(self, n):
        return self.sem, self.base + n


def build(nc, t_vecs, t_mats, t_tabs, t_rope, t_x, t_w, out):
    with ExitStack() as top:
        signals = {}

        def sig(name):
            if name not in signals:
                signals[name] = Signal(top.enter_context(nc.semaphore(name)))
            return signals[name]

        def stage_end():
            for s in signals.values():
                s.base = s.total

        taken = {}

        def sb(ctx, name, *shape):
            taken[name] = taken.get(name, 0) + 1
            name = name if taken[name] == 1 else f"{name}_{taken[name]}"
            return ctx.enter_context(nc.sbuf_tensor(name, [P, *shape], F32))

        ring = sb(top, "ring", RING, UNIT)
        vecs = sb(top, "vecs", NVEC)
        tabs = sb(top, "tabs", NTAB)
        mod = sb(top, "mod", 48, 2)
        mats = sb(top, "mats", 6 * P)
        ps = top.enter_context(nc.psum_tensor("ps", [P, 8, 512], F32))

        def vec(name, i=0, n=1):
            return vecs[:, VEC[name] + i:VEC[name] + i + n]

        def tab(name, i=0, n=P):
            return tabs[:, TAB[name] + i:TAB[name] + i + n]

        ident, ones = tab("ident"), tab("ones")

        units = []
        for name in ("mod", "attn_in", "gates", "gdn_in", "z", "merge", "out", "up", "down"):
            units += t_w[name]
        for layer in range(DEPTH2):
            for name in ("in2a", "in2g", "in2b", "out2", "mlp1", "mlp2"):
                units += t_w[f"{name}_{layer}"]
        loaded = [top.enter_context(nc.semaphore(f"unit_loaded{s}")) for s in range(RING)]
        unit_used = sig("unit_used")
        at = {"issued": 0, "used": 0}

        def stream_weights(sp, n_stage):
            last = min(at["used"] + n_stage + RING, len(units))
            for n in range(at["issued"], last):
                if n >= RING:
                    sp.wait_ge(unit_used.sem, n - RING + 1)
                w = units[n]
                sp.dma_start(ring[:, n % RING, 0:w.shape[1]], w).then_inc(loaded[n % RING], 16)
            at["issued"] = last

        def unit(pe):
            n = at["used"]
            pe.wait_ge(loaded[n % RING], 16 * (n // RING + 1))
            at["used"] += 1
            return ring[:, n % RING, :]

        def pair(n):
            return ps[:, 2 * (n % 4):2 * (n % 4) + 2, :].rearrange("p b n -> p (b n)")

        def product(pe, w, src, dst, n_tok, k0=0, nk=KD, start=True, stop=True):
            for k in range(nk):
                for a, b in ((0, min(n_tok, LAT)), (LAT, n_tok)):
                    if a < b:
                        mm = nc.tensor.matmul(dst[:, a:b], w[:, k * P:(k + 1) * P], src[:, k0 + k, a:b],
                                              start=start and k == 0, stop=stop and k == nk - 1)
            return mm

        def product_tok(pe, w, src, dst, n_tiles, cols):
            for t in range(n_tiles):
                for k in range(KD):
                    mm = nc.tensor.matmul(dst[:, t * cols:(t + 1) * cols], src[:, k, t * P:(t + 1) * P],
                                          w[:, k * cols:(k + 1) * cols], start=k == 0, stop=k == KD - 1)
            return mm

        def stage_modulation():
            landed, silu_c, mod_b = sig("inputs_landed"), sig("silu_c"), sig("mod_b")
            with nc.Block() as block:
                @block.sync
                def _(sp):
                    sp.dma_start(vecs[:], t_vecs).then_inc(*landed.dma())
                    sp.dma_start(tabs[:], t_tabs).then_inc(*landed.dma())
                    sp.dma_start(mats[:], t_mats).then_inc(*landed.dma())
                    stream_weights(sp, 48)

                @block.scalar
                def _(act):
                    act.wait_ge(*landed.at(48))
                    nc.scalar.activation(cs[:], vec("c", 0, 16), ACT.Silu).then_inc(*silu_c.one())

                @block.tensor
                def _(pe):
                    pe.wait_ge(*silu_c.at(1))
                    cv = cs[:].rearrange("p (k v) -> p k v", v=2)
                    for j in range(48):
                        w = unit(pe)
                        for k in range(KD):
                            mm = nc.tensor.matmul(ps[:, 0, 2 * j:2 * j + 2], w[:, k * P:(k + 1) * P],
                                                  cv[:, k, :], start=k == 0, stop=k == KD - 1)
                        mm.then_inc(*unit_used.one())

                @block.vector
                def _(dve):
                    dve.wait_ge(*unit_used.at(48))
                    nc.vector.tensor_tensor(mod[:], ps[:, 0, 0:96].rearrange("p (j v) -> p j v", v=2),
                                            vec("b_mod", 0, 48).unsqueeze(2).to_broadcast([P, 48, 2]),
                                            ALU.add).then_inc(*mod_b.one())
                    dve.wait_ge(*mod_b.at(1))
                    for a in (8, 32):
                        nc.vector.tensor_scalar(mod[:, a:a + 8, :], mod[:, a:a + 8, :], 1.0, None,
                                                ALU.add).then_inc(*mod_b.one())
            stage_end()

        def stage_norm(src, dst, n_tok, scale_of, shift_of=None, load=None, store=None):
            x_in, sq_ok, sum_ok, root_ok, rstd_ok = (sig("norm_in"), sig("norm_sq"), sig("norm_sum"),
                                                     sig("norm_root"), sig("norm_rstd"))
            scaled, shifted, stored = sig("norm_scaled"), sig("norm_shifted"), sig("norm_stored")
            parts = [(0, LAT)] + ([(LAT, TOK)] if n_tok > LAT else [])
            with ExitStack() as s:
                sq = sb(s, "norm_sq_buf", 2, n_tok)
                root = sb(s, "norm_root_buf", n_tok)
                acc = pair(0)
                with nc.Block() as block:
                    @block.sync
                    def _(sp):
                        if load is not None:
                            for k in range(KD):
                                sp.dma_start(src[:, k, 0:n_tok], load[k][:, 0:n_tok]).then_inc(*norm_in[k].dma())
                        if store is not None:
                            for k in range(KD):
                                sp.wait_ge(*scaled.at(k + 1))
                                sp.dma_start(store[k], dst[:, k, :]).then_inc(*stored.dma())
                            sp.wait_ge(*stored.at(16 * KD))
                        stream_weights(sp, 0)

                    @block.scalar
                    def _(act):
                        for k in range(KD):
                            if load is not None:
                                act.wait_ge(*norm_in[k].at(16))
                            if k - 1 > 0:
                                act.wait_ge(*sum_ok.at(k - 1))
                            nc.scalar.activation(sq[:, k % 2, :], src[:, k, 0:n_tok],
                                                 ACT.Square).then_inc(*sq_ok.one())
                        act.wait_ge(*sum_ok.at(KD))
                        nc.scalar.activation(root[:], acc[:, 0:n_tok], ACT.Sqrt, scale=1.0 / D,
                                             bias=tab("eps", 0, 1)).then_inc(*root_ok.one())
                        if shift_of is not None:
                            n = 0
                            for k in range(KD):
                                for p, (a, b) in enumerate(parts):
                                    n += 1
                                    act.wait_ge(*scaled.at(n))
                                    nc.scalar.activation(dst[:, k, a:b], dst[:, k, a:b], ACT.Identity,
                                                         bias=shift_of(k, p)).then_inc(*shifted.one())

                    @block.tensor
                    def _(pe):
                        for k in range(KD):
                            pe.wait_ge(*sq_ok.at(k + 1))
                            for a, b in parts:
                                mm = nc.tensor.matmul(acc[:, a:b], ones, sq[:, k % 2, a:b],
                                                      start=k == 0, stop=k == KD - 1)
                            mm.then_inc(*sum_ok.one())

                    @block.vector
                    def _(dve):
                        dve.wait_ge(*root_ok.at(1))
                        nc.vector.reciprocal(root[:], root[:]).then_inc(*rstd_ok.one())
                        dve.wait_ge(*rstd_ok.at(1))
                        for k in range(KD):
                            for p, (a, b) in enumerate(parts):
                                nc.vector.scalar_tensor_tensor(
                                    out=dst[:, k, a:b], in0=src[:, k, a:b], scalar=scale_of(k, p),
                                    in1=root[:, a:b], op0=ALU.mult, op1=ALU.mult).then_inc(*scaled.one())
            stage_end()

        norm_in = [sig(f"norm_in{k}") for k in range(KD)]

        def stage_attn_inputs(h, q, kk, vtok):
            evac = sig("gemm_evac")
            rope_in, sq_ok, ss_ok, root_ok = sig("rope_in"), sig("qk_sq"), sig("qk_ss"), sig("qk_root")
            rs_ok, n_ok, rot_ok = sig("qk_rstd"), sig("qk_normed"), sig("qk_rot")
            cos_ok, sin_ok, done = sig("qk_cos"), sig("qk_sin"), sig("qk_done")
            items = [(q[:, i, :], LAT, "q_norm") for i in range(HEADS)] + \
                    [(kk[:, i, :], TOK, "k_norm") for i in range(KV_HEADS)]
            n_items = len(items)
            with ExitStack() as s:
                sq = sb(s, "qk_sq_buf", 2, TOK)
                root = sb(s, "qk_root_buf", 2, TOK)
                t1 = sb(s, "qk_t1", 2, LAT)
                rope = sb(s, "rope", 2 * LAT)
                with nc.Block() as block:
                    @block.sync
                    def _(sp):
                        sp.dma_start(rope[:], t_rope).then_inc(*rope_in.dma())
                        stream_weights(sp, 12)

                    @block.tensor
                    def _(pe):
                        for n in range(12):
                            w = unit(pe)
                            if n - 3 > 0:
                                pe.wait_ge(*evac.at(n - 3))
                            if n < 2:
                                mm = product(pe, w, h, pair(n), TOK)
                            elif n < 4:
                                mm = product_tok(pe, w, h, pair(n), TT, P)
                            else:
                                mm = product(pe, w, h, pair(n), LAT)
                            mm.then_inc(*unit_used.one())
                        pe.wait_ge(*evac.at(12))

                        def sums(i):
                            pe.wait_ge(*sq_ok.at(i + 1))
                            if i - 1 > 0:
                                pe.wait_ge(*root_ok.at(i - 1))
                            n = items[i][1]
                            for a, b in ((0, LAT), (LAT, n)):
                                if a < b:
                                    mm = nc.tensor.matmul(pair(i % 2)[:, a:b], ones, sq[:, i % 2, a:b],
                                                          start=True, stop=True)
                            mm.then_inc(*ss_ok.one())

                        sums(0)
                        for i in range(n_items):
                            if i + 1 < n_items:
                                sums(i + 1)
                            pe.wait_ge(*n_ok.at(i + 1))
                            if i - 1 > 0:
                                pe.wait_ge(*sin_ok.at(i - 1))
                            nc.tensor.matmul(ps[:, 4 + 2 * (i % 2), :], tab("rot"), items[i][0][:, 0:LAT],
                                             start=True, stop=True).then_inc(*rot_ok.one())

                    @block.scalar
                    def _(act):
                        for n in range(12):
                            act.wait_ge(*unit_used.at(n + 1))
                            if n < 2:
                                nc.scalar.copy(kk[:, n, :], pair(n)[:, 0:TOK]).then_inc(*evac.one())
                            elif n < 4:
                                c = (n - 2) * P
                                nc.scalar.copy(vtok[:, :, c:c + P],
                                               pair(n)[:, 0:TOK].rearrange("p (t c) -> p t c", c=P)
                                               ).then_inc(*evac.one())
                            else:
                                nc.scalar.copy(q[:, n - 4, :], pair(n)[:, 0:LAT]).then_inc(*evac.one())
                        act.wait_ge(*evac.at(12))

                        def square(i):
                            src, n, _ = items[i]
                            if i - 1 > 0:
                                act.wait_ge(*ss_ok.at(i - 1))
                            nc.scalar.activation(sq[:, i % 2, 0:n], src, ACT.Square).then_inc(*sq_ok.one())

                        square(0)
                        for i in range(n_items):
                            if i + 1 < n_items:
                                square(i + 1)
                            n = items[i][1]
                            act.wait_ge(*ss_ok.at(i + 1))
                            if i - 1 > 0:
                                act.wait_ge(*n_ok.at(i - 1))
                            nc.scalar.activation(root[:, i % 2, 0:n], pair(i % 2)[:, 0:n], ACT.Sqrt,
                                                 scale=1.0 / HD, bias=tab("eps", 0, 1)).then_inc(*root_ok.one())

                    @block.vector
                    def _(dve):
                        for i in range(n_items):
                            src, n, gain = items[i]
                            dve.wait_ge(*root_ok.at(i + 1))
                            nc.vector.reciprocal(root[:, i % 2, 0:n], root[:, i % 2, 0:n]).then_inc(*rs_ok.one())
                            dve.wait_ge(*rs_ok.at(i + 1))
                            nc.vector.scalar_tensor_tensor(out=src, in0=src, scalar=vec(gain), in1=root[:, i % 2, 0:n],
                                                           op0=ALU.mult, op1=ALU.mult).then_inc(*n_ok.one())
                            dve.wait_ge(*rot_ok.at(i + 1))
                            if i - 1 > 0:
                                dve.wait_ge(*done.at(i - 1))
                            dve.wait_ge(*rope_in.at(16))
                            nc.vector.tensor_tensor(t1[:, i % 2, :], ps[:, 4 + 2 * (i % 2), :], rope[:, LAT:],
                                                    ALU.mult).then_inc(*sin_ok.one())

                    @block.gpsimd
                    def _(pool):
                        pool.wait_ge(*rope_in.at(16))
                        for i in range(n_items):
                            x = items[i][0][:, 0:LAT]
                            pool.wait_ge(*rot_ok.at(i + 1))
                            nc.gpsimd.tensor_tensor(x, x, rope[:, 0:LAT], ALU.mult).then_inc(*cos_ok.one())
                            pool.wait_ge(*cos_ok.at(i + 1))
                            pool.wait_ge(*sin_ok.at(i + 1))
                            nc.gpsimd.tensor_tensor(x, x, t1[:, i % 2, :], ALU.add).then_inc(*done.one())
            stage_end()

        def stage_attention(q, kk, vtok, attn, spill):
            s_ok, max_ok, nmax_ok, exp_ok, rinv_ok = (sig("score_done"), sig("max_done"), sig("nmax_done"),
                                                      sig("exp_done"), sig("rinv_done"))
            p_ok, t_ok, tev, pv_ok, o_ok = (sig("prob_done"), sig("probT_done"), sig("probT_evac"),
                                            sig("pv_done"), sig("pv_evac"))
            spilled = sig("spilled")
            n_items = HEADS * TL
            scale = HD ** -0.5
            with ExitStack() as s:
                pr = sb(s, "probs", 2, TOK)
                pt = sb(s, "probsT", 2, TT, LAT)
                mx = sb(s, "row_max", n_items)
                nmx = sb(s, "neg_max", n_items)
                rsum = sb(s, "row_sum", n_items)
                rinv = sb(s, "row_inv", n_items)
                pt_bank = ps[:, 4:6, :].rearrange("p b n -> p (b n)")
                with nc.Block() as block:
                    @block.sync
                    def _(sp):
                        stream_weights(sp, 0)
                        for h in range(HEADS):
                            sp.wait_ge(*o_ok.at(h + 1))
                            sp.dma_start(spill[h], attn[:, h, :]).then_inc(*spilled.dma())
                        sp.wait_ge(*spilled.at(16 * HEADS))

                    @block.tensor
                    def _(pe):
                        def scores(i):
                            h, t = divmod(i, TL)
                            if i - 1 > 0:
                                pe.wait_ge(*exp_ok.at(i - 1))
                            for a, b in ((0, LAT), (LAT, TOK)):
                                mm = nc.tensor.matmul(pair(i % 2)[:, a:b], q[:, h, t * P:(t + 1) * P],
                                                      kk[:, h // GROUP, a:b], start=True, stop=True)
                            mm.then_inc(*s_ok.one())

                        scores(0)
                        for i in range(n_items):
                            h, t = divmod(i, TL)
                            if i + 1 < n_items:
                                scores(i + 1)
                            pe.wait_ge(*p_ok.at(i + 1))
                            if i > 0:
                                pe.wait_ge(*tev.at(i))
                            for k in range(TT):
                                mm = nc.tensor.transpose(pt_bank[:, k * P:(k + 1) * P],
                                                         pr[:, i % 2, k * P:(k + 1) * P], ident)
                            mm.then_inc(*t_ok.one())
                            if t == TL - 1:
                                pe.wait_ge(*tev.at(i + 1))
                                if h - 1 > 0:
                                    pe.wait_ge(*o_ok.at(h - 1))
                                for k in range(TT):
                                    c = (h // GROUP) * P
                                    mm = nc.tensor.matmul(ps[:, 6 + h % 2, :], vtok[:, k, c:c + P],
                                                          pt[:, h % 2, k, :], start=k == 0, stop=k == TT - 1)
                                mm.then_inc(*pv_ok.one())

                    @block.vector
                    def _(dve):
                        def maximum(i):
                            dve.wait_ge(*s_ok.at(i + 1))
                            nc.vector.reduce_max(mx[:, i:i + 1], pair(i % 2)[:, 0:TOK], AX_X).then_inc(*max_ok.one())
                            dve.wait_ge(*max_ok.at(i + 1))
                            nc.vector.tensor_scalar(nmx[:, i:i + 1], mx[:, i:i + 1], -scale, None,
                                                    ALU.mult).then_inc(*nmax_ok.one())

                        maximum(0)
                        for i in range(n_items):
                            h, t = divmod(i, TL)
                            dve.wait_ge(*exp_ok.at(i + 1))
                            nc.vector.reciprocal(rinv[:, i:i + 1], rsum[:, i:i + 1]).then_inc(*rinv_ok.one())
                            dve.wait_ge(*rinv_ok.at(i + 1))
                            nc.vector.tensor_scalar(pr[:, i % 2, :], pr[:, i % 2, :], rinv[:, i:i + 1], None,
                                                    ALU.mult).then_inc(*p_ok.one())
                            if i + 1 < n_items:
                                maximum(i + 1)
                            dve.wait_ge(*t_ok.at(i + 1))
                            if h - 1 > 0:
                                dve.wait_ge(*pv_ok.at(h - 1))
                            nc.vector.tensor_copy(pt[:, h % 2, :, t * P:(t + 1) * P],
                                                  pt_bank[:, 0:TOK].rearrange("p (k c) -> p k c", c=P)
                                                  ).then_inc(*tev.one())

                    @block.scalar
                    def _(act):
                        for i in range(n_items):
                            act.wait_ge(*nmax_ok.at(i + 1))
                            if i - 1 > 0:
                                act.wait_ge(*t_ok.at(i - 1))
                            nc.scalar.activation(pr[:, i % 2, :], pair(i % 2)[:, 0:TOK], ACT.Exp, scale=scale,
                                                 bias=nmx[:, i:i + 1],
                                                 accum_out=rsum[:, i:i + 1]).then_inc(*exp_ok.one())
                            if i % TL == TL - 1 and i >= TL:
                                h = i // TL - 1
                                act.wait_ge(*pv_ok.at(h + 1))
                                nc.scalar.copy(attn[:, h, :], ps[:, 6 + h % 2, :]).then_inc(*o_ok.one())
                        act.wait_ge(*pv_ok.at(HEADS))
                        nc.scalar.copy(attn[:, HEADS - 1, :],
                                       ps[:, 6 + (HEADS - 1) % 2, :]).then_inc(*o_ok.one())
            stage_end()

        def stage_gdn_inputs(h, q, kk, v, beta, log_a, spill):
            evac, taps, conv_ok, silu_ok = (sig("gemm_evac"), sig("conv_tap"), sig("conv_done"),
                                            sig("silu_done"))
            pad_ok, ga_ok, gd_ok = sig("pad_zero"), sig("gate_act"), sig("gate_dve")
            spilled = sig("spilled")
            dst = [q[:, i, :] for i in range(GH)] + [kk[:, i, :] for i in range(GH)] + \
                  [v[:, i, :] for i in range(GH)]
            n_items = len(dst)
            wide = TOK + 4
            c0 = LAT + 3
            with ExitStack() as s:
                cb = sb(s, "conv_in", 2, wide)
                cv = sb(s, "conv_out", 2, wide)
                gt = sb(s, "gate_tmp", 6, 96)
                with nc.Block() as block:
                    @block.sync
                    def _(sp):
                        stream_weights(sp, n_items + 1)
                        for k in range(KD):
                            sp.dma_start(spill[k], h[:, k, 0:LAT]).then_inc(*spilled.dma())
                        sp.wait_ge(*spilled.at(16 * KD))

                    @block.gpsimd
                    def _(pool):
                        nc.gpsimd.memset(cb[:], 0.0).then_inc(*pad_ok.one())

                    @block.tensor
                    def _(pe):
                        w = unit(pe)
                        product_tok(pe, w, h, ps[:, 7, :], TT, 32).then_inc(*unit_used.one())
                        for n in range(n_items):
                            w = unit(pe)
                            if n - 2 > 0:
                                pe.wait_ge(*evac.at(n - 2))
                            product(pe, w, h, pair(n % 3), LAT if n < GH else TOK).then_inc(*unit_used.one())

                    @block.scalar
                    def _(act):
                        act.wait_ge(*unit_used.at(1))
                        raw = ps[:, 7, 0:192].rearrange("p (t s c) -> p s t c", s=2, c=16)
                        gv = [gt[:, i, :].rearrange("p (t c) -> p t c", c=16) for i in range(6)]
                        nc.scalar.activation(beta[:].rearrange("p d t h -> p t d h"),
                                             raw[:, 0].rearrange("p t (d h) -> p t d h", d=2),
                                             ACT.Sigmoid).then_inc(*ga_ok.one())
                        act.wait_ge(*gd_ok.at(2))
                        nc.scalar.activation(gt[:, 2, :], gt[:, 1, :], ACT.Exp, scale=-1.0).then_inc(*ga_ok.one())
                        nc.scalar.activation(gt[:, 5, 0:16], vec("a_log", 0, 16), ACT.Exp).then_inc(*ga_ok.one())
                        act.wait_ge(*ga_ok.at(3))
                        nc.scalar.activation(gt[:, 3, :], gt[:, 2, :], ACT.Ln, bias=1.0).then_inc(*ga_ok.one())
                        act.wait_ge(*pad_ok.at(1))

                        def silu(n):
                            act.wait_ge(*conv_ok.at(n + 1))
                            mm = nc.scalar.activation(dst[n][:, 0:LAT], cv[:, n % 2, 0:LAT], ACT.Silu)
                            if n >= GH:
                                mm = nc.scalar.activation(dst[n][:, LAT:TOK], cv[:, n % 2, LAT + 2:TOK + 2],
                                                          ACT.Silu)
                            mm.then_inc(*silu_ok.one())

                        for n in range(n_items):
                            act.wait_ge(*unit_used.at(n + 2))
                            if n - 1 > 0:
                                act.wait_ge(*conv_ok.at(n - 1))
                            mm = nc.scalar.copy(cb[:, n % 2, 1:1 + LAT], pair(n % 3)[:, 0:LAT])
                            if n >= GH:
                                mm = nc.scalar.copy(cb[:, n % 2, c0:c0 + CTX], pair(n % 3)[:, LAT:TOK])
                            mm.then_inc(*evac.one())
                            if n >= 1:
                                silu(n - 1)
                        silu(n_items - 1)

                    @block.vector
                    def _(dve):
                        dve.wait_ge(*ga_ok.at(1))
                        raw = ps[:, 7, 0:192].rearrange("p (t s c) -> p s t c", s=2, c=16)
                        gv = [gt[:, i, :].rearrange("p (t c) -> p t c", c=16) for i in range(6)]
                        nc.vector.tensor_tensor(gv[0], raw[:, 1], vec("dt_bias", 0, 16).unsqueeze(1)
                                                .to_broadcast([P, TT, 16]), ALU.add).then_inc(*gd_ok.one())
                        dve.wait_ge(*gd_ok.at(1))
                        nc.vector.scalar_tensor_tensor(out=gt[:, 1, :], in0=gt[:, 0, :], scalar=-1.0,
                                                       in1=gt[:, 0, :], op0=ALU.mult,
                                                       op1=ALU.max).then_inc(*gd_ok.one())
                        nc.vector.tensor_scalar(gt[:, 4, :], gt[:, 0, :], 0.0, None, ALU.max).then_inc(*gd_ok.one())
                        dve.wait_ge(*gd_ok.at(3))
                        dve.wait_ge(*ga_ok.at(4))
                        nc.vector.tensor_tensor(gt[:, 4, :], gt[:, 4, :], gt[:, 3, :],
                                                ALU.add).then_inc(*gd_ok.one())
                        dve.wait_ge(*gd_ok.at(4))
                        for d in range(2):
                            nc.vector.scalar_tensor_tensor(
                                out=log_a[:, d], in0=gv[4][:, :, 8 * d:8 * d + 8], scalar=-1.0,
                                in1=gt[:, 5, 8 * d:8 * d + 8].unsqueeze(1).to_broadcast([P, TT, 8]),
                                op0=ALU.mult, op1=ALU.mult).then_inc(*gd_ok.one())
                        for n in range(n_items):
                            m = LAT if n < GH else TOK + 2
                            dve.wait_ge(*evac.at(n + 1))
                            if n - 1 > 0:
                                dve.wait_ge(*silu_ok.at(n - 1))
                            x, y, c = cb[:, n % 2, :], cv[:, n % 2, 0:m], VEC["conv_qkv"] + 3 * n
                            nc.vector.tensor_scalar(y, x[:, 0:m], vecs[:, c:c + 1], None,
                                                    ALU.mult).then_inc(*taps.one())
                            dve.wait_ge(*taps.at(2 * n + 1))
                            nc.vector.scalar_tensor_tensor(out=y, in0=x[:, 1:1 + m], scalar=vecs[:, c + 1:c + 2],
                                                           in1=y, op0=ALU.mult, op1=ALU.add).then_inc(*taps.one())
                            dve.wait_ge(*taps.at(2 * n + 2))
                            nc.vector.scalar_tensor_tensor(out=y, in0=x[:, 2:2 + m], scalar=vecs[:, c + 2:c + 3],
                                                           in1=y, op0=ALU.mult,
                                                           op1=ALU.add).then_inc(*conv_ok.one())
            stage_end()

        def stage_l2(q, kk):
            sq_ok, ss_ok, root_ok, rs_ok, done = (sig("qk_sq"), sig("qk_ss"), sig("qk_root"),
                                                  sig("qk_rstd"), sig("qk_normed"))
            items = [(q[:, i, :], LAT, HD ** -0.5) for i in range(GH)] + \
                    [(kk[:, i, :], TOK, 1.0) for i in range(GH)]
            n_items = len(items)
            with ExitStack() as s:
                sq = sb(s, "l2_sq", 2, TOK)
                root = sb(s, "l2_root", 2, TOK)
                with nc.Block() as block:
                    @block.sync
                    def _(sp):
                        stream_weights(sp, 0)

                    @block.tensor
                    def _(pe):
                        for i in range(n_items):
                            n = items[i][1]
                            pe.wait_ge(*sq_ok.at(i + 1))
                            if i - 1 > 0:
                                pe.wait_ge(*root_ok.at(i - 1))
                            for a, b in ((0, LAT), (LAT, n)):
                                if a < b:
                                    mm = nc.tensor.matmul(pair(i % 2)[:, a:b], ones, sq[:, i % 2, a:b],
                                                          start=True, stop=True)
                            mm.then_inc(*ss_ok.one())

                    @block.scalar
                    def _(act):
                        def square(i):
                            src, n, _ = items[i]
                            if i - 1 > 0:
                                act.wait_ge(*ss_ok.at(i - 1))
                            nc.scalar.activation(sq[:, i % 2, 0:n], src, ACT.Square).then_inc(*sq_ok.one())

                        square(0)
                        for i in range(n_items):
                            if i + 1 < n_items:
                                square(i + 1)
                            n = items[i][1]
                            act.wait_ge(*ss_ok.at(i + 1))
                            if i - 1 > 0:
                                act.wait_ge(*done.at(i - 1))
                            nc.scalar.activation(root[:, i % 2, 0:n], pair(i % 2)[:, 0:n], ACT.Sqrt,
                                                 bias=tab("eps", 0, 1)).then_inc(*root_ok.one())

                    @block.vector
                    def _(dve):
                        for i in range(n_items):
                            src, n, c = items[i]
                            dve.wait_ge(*root_ok.at(i + 1))
                            nc.vector.reciprocal(root[:, i % 2, 0:n], root[:, i % 2, 0:n]).then_inc(*rs_ok.one())
                            dve.wait_ge(*rs_ok.at(i + 1))
                            nc.vector.scalar_tensor_tensor(out=src, in0=src, scalar=c, in1=root[:, i % 2, 0:n],
                                                           op0=ALU.mult, op1=ALU.mult).then_inc(*done.one())
            stage_end()

        def stage_gdn(q, kk, v, beta, log_a, o_tok):
            def S1(name):
                return sig("gdn_" + name)

            sums_ok, exp_ok, be_ok, zero_ok = S1("sums"), S1("exps"), S1("beta_eg"), S1("zero")
            pD, pKK, pQK, pKT, pVT, pPT, pUI = (S1("pe_decay"), S1("pe_kk"), S1("pe_qk"), S1("pe_ktok"),
                                                S1("pe_vtok"), S1("pe_attnT"), S1("pe_u0"))
            pY, pU, pT = S1("pe_y"), S1("pe_u"), S1("pe_t")
            pKS, pO1, pDL, pS, pO2 = S1("pe_ks"), S1("pe_qs"), S1("pe_delta"), S1("pe_state"), S1("pe_attn_v")
            aE, aU, aDL = S1("act_decay"), S1("act_u0"), S1("act_delta")
            dN1, dN, dP, dPT, dKD, dBV = (S1("dve_n1"), S1("dve_n"), S1("dve_attn"), S1("dve_attnT"),
                                          S1("dve_kdec"), S1("dve_bv"))
            dY, dU, dT = S1("dve_y"), S1("dve_u"), S1("dve_t")
            dR1, dS, dO1, dO2 = S1("dve_r1"), S1("dve_state"), S1("dve_o1"), S1("dve_o2")
            lAu, lT1, lTI, lR, lSg, lO = (S1("pool_au"), S1("pool_t1"), S1("pool_t0"), S1("pool_r"),
                                          S1("pool_sg"), S1("pool_o"))
            G, STEPS, CS = 4, TT, CTX // P
            order = [[TL + i for i in range(CS)] + list(range(TL)),
                     [TL + CS - 1 - i for i in range(CS)] + list(range(TL - 1, -1, -1))]

            def n_of(t, g):
                return G * t + g + 1

            def l_of(t, lev, g):
                return (LEVELS * t + lev) * G + g + 1

            def t_of(t, lev, g):
                return ((LEVELS - 1) * t + lev) * G + g + 1

            with ExitStack() as s:
                buf = {n: sb(s, "gdn_" + n, G, QUAD * P) for n in
                       ("E", "N", "T", "U", "Y", "kd", "bv", "St", "Pt")}
                fac = sb(s, "gdn_fac", 3, 2 * TT * GH)
                be = sb(s, "gdn_be", 2, TT, GH)
                la = log_a[:].rearrange("p d t h -> p d (t h)")

                def B(name, g):
                    return buf[name][:, g, :]

                def Bh(name, g):
                    return buf[name][:, g, :].rearrange("p (h s) -> p h s", h=QUAD)

                def bank(g, b):
                    return ps[:, 4 * b + g, :]

                def bankh(g, b):
                    return bank(g, b).rearrange("p (h s) -> p h s", h=QUAD)

                def col(a, t, g):
                    d, h0, tile = g // 2, QUAD * (g % 2), order[g // 2][t]
                    return a[:, d, tile, h0:h0 + QUAD].unsqueeze(2).to_broadcast([P, QUAD, P])

                def facs(i):
                    return fac[:, i, :].rearrange("p (d t h) -> p d t h", d=2, h=GH)

                def rows(m):
                    return m.unsqueeze(1).to_broadcast([P, QUAD, P])

                def chunk(x, t, g, h):
                    c = order[g // 2][t] * P
                    return x[:, QUAD * (g % 2) + h, c:c + P]

                with nc.Block() as block:
                    @block.sync
                    def _(sp):
                        stream_weights(sp, 0)

                    @block.gpsimd
                    def _(pool):
                        nc.gpsimd.memset(buf["St"][:], 0.0).then_inc(*zero_ok.one())
                        nc.gpsimd.memset(o_tok[:], 0.0).then_inc(*zero_ok.one())
                        pool.wait_ge(*zero_ok.at(2))
                        pool.wait_ge(*exp_ok.at(1))
                        for t in range(STEPS):
                            for g in range(G):
                                if t > 0:
                                    pool.wait_ge(*pU.at(l_of(t - 1, LEVELS - 1, g)))
                                nc.gpsimd.tensor_tensor(Bh("T", g), rows(tab("gt" if g < 2 else "lt")),
                                                        col(log_a, t, g), ALU.mult).then_inc(*lAu.one())
                            for g in range(G):
                                pool.wait_ge(*dN.at(n_of(t, g)))
                                nc.gpsimd.tensor_tensor(Bh("T", g), Bh("N", g),
                                                        rows(tab("lo" if g < 2 else "up")),
                                                        ALU.mult).then_inc(*lT1.one())
                                pool.wait_ge(*lT1.at(n_of(t, g)))
                                nc.gpsimd.tensor_tensor(Bh("T", g), rows(ident), Bh("T", g),
                                                        ALU.subtract).then_inc(*lTI.one())
                            for g in range(G):
                                pool.wait_ge(*dR1.at(n_of(t, g)))
                                nc.gpsimd.tensor_tensor(B("bv", g), B("bv", g), B("N", g),
                                                        ALU.subtract).then_inc(*lR.one())
                            for g in range(G):
                                pool.wait_ge(*pKS.at(n_of(t, g)))
                                if t >= CS:
                                    pool.wait_ge(*pO1.at(n_of(t - CS, g)))
                                nc.gpsimd.tensor_tensor(Bh("St", g), Bh("St", g), col(facs(2), t, g),
                                                        ALU.mult).then_inc(*lSg.one())
                            if t >= CS:
                                for g in range(G):
                                    d, tile, h0 = g // 2, order[g // 2][t], QUAD * (g % 2)
                                    dst = o_tok[:, tile, h0 * P:(h0 + QUAD) * P]
                                    if t >= CS:
                                        pool.wait_ge(*dO2.at(n_of(t - CS, g)))
                                    if t > CS or g:
                                        pool.wait_ge(*lO.at(n_of(t - CS, g) - 1))
                                    nc.gpsimd.tensor_tensor(dst, dst, B("Y", g), ALU.add).then_inc(*lO.one())

                    @block.scalar
                    def _(act):
                        act.wait_ge(*sums_ok.at(1))
                        nc.scalar.activation(fac[:].rearrange("p a b -> p (a b)"), ps[:, 7, 0:6 * TT * GH],
                                             ACT.Exp).then_inc(*exp_ok.one())
                        for t in range(STEPS):
                            for g in range(G):
                                act.wait_ge(*pD.at(n_of(t, g)))
                                if t > 0:
                                    act.wait_ge(*pS.at(n_of(t - 1, g)))
                                if t > CS:
                                    act.wait_ge(*pO2.at(n_of(t - CS - 1, g)))
                                nc.scalar.activation(B("E", g), bank(g, 0), ACT.Exp).then_inc(*aE.one())
                            for g in range(G):
                                act.wait_ge(*pUI.at(n_of(t, g)))
                                if t > 0:
                                    act.wait_ge(*pDL.at(n_of(t - 1, g)))
                                nc.scalar.copy(B("U", g), bank(g, 1)).then_inc(*aU.one())
                            for g in range(G):
                                act.wait_ge(*pDL.at(n_of(t, g)))
                                nc.scalar.copy(B("E", g), bank(g, 1)).then_inc(*aDL.one())

                    @block.vector
                    def _(dve):
                        dve.wait_ge(*exp_ok.at(1))
                        nc.vector.tensor_tensor(be[:], beta[:], facs(0), ALU.mult).then_inc(*be_ok.one())
                        dve.wait_ge(*be_ok.at(1))
                        for t in range(STEPS):
                            for g in range(G):
                                dve.wait_ge(*aE.at(n_of(t, g)))
                                dve.wait_ge(*pKK.at(n_of(t, g)))
                                if t > 0:
                                    dve.wait_ge(*lR.at(n_of(t - 1, g)))
                                nc.vector.tensor_tensor(B("N", g), B("E", g), bank(g, 1),
                                                        ALU.mult).then_inc(*dN1.one())
                                dve.wait_ge(*dN1.at(n_of(t, g)))
                                nc.vector.tensor_tensor(Bh("N", g), Bh("N", g), col(beta, t, g),
                                                        ALU.mult).then_inc(*dN.one())
                            if t >= CS:
                                for g in range(G):
                                    if t >= CS:
                                        dve.wait_ge(*pQK.at(n_of(t - CS, g)))
                                    nc.vector.tensor_tensor(B("E", g), B("E", g), bank(g, 0),
                                                            ALU.mult).then_inc(*dP.one())
                            for g in range(G):
                                dve.wait_ge(*pVT.at(n_of(t, g)))
                                if t > 0:
                                    dve.wait_ge(*pDL.at(n_of(t - 1, g)))
                                nc.vector.tensor_tensor(Bh("bv", g), bankh(g, 1), col(beta, t, g),
                                                        ALU.mult).then_inc(*dBV.one())
                                dve.wait_ge(*pKT.at(n_of(t, g)))
                                if t > 0:
                                    dve.wait_ge(*pS.at(n_of(t - 1, g)))
                                nc.vector.tensor_tensor(Bh("kd", g), bankh(g, 0), col(facs(1), t, g),
                                                        ALU.mult).then_inc(*dKD.one())
                            if t >= CS:
                                for g in range(G):
                                    if t >= CS:
                                        dve.wait_ge(*pPT.at(n_of(t - CS, g)))
                                    if t > CS:
                                        dve.wait_ge(*pO2.at(n_of(t - CS - 1, g)))
                                    nc.vector.tensor_tensor(Bh("Pt", g), bankh(g, 1),
                                                            rows(tab("le" if g < 2 else "ge")),
                                                            ALU.mult).then_inc(*dPT.one())
                            for lev in range(LEVELS):
                                for g in range(G):
                                    m = tab("up" if g < 2 else "lo", (lev + 1) * P)
                                    dve.wait_ge(*pY.at(l_of(t, lev, g)))
                                    if lev == 0:
                                        if t > CS:
                                            dve.wait_ge(*lO.at(n_of(t - CS - 1, g)))
                                    nc.vector.tensor_tensor(Bh("Y", g), bankh(g, 0), rows(m),
                                                            ALU.mult).then_inc(*dY.one())
                                for g in range(G):
                                    dve.wait_ge(*pU.at(l_of(t, lev, g)))
                                    nc.vector.tensor_tensor(B("U", g), B("U", g), bank(g, 1),
                                                            ALU.subtract).then_inc(*dU.one())
                                    if lev < LEVELS - 1:
                                        dve.wait_ge(*pT.at(t_of(t, lev, g)))
                                        nc.vector.tensor_tensor(B("T", g), B("T", g), bank(g, 0),
                                                                ALU.subtract).then_inc(*dT.one())
                            for g in range(G):
                                dve.wait_ge(*pKS.at(n_of(t, g)))
                                nc.vector.tensor_tensor(Bh("N", g), bankh(g, 0), col(be, t, g),
                                                        ALU.mult).then_inc(*dR1.one())
                                if t >= CS:
                                    if t >= CS:
                                        dve.wait_ge(*pO1.at(n_of(t - CS, g)))
                                    nc.vector.tensor_tensor(Bh("Y", g), bankh(g, 1), col(facs(0), t, g),
                                                            ALU.mult).then_inc(*dO1.one())
                            for g in range(G):
                                dve.wait_ge(*pS.at(n_of(t, g)))
                                dve.wait_ge(*lSg.at(n_of(t, g)))
                                nc.vector.tensor_tensor(B("St", g), B("St", g), bank(g, 0),
                                                        ALU.add).then_inc(*dS.one())
                            if t >= CS:
                                for g in range(G):
                                    if t >= CS:
                                        dve.wait_ge(*pO2.at(n_of(t - CS, g)))
                                    if t >= CS:
                                        dve.wait_ge(*dO1.at(n_of(t - CS, g)))
                                    nc.vector.tensor_tensor(B("Y", g), B("Y", g), bank(g, 0),
                                                            ALU.add).then_inc(*dO2.one())

                    @block.tensor
                    def _(pe):
                        for d in range(2):
                            for i, m in enumerate((tab("le" if d == 0 else "ge"), tab("gt" if d == 0 else "lt"),
                                                   ones)):
                                c = (2 * i + d) * TT * GH
                                mm = nc.tensor.matmul(ps[:, 7, c:c + TT * GH], m, la[:, d, :],
                                                      start=True, stop=True)
                        mm.then_inc(*sums_ok.one())
                        pe.wait_ge(*exp_ok.at(1))
                        pe.wait_ge(*zero_ok.at(1))

                        def four(dst, lhs, rhs, done):
                            for h in range(QUAD):
                                mm = nc.tensor.matmul(dst[:, h * P:(h + 1) * P], lhs(h), rhs(h),
                                                      start=True, stop=True)
                            mm.then_inc(*done.one())

                        def four_t(dst, src, done):
                            for h in range(QUAD):
                                mm = nc.tensor.transpose(dst[:, h * P:(h + 1) * P], src(h), ident)
                            mm.then_inc(*done.one())

                        def part(name, g):
                            return lambda h: buf[name][:, g, h * P:(h + 1) * P]

                        for t in range(STEPS):
                            for g in range(G):
                                pe.wait_ge(*lAu.at(n_of(t, g)))
                                if t > 0:
                                    pe.wait_ge(*dS.at(n_of(t - 1, g)))
                                if t > CS:
                                    pe.wait_ge(*dO2.at(n_of(t - CS - 1, g)))
                                nc.tensor.matmul(bank(g, 0), tab("le" if g < 2 else "ge"), B("T", g),
                                                 start=True, stop=True).then_inc(*pD.one())
                                if t > 0:
                                    pe.wait_ge(*aDL.at(n_of(t - 1, g)))
                                four(bank(g, 1), lambda h: chunk(kk, t, g, h), lambda h: chunk(kk, t, g, h), pKK)
                            if t >= CS:
                                for g in range(G):
                                    pe.wait_ge(*aE.at(n_of(t, g)))
                                    four(bank(g, 0), lambda h: chunk(q, t, g, h), lambda h: chunk(kk, t, g, h),
                                         pQK)
                            for g in range(G):
                                pe.wait_ge(*dN.at(n_of(t, g)))
                                four_t(bank(g, 1), lambda h: chunk(v, t, g, h), pVT)
                                pe.wait_ge(*aE.at(n_of(t, g)))
                                if t >= CS:
                                    pe.wait_ge(*dP.at(n_of(t - CS, g)))
                                four_t(bank(g, 0), lambda h: chunk(kk, t, g, h), pKT)
                            if t >= CS:
                                for g in range(G):
                                    if t >= CS:
                                        pe.wait_ge(*dP.at(n_of(t - CS, g)))
                                    pe.wait_ge(*dBV.at(n_of(t, g)))
                                    four_t(bank(g, 1), part("E", g), pPT)
                            for g in range(G):
                                pe.wait_ge(*lTI.at(n_of(t, g)))
                                pe.wait_ge(*dBV.at(n_of(t, g)))
                                if t >= CS:
                                    pe.wait_ge(*dPT.at(n_of(t - CS, g)))
                                four_t(bank(g, 1), part("T", g), pUI)
                            for lev in range(LEVELS):
                                for g in range(G):
                                    if lev == 0:
                                        pe.wait_ge(*aU.at(n_of(t, g)))
                                        pe.wait_ge(*dKD.at(n_of(t, g)))
                                    else:
                                        pe.wait_ge(*dU.at(l_of(t, lev - 1, g)))
                                        pe.wait_ge(*dT.at(t_of(t, lev - 1, g)))
                                    four(bank(g, 0), part("N", g), part("U", g), pY)
                                for g in range(G):
                                    pe.wait_ge(*dY.at(l_of(t, lev, g)))
                                    four(bank(g, 1), part("T", g), part("Y", g), pU)
                                    if lev < LEVELS - 1:
                                        four(bank(g, 0), part("Y", g), part("T", g), pT)
                            for g in range(G):
                                if t > 0:
                                    pe.wait_ge(*dS.at(n_of(t - 1, g)))
                                four(bank(g, 0), lambda h: chunk(kk, t, g, h), part("St", g), pKS)
                                pe.wait_ge(*dU.at(l_of(t, LEVELS - 1, g)))
                                if t >= CS:
                                    four(bank(g, 1), lambda h: chunk(q, t, g, h), part("St", g), pO1)
                            for g in range(G):
                                pe.wait_ge(*lR.at(n_of(t, g)))
                                if t >= CS:
                                    pe.wait_ge(*dO1.at(n_of(t - CS, g)))
                                four(bank(g, 1), part("U", g), part("bv", g), pDL)
                            for g in range(G):
                                pe.wait_ge(*aDL.at(n_of(t, g)))
                                four(bank(g, 0), part("kd", g), part("E", g), pS)
                            if t >= CS:
                                for g in range(G):
                                    pe.wait_ge(*dS.at(n_of(t, g)))
                                    four(bank(g, 0), part("Pt", g), part("E", g), pO2)
            stage_end()

        def stage_gdn_out(h, o_tok, gdn, attn, spill_h, spill_attn):
            z_ok, sq_ok, ss_ok, root_ok = sig("z_silu"), sig("o_sq"), sig("o_ss"), sig("o_root")
            rs_ok, on_ok, tr_ok, done = sig("o_rstd"), sig("o_normed"), sig("o_tr"), sig("gdn_done")
            spilled = sig("spilled")
            ov = o_tok[:].rearrange("p t (h e) -> p (t h) e", e=P)
            with ExitStack() as s:
                sq = sb(s, "o_sq_buf", TL * GH, P)
                ss = sb(s, "o_ss_buf", TL * GH)
                zs = sb(s, "z_buf", 2, LAT)
                with nc.Block() as block:
                    @block.sync
                    def _(sp):
                        for k in range(KD):
                            sp.dma_start(h[:, k, :], spill_h[k]).then_inc(*norm_in[k].dma())
                        stream_weights(sp, GH)
                        for k in range(KD):
                            sp.dma_start(attn[:, k, :], spill_attn[k]).then_inc(*spilled.dma())
                        sp.wait_ge(*spilled.at(16 * KD))

                    @block.tensor
                    def _(pe):
                        for k in range(KD):
                            pe.wait_ge(*norm_in[k].at(16))
                        for n in range(GH):
                            w = unit(pe)
                            if n - 1 > 0:
                                pe.wait_ge(*z_ok.at(n - 1))
                            product(pe, w, h, ps[:, n % 2, :], LAT).then_inc(*unit_used.one())
                            pe.wait_ge(*on_ok.at(1))
                            if n - 1 > 0:
                                pe.wait_ge(*done.at(n - 1))
                            for t in range(TL):
                                mm = nc.tensor.transpose(ps[:, 2 + n % 2, t * P:(t + 1) * P],
                                                         o_tok[:, t, n * P:(n + 1) * P], ident)
                            mm.then_inc(*tr_ok.one())

                    @block.scalar
                    def _(act):
                        act.wait_ge(*ss_ok.at(1))
                        nc.scalar.activation(ss[:], ss[:], ACT.Sqrt, scale=1.0 / HD,
                                             bias=tab("eps", 0, 1)).then_inc(*root_ok.one())
                        for n in range(GH):
                            act.wait_ge(*unit_used.at(n + 1))
                            if n - 1 > 0:
                                act.wait_ge(*done.at(n - 1))
                            nc.scalar.activation(zs[:, n % 2, :], ps[:, n % 2, :], ACT.Silu).then_inc(*z_ok.one())

                    @block.vector
                    def _(dve):
                        nc.vector.tensor_tensor(sq[:], ov, ov, ALU.mult).then_inc(*sq_ok.one())
                        dve.wait_ge(*sq_ok.at(1))
                        nc.vector.reduce_sum(ss[:], sq[:], AX_X).then_inc(*ss_ok.one())
                        dve.wait_ge(*root_ok.at(1))
                        nc.vector.reciprocal(ss[:], ss[:]).then_inc(*rs_ok.one())
                        dve.wait_ge(*rs_ok.at(1))
                        nc.vector.tensor_tensor(ov, ov, ss[:].unsqueeze(2).to_broadcast([P, TL * GH, P]),
                                                ALU.mult).then_inc(*on_ok.one())
                        for n in range(GH):
                            dve.wait_ge(*tr_ok.at(n + 1))
                            dve.wait_ge(*z_ok.at(n + 1))
                            nc.vector.scalar_tensor_tensor(out=gdn[:, n, :], in0=ps[:, 2 + n % 2, :],
                                                           scalar=vec("gdn_norm"), in1=zs[:, n % 2, :],
                                                           op0=ALU.mult, op1=ALU.mult).then_inc(*done.one())
            stage_end()

        def stage_merge(h, attn, gdn, y):
            gate_ok, prod_ok, done = sig("merge_gate"), sig("merge_prod"), sig("merged")
            with ExitStack() as s:
                gate = sb(s, "merge_gates", 2, LAT)
                with nc.Block() as block:
                    @block.sync
                    def _(sp):
                        stream_weights(sp, 4 * KD)

                    @block.tensor
                    def _(pe):
                        for n in range(2 * KD):
                            w = unit(pe)
                            if n - 1 > 0:
                                pe.wait_ge(*gate_ok.at(n - 1))
                            product(pe, w, h, ps[:, n % 2, :], LAT).then_inc(*unit_used.one())
                            w = unit(pe)
                            if n - 1 > 0:
                                pe.wait_ge(*prod_ok.at(n - 1))
                            product(pe, w, (attn, gdn)[n % 2], ps[:, 2 + n % 2, :], LAT).then_inc(*unit_used.one())

                    @block.scalar
                    def _(act):
                        for n in range(2 * KD):
                            act.wait_ge(*unit_used.at(2 * n + 1))
                            if n - 1 > 0:
                                act.wait_ge(*prod_ok.at(n - 1))
                            if n % 2:
                                if n // 2 > 0:
                                    act.wait_ge(*done.at(n // 2))
                            nc.scalar.activation(gate[:, n % 2, :], ps[:, n % 2, :],
                                                 ACT.Sigmoid).then_inc(*gate_ok.one())

                    @block.vector
                    def _(dve):
                        for n in range(2 * KD):
                            dve.wait_ge(*gate_ok.at(n + 1))
                            dve.wait_ge(*unit_used.at(2 * n + 2))
                            dst = y[:, n // 2, :] if n % 2 == 0 else gate[:, 1, :]
                            nc.vector.tensor_tensor(dst, gate[:, n % 2, :], ps[:, 2 + n % 2, :],
                                                    ALU.mult).then_inc(*prod_ok.one())
                            if n % 2:
                                dve.wait_ge(*prod_ok.at(n + 1))
                                nc.vector.tensor_tensor(y[:, n // 2, :], y[:, n // 2, :], gate[:, 1, :],
                                                        ALU.add).then_inc(*done.one())
            stage_end()

        def stage_project(src, x, nk, gain_of=None, load=None):
            done = sig("gemm_evac")
            per = -(-nk // 8)
            with nc.Block() as block:
                @block.sync
                def _(sp):
                    if load is not None:
                        for k in range(KD):
                            sp.dma_start(x[:, k, :], load[k][:, 0:LAT]).then_inc(*norm_in[k].dma())
                    stream_weights(sp, KD * per)

                @block.tensor
                def _(pe):
                    for n in range(KD):
                        if n - 3 > 0:
                            pe.wait_ge(*done.at(n - 3))
                        for u in range(per):
                            w = unit(pe)
                            product(pe, w, src, ps[:, n % 4, :], LAT, k0=8 * u, nk=min(8, nk - 8 * u),
                                    start=u == 0, stop=u == per - 1).then_inc(*unit_used.one())

                @block.vector
                def _(dve):
                    for n in range(KD):
                        if load is not None:
                            dve.wait_ge(*norm_in[n].at(16))
                        dve.wait_ge(*unit_used.at(per * (n + 1)))
                        if gain_of is None:
                            nc.vector.tensor_tensor(x[:, n, :], x[:, n, :], ps[:, n % 4, :],
                                                    ALU.add).then_inc(*done.one())
                        else:
                            nc.vector.scalar_tensor_tensor(out=x[:, n, :], in0=ps[:, n % 4, :], scalar=gain_of(n),
                                                           in1=x[:, n, :], op0=ALU.mult,
                                                           op1=ALU.add).then_inc(*done.one())
            stage_end()

        def stage_up(h, mid):
            evac, taps, conv_ok, silu_ok, done = (sig("gemm_evac"), sig("conv_tap"), sig("conv_done"),
                                                  sig("silu_done"), sig("up_done"))
            pad_ok = sig("pad_zero")
            n_items = 2 * KF
            with ExitStack() as s:
                cb = sb(s, "up_in", 2, LAT + 2)
                cv = sb(s, "up_conv", 4, LAT)
                with nc.Block() as block:
                    @block.sync
                    def _(sp):
                        stream_weights(sp, n_items)

                    @block.gpsimd
                    def _(pool):
                        nc.gpsimd.memset(cb[:], 0.0).then_inc(*pad_ok.one())
                        for j in range(KF):
                            pool.wait_ge(*silu_ok.at(j + 1))
                            pool.wait_ge(*conv_ok.at(2 * j + 2))
                            nc.gpsimd.tensor_tensor(mid[:, j, :], cv[:, (2 * j) % 4, :], cv[:, (2 * j + 1) % 4, :],
                                                    ALU.mult).then_inc(*done.one())

                    @block.tensor
                    def _(pe):
                        for n in range(n_items):
                            w = unit(pe)
                            if n - 3 > 0:
                                pe.wait_ge(*evac.at(n - 3))
                            product(pe, w, h, ps[:, n % 4, :], LAT).then_inc(*unit_used.one())

                    @block.scalar
                    def _(act):
                        act.wait_ge(*pad_ok.at(1))
                        for n in range(n_items):
                            act.wait_ge(*unit_used.at(n + 1))
                            if n - 1 > 0:
                                act.wait_ge(*conv_ok.at(n - 1))
                            nc.scalar.copy(cb[:, n % 2, 1:1 + LAT], ps[:, n % 4, :]).then_inc(*evac.one())
                            if n % 2:
                                act.wait_ge(*conv_ok.at(n))
                                g = cv[:, (n - 1) % 4, :]
                                nc.scalar.activation(g, g, ACT.Silu).then_inc(*silu_ok.one())

                    @block.vector
                    def _(dve):
                        for n in range(n_items):
                            tile = n // 2 + KF * (n % 2)
                            x, y = cb[:, n % 2, :], cv[:, n % 4, :]
                            c, b = VEC["ffn_w"] + 3 * tile, VEC["ffn_b"] + tile
                            dve.wait_ge(*evac.at(n + 1))
                            if n // 2 - 1 > 0:
                                dve.wait_ge(*done.at(n // 2 - 1))
                            nc.vector.tensor_scalar(y, x[:, 0:LAT], vecs[:, c:c + 1], vecs[:, b:b + 1], ALU.mult,
                                                    ALU.add).then_inc(*taps.one())
                            dve.wait_ge(*taps.at(2 * n + 1))
                            nc.vector.scalar_tensor_tensor(out=y, in0=x[:, 1:1 + LAT], scalar=vecs[:, c + 1:c + 2],
                                                           in1=y, op0=ALU.mult, op1=ALU.add).then_inc(*taps.one())
                            dve.wait_ge(*taps.at(2 * n + 2))
                            nc.vector.scalar_tensor_tensor(out=y, in0=x[:, 2:2 + LAT], scalar=vecs[:, c + 2:c + 3],
                                                           in1=y, op0=ALU.mult,
                                                           op1=ALU.add).then_inc(*conv_ok.one())
            stage_end()

        def stage_mixer_inputs(u, pin, gq, gk, gr, gg, qz, dk, dv, gv):
            evac, zeroed = sig("gemm_evac"), sig("pad_zero")
            kinds = [("pin", i) for i in range(2)] + [("gq", 0), ("gk", 0)] + [("gr", i) for i in range(2)] + \
                    [("gg", 0)] + [("dq", i) for i in range(DH2)] + [("dk", i) for i in range(DH2)] + \
                    [("dv", i) for i in range(DH2)] + [("gv", i) for i in range(2)]
            with nc.Block() as block:
                @block.sync
                def _(sp):
                    stream_weights(sp, len(kinds))

                @block.gpsimd
                def _(pool):
                    nc.gpsimd.memset(qz[:], 0.0).then_inc(*zeroed.one())

                @block.tensor
                def _(pe):
                    for n, (kind, i) in enumerate(kinds):
                        w = unit(pe)
                        if n - 3 > 0:
                            pe.wait_ge(*evac.at(n - 3))
                        dst = ps[:, n % 4, :]
                        if kind in ("dv", "gv"):
                            mm = product_tok(pe, w, u, dst, TL, P)
                        elif kind == "gg":
                            for k in range(KD):
                                mm = nc.tensor.matmul(dst[0:16, :], w[:, 16 * k:16 * k + 16], u[:, k, :],
                                                      start=k == 0, stop=k == KD - 1)
                        else:
                            mm = product(pe, w, u, dst, LAT)
                        mm.then_inc(*unit_used.one())

                @block.scalar
                def _(act):
                    act.wait_ge(*zeroed.at(1))
                    for n, (kind, i) in enumerate(kinds):
                        act.wait_ge(*unit_used.at(n + 1))
                        b = ps[:, n % 4, :]
                        if kind == "gr":
                            mm = nc.scalar.activation(gr[:, i, :], b, ACT.Silu)
                        elif kind == "gg":
                            mm = nc.scalar.copy(gg[0:16, :], b[0:16, :])
                        elif kind == "dq":
                            for m in range(2):
                                mm = nc.scalar.copy(qz[64 * m:64 * m + 64, m, i, :], b[64 * m:64 * m + 64, :])
                        elif kind in ("dv", "gv"):
                            mm = nc.scalar.copy((dv if kind == "dv" else gv)[:, :, i * P:(i + 1) * P],
                                                b.rearrange("p (t c) -> p t c", c=P))
                        else:
                            dst = {"pin": pin, "gq": gq, "gk": gk, "dk": dk}[kind]
                            mm = nc.scalar.copy(dst[:, i, :] if kind in ("pin", "dk") else dst[:], b)
                        mm.then_inc(*evac.one())
            stage_end()

        def stage_pool_gla(layer, pin, gq, gk, gr, gg, gv, mix):
            a_ok, d_ok, l_ok, p_ok = sig("gla_act"), sig("gla_dve"), sig("gla_pool"), sig("gla_pe")
            with ExitStack() as s:
                cs_ = sb(s, "pool_csum", 2, 16 + LAT)
                pw = sb(s, "pool_mean", 2, LAT)
                x = sb(s, "gla_x", 3, LAT)
                bc = sb(s, "gla_cum", LAT)
                ex = sb(s, "gla_exp", 3, LAT)
                qd = sb(s, "gla_qdec", LAT)
                ke = x[:, 0, :]
                kp = sb(s, "gla_kinv", 4, LAT)
                vp = sb(s, "gla_vpad", TL, 4, P)
                kt = sb(s, "gla_kend_tok", 2, TL, P)
                at_ = sb(s, "gla_att", TL, 4, P)
                kv = sb(s, "gla_kv", NCH, 256)
                st = sb(s, "gla_state", NCH, 256)
                og = sb(s, "gla_o", 2, LAT)
                rt = sb(s, "gla_root", 2, LAT)
                chunks = lambda a: a.rearrange("p (c i) -> p c i", i=GLA_C)
                with nc.Block() as block:
                    @block.sync
                    def _(sp):
                        stream_weights(sp, 0)

                    @block.gpsimd
                    def _(pool):
                        nc.gpsimd.memset(kp[:], 0.0).then_inc(*l_ok.one())
                        nc.gpsimd.memset(cs_[:], 0.0).then_inc(*l_ok.one())
                        nc.gpsimd.memset(vp[:], 0.0).then_inc(*l_ok.one())
                        nc.gpsimd.memset(st[:, 0, :], 0.0).then_inc(*l_ok.one())
                        pool.wait_ge(*l_ok.at(4))
                        for h in range(4):
                            c = 64 * (h % 2)
                            nc.gpsimd.tensor_copy(vp[:, :, h, c:c + 64],
                                                  gv[:, :, 64 * h:64 * h + 64]).then_inc(*l_ok.one())
                        pool.wait_ge(*d_ok.at(2))
                        for tile in range(2):
                            for half in range(2):
                                w, r = POOL_WINDOWS[2 * tile + half], slice(64 * half, 64 * half + 64)
                                pool.wait_ge(*l_ok.at(8 + 2 * tile + half))
                                nc.gpsimd.tensor_tensor(pw[r, tile, :], cs_[r, tile, 16:16 + LAT],
                                                        cs_[r, tile, 16 - w:16 - w + LAT],
                                                        ALU.subtract).then_inc(*l_ok.one())
                        pool.wait_ge(*l_ok.at(12))
                        nc.gpsimd.tensor_tensor(pw[:].rearrange("p a b -> p (a b)"),
                                                pw[:].rearrange("p a b -> p (a b)"), tab("inv_count", 0, 2 * LAT),
                                                ALU.mult).then_inc(*l_ok.one())
                        pool.wait_ge(*l_ok.at(13))
                        nc.gpsimd.tensor_tensor(pw[:], pw[:], pin[:], ALU.subtract).then_inc(*l_ok.one())

                    @block.scalar
                    def _(act):
                        act.wait_ge(*d_ok.at(4))
                        nc.scalar.activation(x[:, 1, :], x[:, 1, :], ACT.Exp, scale=-1.0).then_inc(*a_ok.one())
                        act.wait_ge(*a_ok.at(1))
                        nc.scalar.activation(x[:, 1, :], x[:, 1, :], ACT.Ln, bias=1.0).then_inc(*a_ok.one())
                        act.wait_ge(*d_ok.at(8))
                        nc.scalar.activation(ex[:, 0, :], bc[:], ACT.Exp).then_inc(*a_ok.one())
                        nc.scalar.activation(ex[:, 1, :], bc[:], ACT.Exp, scale=-1.0).then_inc(*a_ok.one())
                        act.wait_ge(*d_ok.at(9))
                        nc.scalar.activation(ex[:, 2, :], x[:, 2, :], ACT.Exp).then_inc(*a_ok.one())
                        act.wait_ge(*p_ok.at(3))
                        for tile in range(2):
                            nc.scalar.activation(mix[:, tile, :], ps[:, 1 + tile, :], ACT.Copy,
                                                 scale=vec("pool_scale", 2 * layer + tile)).then_inc(*a_ok.one())
                        for p in range(2):
                            act.wait_ge(*p_ok.at(13 + p))
                            nc.scalar.copy(og[:, p, :], ps[:, 4 + p, :]).then_inc(*a_ok.one())
                        act.wait_ge(*a_ok.at(9))
                        for p in range(2):
                            nc.scalar.activation(rt[:, p, :], og[:, p, :], ACT.Square).then_inc(*a_ok.one())
                        for p in range(2):
                            act.wait_ge(*p_ok.at(15 + p))
                            nc.scalar.activation(rt[:, p, :], ps[:, 6 + p, :], ACT.Sqrt, scale=1.0 / 64,
                                                 bias=tab("eps", 0, 1)).then_inc(*a_ok.one())

                    @block.vector
                    def _(dve):
                        dve.wait_ge(*l_ok.at(4))
                        for tile in range(2):
                            nc.vector.tensor_tensor_scan(cs_[:, tile, 16:16 + LAT],
                                                         ones[:, 0:1].to_broadcast([P, LAT]), pin[:, tile, :], 0.0,
                                                         ALU.mult, ALU.add).then_inc(*d_ok.one())
                        dve.wait_ge(*p_ok.at(1))
                        nc.vector.tensor_scalar(x[:, 0, :], ps[:, 0, :], vec("gla_b", layer), None,
                                                ALU.add).then_inc(*d_ok.one())
                        dve.wait_ge(*d_ok.at(3))
                        nc.vector.scalar_tensor_tensor(out=x[:, 1, :], in0=x[:, 0, :], scalar=-1.0,
                                                       in1=x[:, 0, :], op0=ALU.mult,
                                                       op1=ALU.max).then_inc(*d_ok.one())
                        nc.vector.tensor_scalar(x[:, 0, :], x[:, 0, :], 0.0, None, ALU.min).then_inc(*d_ok.one())
                        dve.wait_ge(*d_ok.at(5))
                        dve.wait_ge(*a_ok.at(2))
                        nc.vector.tensor_tensor(x[:, 0, :], x[:, 0, :], x[:, 1, :],
                                                ALU.subtract).then_inc(*d_ok.one())
                        dve.wait_ge(*d_ok.at(6))
                        nc.vector.tensor_scalar(x[:, 0, :], x[:, 0, :], 1.0 / 16, None,
                                                ALU.mult).then_inc(*d_ok.one())
                        dve.wait_ge(*d_ok.at(7))
                        nc.vector.tensor_tensor_scan(bc[:], tab("keep", 0, LAT), x[:, 0, :], 0.0, ALU.mult,
                                                     ALU.add).then_inc(*d_ok.one())
                        dve.wait_ge(*d_ok.at(8))
                        nc.vector.tensor_tensor(chunks(x[:, 2, :]),
                                                chunks(bc[:])[:, :, GLA_C - 1:GLA_C].to_broadcast([P, NCH, GLA_C]),
                                                chunks(bc[:]), ALU.subtract).then_inc(*d_ok.one())
                        dve.wait_ge(*a_ok.at(5))
                        nc.vector.scalar_tensor_tensor(out=qd[:], in0=gq[:], scalar=32 ** -0.5, in1=ex[:, 0, :],
                                                       op0=ALU.mult, op1=ALU.mult).then_inc(*d_ok.one())
                        nc.vector.tensor_tensor(ke, gk[:], ex[:, 2, :], ALU.mult).then_inc(*d_ok.one())
                        for h in range(4):
                            r = slice(32 * h, 32 * h + 32)
                            nc.vector.tensor_tensor(kp[r, h, :], gk[r, :], ex[r, 1, :], ALU.mult).then_inc(*d_ok.one())
                        dve.wait_ge(*p_ok.at(4))
                        for half in range(2):
                            nc.vector.tensor_scalar(kt[:, half, :, :].rearrange("p t c -> p (t c)"), ps[:, 3, :],
                                                    tab("half", half, 1), None, ALU.mult).then_inc(*d_ok.one())
                        for t in range(TL):
                            dve.wait_ge(*p_ok.at(5 + t))
                            nc.vector.tensor_tensor(at_[:, t], ps[:, 4 + t, :].rearrange("p (h c) -> p h c", h=4),
                                                    tab("causal64").unsqueeze(1).to_broadcast([P, 4, P]),
                                                    ALU.mult).then_inc(*d_ok.one())
                        for t in range(TL):
                            dve.wait_ge(*p_ok.at(9 + t))
                            dve.wait_ge(*a_ok.at(7))
                            nc.vector.tensor_tensor(kv[:, 2 * t:2 * t + 2, :],
                                                    ps[:, t, :].rearrange("p (c n) -> p c n", c=2),
                                                    tab("blockdiag", 0, 256).unsqueeze(1).to_broadcast([P, 2, 256]),
                                                    ALU.mult).then_inc(*d_ok.one())
                        for c in range(NCH - 1):
                            dve.wait_ge(*d_ok.at(25 + c))
                            e = ex[:, 0, c * GLA_C + GLA_C - 1:c * GLA_C + GLA_C]
                            nc.vector.scalar_tensor_tensor(out=st[:, c + 1, :], in0=st[:, c, :], scalar=e,
                                                           in1=kv[:, c, :], op0=ALU.mult,
                                                           op1=ALU.add).then_inc(*d_ok.one())
                        for p in range(2):
                            dve.wait_ge(*a_ok.at(12 + p))
                            nc.vector.reciprocal(rt[:, p, :], rt[:, p, :]).then_inc(*d_ok.one())
                            dve.wait_ge(*d_ok.at(33 + 3 * p))
                            nc.vector.scalar_tensor_tensor(out=og[:, p, :], in0=og[:, p, :],
                                                           scalar=vec("gla_norm", 2 * layer + p), in1=rt[:, p, :],
                                                           op0=ALU.mult, op1=ALU.mult).then_inc(*d_ok.one())
                            dve.wait_ge(*d_ok.at(34 + 3 * p))
                            nc.vector.tensor_tensor(mix[:, 6 + p, :], og[:, p, :], gr[:, p, :],
                                                    ALU.mult).then_inc(*d_ok.one())

                    @block.tensor
                    def _(pe):
                        nc.tensor.matmul(ps[:, 0, :], mats[0:16, layer * P:(layer + 1) * P], gg[0:16, :],
                                         start=True, stop=True).then_inc(*p_ok.one())
                        pe.wait_ge(*l_ok.at(14))
                        for tile in range(2):
                            c = (2 + 2 * layer + tile) * P
                            nc.tensor.matmul(ps[:, 1 + tile, :], mats[:, c:c + P], pw[:, tile, :],
                                             start=True, stop=True).then_inc(*p_ok.one())
                        pe.wait_ge(*d_ok.at(15))
                        for t in range(TL):
                            mm = nc.tensor.transpose(ps[:, 3, t * P:(t + 1) * P], ke[:, t * P:(t + 1) * P], ident)
                        mm.then_inc(*p_ok.one())
                        for t in range(TL):
                            for h in range(4):
                                mm = nc.tensor.matmul(ps[:, 4 + t, h * P:(h + 1) * P], kp[:, h, t * P:(t + 1) * P],
                                                      qd[:, t * P:(t + 1) * P], start=True, stop=True)
                            mm.then_inc(*p_ok.one())
                        pe.wait_ge(*d_ok.at(17))
                        pe.wait_ge(*a_ok.at(7))
                        for t in range(TL):
                            for half in range(2):
                                mm = nc.tensor.matmul(ps[:, t, 256 * half:256 * half + 256], kt[:, half, t, :],
                                                      gv[:, t, :], start=True, stop=True)
                            mm.then_inc(*p_ok.one())
                        pe.wait_ge(*d_ok.at(32))
                        for p in range(2):
                            for t in range(TL):
                                o = ps[:, 4 + p, t * P:(t + 1) * P]
                                for i in range(2):
                                    nc.tensor.matmul(o, vp[:, t, 2 * p + i, :], at_[:, t, 2 * p + i, :],
                                                     start=i == 0, stop=False)
                                for half in range(2):
                                    c = 2 * t + half
                                    mm = nc.tensor.matmul(o[:, 64 * half:64 * half + 64],
                                                          st[:, c, p * P:(p + 1) * P],
                                                          qd[:, c * GLA_C:(c + 1) * GLA_C], start=False,
                                                          stop=half == 1)
                            mm.then_inc(*p_ok.one())
                        for p in range(2):
                            pe.wait_ge(*a_ok.at(10 + p))
                            nc.tensor.matmul(ps[:, 6 + p, :], tab("ones64"), rt[:, p, :], start=True,
                                             stop=True).then_inc(*p_ok.one())
            stage_end()

        def stage_diff(layer, qz, dk, dv, mix):
            lam0 = 0.8 - 0.6 * float(np.exp(-0.3 * layer))
            scale = 64 ** -0.5
            s_ok, max_ok, nmax_ok, exp_ok, rinv_ok = (sig("score_done"), sig("max_done"), sig("nmax_done"),
                                                      sig("exp_done"), sig("rinv_done"))
            w_ok, t1_ok, p_ok, t_ok, tev = (sig("weight_done"), sig("map1_done"), sig("prob_done"),
                                            sig("probT_done"), sig("probT_evac"))
            pv_ok, o_ok, lam_ok, lame_ok, lams_ok = (sig("pv_done"), sig("pv_evac"), sig("lam_dve"),
                                                     sig("lam_exp"), sig("lam_sum"))
            sq_ok, ss_ok, root_ok, rs_ok, done = (sig("qk_sq"), sig("qk_ss"), sig("qk_root"), sig("qk_rstd"),
                                                  sig("qk_normed"))
            n_items = DH2 * TL
            with ExitStack() as s:
                pr = sb(s, "diff_probs", 2, 2, LAT)
                pt = sb(s, "diff_probsT", 2, TL, LAT)
                mx = sb(s, "diff_max", n_items, 2)
                nmx = sb(s, "diff_nmax", n_items, 2)
                rsum = sb(s, "diff_sum", n_items, 2)
                rinv = sb(s, "diff_inv", n_items, 2)
                lam = sb(s, "diff_lam", 8)
                gain = sb(s, "diff_gain", DH2)
                o = sb(s, "diff_o", DH2, LAT)
                rt = sb(s, "diff_root", DH2, LAT)
                with nc.Block() as block:
                    @block.sync
                    def _(sp):
                        stream_weights(sp, 0)

                    @block.tensor
                    def _(pe):
                        pe.wait_ge(*lam_ok.at(1))
                        nc.tensor.matmul(ps[:, 7, 0:2], ones, lam[:, 0:2], start=True,
                                         stop=True).then_inc(*lams_ok.one())

                        def scores(i):
                            h, t = divmod(i, TL)
                            if 2 * (i - 1) > 0:
                                pe.wait_ge(*exp_ok.at(2 * (i - 1)))
                            for m in range(2):
                                b = ps[:, 2 * (i % 2) + m, :]
                                nc.tensor.matmul(b[:, 0:(t + 1) * P], qz[:, m, h, t * P:(t + 1) * P],
                                                 dk[:, h, 0:(t + 1) * P], start=True, stop=False)
                                mm = nc.tensor.matmul(b[:, t * P:(t + 1) * P], tab("mask_q"), tab("mask_k"),
                                                      start=False, stop=True)
                            mm.then_inc(*s_ok.one())

                        scores(0)
                        for i in range(n_items):
                            h, t = divmod(i, TL)
                            if i + 1 < n_items:
                                scores(i + 1)
                            pe.wait_ge(*p_ok.at(i + 1))
                            if i - 1 > 0:
                                pe.wait_ge(*tev.at(i - 1))
                            for k in range(t + 1):
                                mm = nc.tensor.transpose(ps[:, 4 + i % 2, k * P:(k + 1) * P],
                                                         pr[:, i % 2, 0, k * P:(k + 1) * P], ident)
                            mm.then_inc(*t_ok.one())
                            if t == TL - 1:
                                pe.wait_ge(*tev.at(i + 1))
                                if h - 1 > 0:
                                    pe.wait_ge(*o_ok.at(h - 1))
                                if h == 1:
                                    pe.wait_ge(*lame_ok.at(1))
                                for k in range(TL):
                                    mm = nc.tensor.matmul(ps[:, 6 + h % 2, k * P:LAT],
                                                          dv[:, k, h * P:(h + 1) * P], pt[:, h % 2, k, k * P:LAT],
                                                          start=k == 0, stop=k == TL - 1)
                                mm.then_inc(*pv_ok.one())
                        for h in range(DH2):
                            pe.wait_ge(*sq_ok.at(h + 1))
                            nc.tensor.matmul(ps[:, h, :], ones, rt[:, h, :], start=True,
                                             stop=True).then_inc(*ss_ok.one())

                    @block.scalar
                    def _(act):
                        act.wait_ge(*lams_ok.at(1))
                        nc.scalar.activation(lam[:, 2:4], ps[:, 7, 0:2], ACT.Exp).then_inc(*lame_ok.one())
                        for i in range(n_items):
                            h, t = divmod(i, TL)
                            act.wait_ge(*nmax_ok.at(i + 1))
                            if i - 1 > 0:
                                act.wait_ge(*t_ok.at(i - 1))
                            for m in range(2):
                                nc.scalar.activation(pr[:, i % 2, m, 0:(t + 1) * P],
                                                     ps[:, 2 * (i % 2) + m, 0:(t + 1) * P], ACT.Exp, scale=scale,
                                                     bias=nmx[:, i, m:m + 1],
                                                     accum_out=rsum[:, i, m:m + 1]).then_inc(*exp_ok.one())
                            act.wait_ge(*t_ok.at(i + 1))
                            if h - 1 > 0:
                                act.wait_ge(*pv_ok.at(h - 1))
                            nc.scalar.copy(pt[:, h % 2, 0:t + 1, t * P:(t + 1) * P],
                                           ps[:, 4 + i % 2, 0:(t + 1) * P].rearrange("p (k c) -> p k c", c=P)
                                           ).then_inc(*tev.one())
                            if t == TL - 1:
                                act.wait_ge(*pv_ok.at(h + 1))
                                nc.scalar.copy(o[:, h, :], ps[:, 6 + h % 2, :]).then_inc(*o_ok.one())
                        for h in range(DH2):
                            act.wait_ge(*o_ok.at(h + 1))
                            nc.scalar.activation(rt[:, h, :], o[:, h, :], ACT.Square).then_inc(*sq_ok.one())
                        for h in range(DH2):
                            act.wait_ge(*ss_ok.at(h + 1))
                            nc.scalar.activation(rt[:, h, :], ps[:, h, :], ACT.Sqrt, scale=1.0 / P,
                                                 bias=tab("eps", 0, 1)).then_inc(*root_ok.one())

                    @block.vector
                    def _(dve):
                        lv = vec("lam", 4 * layer, 4).rearrange("p (m w) -> p w m", w=2)
                        nc.vector.tensor_tensor(lam[:, 0:2], lv[:, 0], lv[:, 1], ALU.mult).then_inc(*lam_ok.one())
                        dve.wait_ge(*lame_ok.at(1))
                        nc.vector.scalar_tensor_tensor(out=lam[:, 4:5], in0=lam[:, 3:4], scalar=lam0,
                                                       in1=lam[:, 2:3], op0=ALU.subtract,
                                                       op1=ALU.subtract).then_inc(*lam_ok.one())
                        nc.vector.tensor_scalar(gain[:], vec("diff_norm", DH2 * layer, DH2), 1.0 - lam0, None,
                                                ALU.mult).then_inc(*lam_ok.one())
                        dve.wait_ge(*lam_ok.at(3))

                        def maximum(i):
                            n = (i % TL + 1) * P
                            b = 2 * (i % 2)
                            dve.wait_ge(*s_ok.at(i + 1))
                            nc.vector.reduce_max(mx[:, i, :], ps[:, b:b + 2, 0:n], AX_X).then_inc(*max_ok.one())
                            dve.wait_ge(*max_ok.at(i + 1))
                            nc.vector.tensor_scalar(nmx[:, i, :], mx[:, i, :], -scale, None,
                                                    ALU.mult).then_inc(*nmax_ok.one())

                        maximum(0)
                        for i in range(n_items):
                            n = (i % TL + 1) * P
                            if i + 1 < n_items:
                                maximum(i + 1)
                            dve.wait_ge(*exp_ok.at(2 * i + 2))
                            nc.vector.reciprocal(rinv[:, i, :], rsum[:, i, :]).then_inc(*rinv_ok.one())
                            dve.wait_ge(*rinv_ok.at(i + 1))
                            nc.vector.tensor_tensor(mx[:, i, 1:2], rinv[:, i, 1:2], lam[:, 4:5],
                                                    ALU.mult).then_inc(*w_ok.one())
                            dve.wait_ge(*w_ok.at(i + 1))
                            nc.vector.tensor_scalar(pr[:, i % 2, 1, 0:n], pr[:, i % 2, 1, 0:n], mx[:, i, 1:2], None,
                                                    ALU.mult).then_inc(*t1_ok.one())
                            dve.wait_ge(*t1_ok.at(i + 1))
                            nc.vector.scalar_tensor_tensor(out=pr[:, i % 2, 0, 0:n], in0=pr[:, i % 2, 0, 0:n],
                                                           scalar=rinv[:, i, 0:1], in1=pr[:, i % 2, 1, 0:n],
                                                           op0=ALU.mult, op1=ALU.add).then_inc(*p_ok.one())
                        for h in range(DH2):
                            dve.wait_ge(*root_ok.at(h + 1))
                            nc.vector.reciprocal(rt[:, h, :], rt[:, h, :]).then_inc(*rs_ok.one())
                            dve.wait_ge(*rs_ok.at(h + 1))
                            nc.vector.scalar_tensor_tensor(out=mix[:, 2 + h, :], in0=o[:, h, :],
                                                           scalar=gain[:, h:h + 1], in1=rt[:, h, :],
                                                           op0=ALU.mult, op1=ALU.mult).then_inc(*done.one())
            stage_end()

        def stage_mlp1(z, mid):
            evac, done = sig("gemm_evac"), sig("up_done")
            with nc.Block() as block:
                @block.sync
                def _(sp):
                    stream_weights(sp, KF2)

                @block.tensor
                def _(pe):
                    for n in range(KF2):
                        w = unit(pe)
                        if n - 3 > 0:
                            pe.wait_ge(*evac.at(n - 3))
                        product(pe, w, z, ps[:, n % 4, :], LAT).then_inc(*unit_used.one())

                @block.scalar
                def _(act):
                    for n in range(KF2):
                        act.wait_ge(*unit_used.at(n + 1))
                        nc.scalar.activation(mid[:, n, :], ps[:, n % 4, :], ACT.Relu).then_inc(*evac.one())

                @block.vector
                def _(dve):
                    for n in range(KF2):
                        dve.wait_ge(*evac.at(n + 1))
                        nc.vector.tensor_tensor(mid[:, n, :], mid[:, n, :], mid[:, n, :],
                                                ALU.mult).then_inc(*done.one())
            stage_end()

        def lat_mod(j):
            return lambda k, part: mod[:, j * KD + k, part:part + 1]

        spill_h = nc.dram_tensor("spill_h", (KD, P, LAT), F32, kind="Internal").ap()
        spill_attn = nc.dram_tensor("spill_attn", (KD, P, LAT), F32, kind="Internal").ap()

        with ExitStack() as s:
            cs = sb(s, "silu_c_buf", 16)
            stage_modulation()
        with ExitStack() as s:
            o_tok = sb(s, "o_tok", TL, GH * P)
            with ExitStack() as s2:
                gk_ = sb(s2, "gdn_k", GH, TOK)
                gv_ = sb(s2, "gdn_v", GH, TOK)
                gq_ = sb(s2, "gdn_q", GH, LAT)
                beta = sb(s2, "gdn_beta", 2, TT, GH)
                log_a = sb(s2, "gdn_log_a", 2, TT, GH)
                with ExitStack() as s3:
                    h = sb(s3, "h", KD, TOK)
                    stage_norm(h, h, TOK, lat_mod(1), lat_mod(0), load=t_x)
                    with ExitStack() as s4:
                        vtok = gv_[:, 0:2, :].rearrange("p a n -> p (a n)").rearrange("p (t c) -> p t c", t=TT)
                        attn = sb(s4, "attn", HEADS, LAT)
                        stage_attn_inputs(h, gq_, gk_, vtok)
                        stage_attention(gq_, gk_, vtok, attn, spill_attn)
                    stage_gdn_inputs(h, gq_, gk_, gv_, beta, log_a, spill_h)
                stage_l2(gq_, gk_)
                stage_gdn(gq_, gk_, gv_, beta, log_a, o_tok)
            with ExitStack() as s2:
                y = sb(s2, "y", KD, LAT)
                with ExitStack() as s3:
                    h = sb(s3, "h_lat", KD, LAT)
                    attn = sb(s3, "attn_back", KD, LAT)
                    gdn = sb(s3, "gdn_o", GH, LAT)
                    stage_gdn_out(h, o_tok, gdn, attn, spill_h, spill_attn)
                    stage_merge(h, attn, gdn, y)
                x = o_tok[:].rearrange("p t n -> p (t n)").rearrange("p (k n) -> p k n", k=KD)
                stage_project(y, x, KD, gain_of=lambda n: mod[:, 2 * KD + n, 0:1], load=t_x)
            with ExitStack() as s2:
                mid = sb(s2, "mid", KF, LAT)
                with ExitStack() as s3:
                    h = sb(s3, "h_ffn", KD, LAT)
                    stage_norm(x, h, LAT, lat_mod(4), lat_mod(3))
                    stage_up(h, mid)
                stage_project(mid, x, KF, gain_of=lambda n: mod[:, 5 * KD + n, 0:1])
            stage_norm(x, x, LAT, lambda k, part: vec("final", k))

            for layer in range(DEPTH2):
                with ExitStack() as s2:
                    mix = sb(s2, "mix", KD, LAT)
                    pin = sb(s2, "pool_in", 2, LAT)
                    gq, gk = sb(s2, "gla_q", LAT), sb(s2, "gla_k", LAT)
                    gr, gg = sb(s2, "gla_r", 2, LAT), sb(s2, "gla_g", LAT)
                    gv = sb(s2, "gla_v", TL, 256)
                    qz, dk = sb(s2, "diff_q", 2, DH2, LAT), sb(s2, "diff_k", DH2, LAT)
                    dv = sb(s2, "diff_v", TL, DH2 * P)
                    with ExitStack() as s3:
                        u = sb(s3, "u", KD, LAT)
                        stage_norm(x, u, LAT, lambda k, part: vec("norm1", KD * layer + k))
                        stage_mixer_inputs(u, pin, gq, gk, gr, gg, qz, dk, dv, gv)
                    stage_pool_gla(layer, pin, gq, gk, gr, gg, gv, mix)
                    stage_diff(layer, qz, dk, dv, mix)
                    stage_project(mix, x, KD)
                with ExitStack() as s2:
                    mid = sb(s2, "mid2", KF2, LAT)
                    with ExitStack() as s3:
                        z = sb(s3, "z_mlp", KD, LAT)
                        stage_norm(x, z, LAT, lambda k, part: vec("norm2", KD * layer + k))
                        stage_mlp1(z, mid)
                    stage_project(mid, x, KF2)
            stage_norm(x, x, LAT, lambda k, part: vec("final2", k), store=out)
        assert at["used"] == len(units)


def _units(w, cols=P, kt=8):
    k, n = w.shape
    out = []
    for j in range(n // cols):
        for a in range(0, k // P, kt):
            b = min(kt, k // P - a)
            t = w[a * P:(a + b) * P, j * cols:(j + 1) * cols].reshape(b, P, cols).transpose(1, 0, 2)
            out.append(t.reshape(P, b * cols))
    return out


def _columns(a):
    return np.asarray(a).reshape(-1, P).T


def kernel(**inputs):
    import concourse.bacc as bacc
    from concourse.bass_utils import run_bass_kernel_spmd

    i = {k: np.asarray(v) for k, v in inputs.items()}
    f32 = np.float32
    xt = np.concatenate([i["x"][0].T, i["ctx"][0].T], 1).reshape(KD, P, TOK)

    vecs = np.zeros((P, NVEC), f32)

    def put(name, a, at=0):
        c = VEC[name] + at
        vecs[:a.shape[0], c:c + a.shape[1]] = a

    put("c", np.stack([_columns(i["c"][0]), _columns(i["c_ctx"])], 2).reshape(P, 16))
    put("b_mod", _columns(i["b_mod"][0]))
    put("q_norm", _columns(i["q_norm_w"][0]))
    put("k_norm", _columns(i["k_norm_w"][0]))
    put("conv_qkv", i["conv_qkv_w"][0].reshape(3, 24, P).transpose(2, 1, 0).reshape(P, 72))
    put("gdn_norm", _columns(i["gdn_norm_w"][0]))
    put("ffn_w", i["ffn_conv_w"][0].reshape(3, 44, P).transpose(2, 1, 0).reshape(P, 132))
    put("ffn_b", _columns(i["ffn_conv_b"][0]))
    put("final", _columns(i["final_norm_w"]))
    put("a_log", np.broadcast_to(i["a_log"].reshape(1, 16), (P, 16)))
    put("dt_bias", np.broadcast_to(i["dt_bias"].reshape(1, 16), (P, 16)))
    put("final2", _columns(i["final_norm_g_2"]))
    mats = np.zeros((P, 6 * P), f32)
    for l in range(DEPTH2):
        put("norm1", _columns(i["norm1_g_2"][l]), KD * l)
        put("norm2", _columns(i["norm2_g_2"][l]), KD * l)
        put("diff_norm", _columns(i["diff_norm_g_2"][l]), DH2 * l)
        put("gla_norm", _columns(i["gla_norm_g_2"][l]), 2 * l)
        put("gla_b", _columns(i["gla_b_gate_2"][l]), l)
        put("pool_scale", _columns(i["pool_scale_2"][l]), 2 * l)
        put("lam", np.stack([i[f"diff_{n}_2"][l] for n in ("lq1", "lk1", "lq2", "lk2")], 1), 4 * l)
        mats[0:16, l * P:(l + 1) * P] = i["gla_w_gate2_2"][l]
        for g in range(4):
            r, c = 64 * (g % 2), (2 + 2 * l + g // 2) * P + 64 * (g % 2)
            mats[r:r + 64, c:c + 64] = i["pool_w_2"][l, g]
    tabs, rope = shape_tables()

    w = i["w_in"][0]
    o = np.cumsum([0, 256, 256, 3072, 16, 16, 1024, 1024, 2048])
    ak, av, qkv, db, da, aq, z, gates = [w[:, o[n]:o[n + 1]] for n in range(8)]
    ga, gd = _units(gates[:, :D]), _units(gates[:, D:])
    pa, pd = _units(i["w_pa"][0]), _units(i["w_pd"][0])
    up = _units(i["w_up"][0])
    weights = {
        "mod": _units(i["w_mod"][0]),
        "attn_in": _units(ak) + _units(av) + _units(aq),
        "gates": _units(np.concatenate([db, da], 1), 32),
        "gdn_in": _units(qkv),
        "z": _units(z),
        "merge": [u for j in range(KD) for u in (ga[j], pa[j], gd[j], pd[j])],
        "out": _units(i["w_out"][0]),
        "up": [up[j + KF * s] for j in range(KF) for s in range(2)],
        "down": _units(i["w_down"][0]),
    }
    for l in range(DEPTH2):
        w = i["w_in_2"][l]
        o = np.cumsum([0, 256, 512, 512, 512, 128, 128, 256, 256, 16])
        p_in, dq, dk, dv, gq, gk, gv, gr, gg = [w[:, o[n]:o[n + 1]] for n in range(9)]
        weights[f"in2a_{l}"] = _units(p_in) + _units(gq) + _units(gk) + _units(gr)
        weights[f"in2g_{l}"] = _units(gg, 16)
        weights[f"in2b_{l}"] = _units(dq) + _units(dk) + _units(dv) + _units(gv)
        weights[f"out2_{l}"] = _units(i["w_out_2"][l])
        weights[f"mlp1_{l}"] = _units(i["w_mlp1_2"][l])
        weights[f"mlp2_{l}"] = _units(i["w_mlp2_2"][l])

    nc = bacc.Bacc("TRN2", target_bir_lowering=False, num_devices=1)
    arrays = {}

    def dram(name, a):
        a = arrays[f"in_{name}"] = np.ascontiguousarray(a)
        return nc.dram_tensor(f"in_{name}", a.shape, F32, kind="ExternalInput").ap()

    t_w = {}
    for name, us in weights.items():
        widths = sorted({u.shape[1] for u in us})
        if len(widths) == 1:
            t = dram(f"w_{name}", np.stack(us))
            t_w[name] = [t[n] for n in range(len(us))]
        else:
            t = {c: dram(f"w_{name}_{c}", np.stack([u for u in us if u.shape[1] == c])) for c in widths}
            at = dict.fromkeys(widths, 0)
            t_w[name] = []
            for u in us:
                c = u.shape[1]
                t_w[name].append(t[c][at[c]])
                at[c] += 1
    out = nc.dram_tensor("out", (KD, P, LAT), F32, kind="ExternalOutput").ap()
    build(nc, dram("vecs", vecs), dram("mats", mats), dram("tabs", tabs), dram("rope", rope),
          dram("xt", xt), t_w, out)
    r = run_bass_kernel_spmd(nc, [arrays], core_ids=[0])
    got = np.asarray(r.results[0]["out"])
    return np.ascontiguousarray(got.reshape(D, LAT).T)[None]
```

```python
from contextlib import ExitStack

import concourse.bass as bass
import numpy as np
from concourse import mybir

F32 = mybir.dt.float32
F32R = mybir.dt.float32r
ALU = mybir.AluOpType
ACT = mybir.ActivationFunctionType
AX_X = mybir.AxisListType.X

P = 128
D = 1024
KD = D // P
LAT, CTX = 512, 256
TOK = LAT + CTX
TT, TL = TOK // P, LAT // P
EPS = 1e-6
HD = 128
HEADS, KV_HEADS = 8, 2
GROUP = HEADS // KV_HEADS
GH = 8
FF = 2816
KF = FF // P
GRID_W = 64
ROPE_THETA = 10000.0
QUAD = 4
LEVELS = 6
DEPTH2 = 2
FF2 = 4096
KF2 = FF2 // P
DH2 = 4
GLA_C = 64
NCH = LAT // GLA_C
RING = 4
UNIT = 8 * P
MOD_FIRST = 16
BIG = -1.0e30
POOL_WINDOWS = (2, 4, 8, 16)

VEC = {}


def _vec_columns():
    at = 0
    for name, n in (("c", 16), ("b_mod", 48), ("q_norm", 1), ("k_norm", 1), ("conv_qkv", 72),
                    ("gdn_norm", 1), ("ffn_w", 132), ("ffn_b", 44), ("final", 8), ("a_log", 16),
                    ("dt_bias", 16), ("norm1", 16), ("norm2", 16), ("final2", 8), ("diff_norm", 8),
                    ("gla_norm", 4), ("gla_b", 2), ("pool_scale", 4), ("lam", 8)):
        VEC[name] = at
        at += n
    return at


NVEC = _vec_columns()

TAB = {}


def _table_columns():
    at = 0
    for name, n in (("ident", P), ("ones", P), ("le", P), ("ge", P), ("lt", P), ("gt", P),
                    ("up", P), ("lo", P), ("join_up", LEVELS * P // 2), ("join_lo", LEVELS * P // 2), ("rot", P), ("ones64", P), ("causal64", P),
                    ("blockdiag", 256), ("half", 2), ("keep", LAT), ("inv_count", 2 * LAT),
                    ("mask_q", P), ("mask_k", P), ("eps", 1)):
        TAB[name] = at
        at += n
    return at


NTAB = _table_columns()


def shape_tables():
    r, c = np.arange(P)[:, None], np.arange(P)[None, :]
    t = np.zeros((P, NTAB), np.float32)

    def put(name, a):
        t[:, TAB[name]:TAB[name] + a.shape[1]] = a

    put("ident", (r == c) * 1.0)
    put("ones", np.ones((P, P)))
    put("le", (r <= c) * 1.0)
    put("ge", (r >= c) * 1.0)
    put("lt", (r < c) * 1.0)
    put("gt", (r > c) * 1.0)
    up = [((r // b) % 2 == 0) & (c // b == r // b + 1) for b in (1, 2, 4, 8, 16, 32, 64)]
    put("up", up[0] * -1.0)
    put("lo", up[0].T * -1.0)
    odd = [np.arange(P) // b % 2 == 1 for b in (2, 4, 8, 16, 32, 64)]
    put("join_up", np.concatenate([u[:, o] for u, o in zip(up[1:], odd)], 1) * 1.0)
    put("join_lo", np.concatenate([u.T[:, ~o] for u, o in zip(up[1:], odd)], 1) * 1.0)
    rot = np.zeros((P, P))
    for a in range(2):
        for i in range(32):
            rot[a * 64 + 32 + i, a * 64 + i] = -1.0
            rot[a * 64 + i, a * 64 + 32 + i] = 1.0
    put("rot", rot)
    put("ones64", (r // 64 == c // 64) * 1.0)
    put("causal64", ((r // 64 == c // 64) & (r <= c)) * 1.0)
    put("blockdiag", (np.arange(P)[:, None] // 32 == np.arange(256)[None, :] // 64) * 1.0)
    put("half", (r // 64 == np.arange(2)[None, :]) * 1.0)
    put("keep", np.broadcast_to((np.arange(LAT) % GLA_C != 0)[None, :] * 1.0, (P, LAT)))
    win = np.array([[POOL_WINDOWS[2 * tile + (p // 64)] for p in range(P)] for tile in range(2)])
    cnt = np.minimum(np.arange(LAT)[None, None, :] + 1, win[:, :, None])
    put("inv_count", (1.0 / cnt).transpose(1, 0, 2).reshape(P, 2 * LAT))
    put("mask_q", np.where(r == 0, (c < 64) * BIG, 0.0))
    put("mask_k", np.where(r == 0, (c >= 64) * 1.0, 0.0))
    put("eps", np.full((P, 1), EPS))
    tok = np.arange(LAT, dtype=np.float32)
    inv = np.float32(ROPE_THETA) ** (-np.arange(0, 64, 2, dtype=np.float32) / np.float32(64))
    row, col = np.floor(tok / GRID_W), tok % GRID_W
    ang = np.stack([(row[None, :] * inv[:, None]), (col[None, :] * inv[:, None])]).astype(np.float32)
    ang = np.repeat(ang[:, None], 2, 1).reshape(P, LAT)
    rope = np.concatenate([np.cos(ang), np.sin(ang)], 1).astype(np.float32)
    return t, rope


class Signal:

    def __init__(self, sem):
        self.sem, self.base, self.total = sem, 0, 0

    def one(self):
        self.total += 1
        return self.sem, 1

    def dma(self):
        self.total += 16
        return self.sem, 16

    def at(self, n):
        return self.sem, self.base + n


def build(nc, t_vecs, t_mats, t_tabs, t_rope, t_x, t_w, out):
    with ExitStack() as top:
        signals = {}

        def sig(name):
            if name not in signals:
                signals[name] = Signal(top.enter_context(nc.semaphore(name)))
            return signals[name]

        def stage_end():
            for s in signals.values():
                s.base = s.total

        taken = {}

        def sb(ctx, name, *shape):
            taken[name] = taken.get(name, 0) + 1
            name = name if taken[name] == 1 else f"{name}_{taken[name]}"
            return ctx.enter_context(nc.sbuf_tensor(name, [P, *shape], F32))

        def sbr(ctx, name, *shape):
            taken[name] = taken.get(name, 0) + 1
            name = name if taken[name] == 1 else f"{name}_{taken[name]}"
            return ctx.enter_context(nc.sbuf_tensor(name, [P, *shape], F32R))

        def as_f32(a):
            return a.bitcast(F32)

        ring = sb(top, "ring", RING, UNIT)
        w_hi, w_lo = sbr(top, "w_hi", 2, UNIT), sbr(top, "w_lo", 2, UNIT)
        vecs = sb(top, "vecs", NVEC)
        tabs = sb(top, "tabs", NTAB)
        mod = sb(top, "mod", 48, 2)
        ps = top.enter_context(nc.psum_tensor("ps", [P, 8, 512], F32))

        def vec(name, i=0, n=1):
            return vecs[:, VEC[name] + i:VEC[name] + i + n]

        def tab(name, i=0, n=P):
            return tabs[:, TAB[name] + i:TAB[name] + i + n]

        ident, ones = tab("ident"), tab("ones")

        units, whole = [], []

        def add(name, split=True):
            units.extend(t_w[name])
            whole.extend([not split] * len(t_w[name]))

        add("mod_first", split=False)
        add("attn_in")
        add("mod_rest", split=False)
        for name in ("gates", "gdn_in", "z", "merge", "out", "up", "down"):
            add(name)
        for layer in range(DEPTH2):
            for name in ("in2", "out2", "mlp1a", "mlp2a", "mlp1b", "mlp2b"):
                add(f"{name}_{layer}")
        n_split = [n - sum(whole[:n]) for n in range(len(units))]
        loaded = [top.enter_context(nc.semaphore(f"unit_loaded{s}")) for s in range(RING)]
        unit_used, hi_ok, lo_ok = sig("unit_used"), sig("w_hi_made"), sig("w_lo_made")
        at = {"issued": 0, "used": 0, "hi": 0, "lo": 0}

        def stream_weights(sp, n_stage):
            at["stage_end"] = unit_used.base + max(n_stage, 1)
            last = min(at["used"] + n_stage + RING, len(units))
            for n in range(at["issued"], last):
                m = n - RING
                if m >= 0 and whole[m]:
                    sp.wait_ge(unit_used.sem, m + 1)
                elif m >= 0:
                    sp.wait_ge(lo_ok.sem, n_split[m] + 1)
                w = units[n]
                sp.dma_start(ring[:, n % RING, 0:w.shape[1]], w).then_inc(loaded[n % RING], 16)
            at["issued"] = last

        def ready_to_split(which, j):
            at[which] = max(at[which], unit_used.base)
            while at[which] <= min(unit_used.base + j, at["stage_end"]) and at[which] < len(units) and not whole[at[which]]:
                n = at[which]
                at[which] += 1
                yield n, n_split[n] % 2, units[n].shape[1]

        def split_hi(act, j):
            for n, slot, width in ready_to_split("hi", j):
                act.wait_ge(loaded[n % RING], 16 * (n // RING + 1))
                if n >= 2:
                    act.wait_ge(unit_used.sem, n - 1)
                nc.scalar.copy(w_hi[:, slot, 0:width], ring[:, n % RING, 0:width]).then_inc(*hi_ok.one())

        def split_lo(dve, j):
            for n, slot, width in ready_to_split("lo", j):
                dve.wait_ge(hi_ok.sem, n_split[n] + 1)
                if n >= 2:
                    dve.wait_ge(unit_used.sem, n - 1)
                nc.vector.tensor_tensor(w_lo[:, slot, 0:width], ring[:, n % RING, 0:width],
                                        as_f32(w_hi[:, slot, 0:width]), ALU.subtract).then_inc(*lo_ok.one())

        def unit(pe):
            n = at["used"]
            at["used"] += 1
            if whole[n]:
                pe.wait_ge(loaded[n % RING], 16 * (n // RING + 1))
                return ring[:, n % RING, :]
            pe.wait_ge(lo_ok.sem, n_split[n] + 1)
            return w_hi[:, n_split[n] % 2, :], w_lo[:, n_split[n] % 2, :]

        def pair(n):
            return ps[:, 2 * (n % 4):2 * (n % 4) + 2, :].rearrange("p b n -> p (b n)")

        def product(pe, w, src, dst, n_tok, k0=0, nk=KD, start=True, stop=True):
            for k in range(nk):
                for wi, xi in ((0, 0), (0, 1), (1, 0)):
                    for a, b in ((0, min(n_tok, LAT)), (LAT, n_tok)):
                        if a < b:
                            mm = nc.tensor.matmul(dst[:, a:b], w[wi][:, k * P:(k + 1) * P],
                                                  src[xi][:, k0 + k, a:b], start=start and k == wi == xi == 0,
                                                  stop=stop and k == nk - 1 and wi == 1)
            return mm

        def product_tok(pe, w, src, dst, n_tiles, cols):
            for t in range(n_tiles):
                for k in range(KD):
                    for xi, wi in ((0, 0), (0, 1), (1, 0)):
                        mm = nc.tensor.matmul(dst[:, t * cols:(t + 1) * cols], src[xi][:, k, t * P:(t + 1) * P],
                                              w[wi][:, k * cols:(k + 1) * cols], start=k == wi == xi == 0,
                                              stop=k == KD - 1 and xi == 1)
            return mm

        def mod_unit(pe, j, bank):
            cv = cs[:].rearrange("p (k v) -> p k v", v=2)
            w = unit(pe)
            for k in range(KD):
                mm = nc.tensor.matmul(ps[:, bank, 2 * j:2 * j + 2], w[:, k * P:(k + 1) * P], cv[:, k, :],
                                      start=k == 0, stop=k == KD - 1)
            mm.then_inc(*unit_used.one())

        def mod_bias(dve, a, b, bank, mod_b):
            nc.vector.tensor_tensor(mod[:, a:b, :], ps[:, bank, 2 * a:2 * b].rearrange("p (j v) -> p j v", v=2),
                                    vec("b_mod", a, b - a).unsqueeze(2).to_broadcast([P, b - a, 2]),
                                    ALU.add).then_inc(*mod_b.one())
            dve.wait_ge(*mod_b.at(1))
            c = KD if a == 0 else 4 * KD
            nc.vector.tensor_scalar(mod[:, c:c + KD, :], mod[:, c:c + KD, :], 1.0, None,
                                    ALU.add).then_inc(*mod_b.one())

        def stage_modulation():
            landed, silu_c, mod_b = sig("inputs_landed"), sig("silu_c"), sig("mod_b")
            with nc.Block() as block:
                @block.sync
                def _(sp):
                    sp.dma_start(vecs[:], t_vecs).then_inc(*landed.dma())
                    stream_weights(sp, MOD_FIRST)

                @block.scalar
                def _(act):
                    act.wait_ge(*landed.at(16))
                    nc.scalar.activation(cs[:], vec("c", 0, 16), ACT.Silu).then_inc(*silu_c.one())
                    act.dma_start(tabs[:], t_tabs).then_inc(*landed.dma())
                    act.wait_ge(*landed.at(32))

                @block.tensor
                def _(pe):
                    pe.wait_ge(*silu_c.at(1))
                    for j in range(MOD_FIRST):
                        mod_unit(pe, j, 0)

                @block.vector
                def _(dve):
                    dve.wait_ge(*unit_used.at(MOD_FIRST))
                    mod_bias(dve, 0, MOD_FIRST, 0, mod_b)
            stage_end()

        def stage_norm(src, dst, n_tok, scale_of, shift_of=None, load=None, store=None):
            sq_ok, sum_ok, root_ok, rstd_ok = (sig("norm_sq"), sig("norm_sum"), sig("norm_root"),
                                               sig("norm_rstd"))
            scaled, high, low, stored = sig("norm_scaled"), sig("norm_hi"), sig("norm_lo"), sig("norm_stored")
            parts = [(0, LAT)] + ([(LAT, TOK)] if n_tok > LAT else [])
            np_ = len(parts)
            split = dst is not src
            with ExitStack() as s:
                sq = sb(s, "norm_sq_buf", 2, n_tok)
                root = sb(s, "norm_root_buf", n_tok)
                acc = pair(0)
                with nc.Block() as block:
                    @block.sync
                    def _(sp):
                        if load is not None:
                            for k in range(KD):
                                sp.dma_start(src[:, k, 0:n_tok], load[k][:, 0:n_tok]).then_inc(*norm_in[k].dma())
                        if store is not None:
                            for k in range(KD):
                                sp.wait_ge(*scaled.at(k + 1))
                                sp.dma_start(store[k], dst[:, k, :]).then_inc(*stored.dma())
                            sp.wait_ge(*stored.at(16 * KD))
                        stream_weights(sp, 0)

                    @block.scalar
                    def _(act):
                        for k in range(KD):
                            if load is not None:
                                act.wait_ge(*norm_in[k].at(16))
                            if k - 1 > 0:
                                act.wait_ge(*sum_ok.at(k - 1))
                            nc.scalar.activation(sq[:, k % 2, :], src[:, k, 0:n_tok],
                                                 ACT.Square).then_inc(*sq_ok.one())
                        act.wait_ge(*sum_ok.at(KD))
                        nc.scalar.activation(root[:], acc[:, 0:n_tok], ACT.Sqrt, scale=1.0 / D,
                                             bias=tab("eps", 0, 1)).then_inc(*root_ok.one())
                        split_hi(act, 1)
                        if split:
                            for k in range(KD):
                                for p, (a, b) in enumerate(parts):
                                    act.wait_ge(*scaled.at(np_ * k + p + 1))
                                    x, y = sq[:, k % 2, a:b], dst[0][:, k, a:b]
                                    if shift_of is None:
                                        mm = nc.scalar.copy(y, x)
                                    else:
                                        mm = nc.scalar.activation(y, x, ACT.Identity, bias=shift_of(k, p))
                                    mm.then_inc(*high.one())

                    @block.tensor
                    def _(pe):
                        for k in range(KD):
                            pe.wait_ge(*sq_ok.at(k + 1))
                            for a, b in parts:
                                mm = nc.tensor.matmul(acc[:, a:b], ones, sq[:, k % 2, a:b],
                                                      start=k == 0, stop=k == KD - 1)
                            mm.then_inc(*sum_ok.one())

                    @block.vector
                    def _(dve):
                        dve.wait_ge(*root_ok.at(1))
                        nc.vector.reciprocal(root[:], root[:]).then_inc(*rstd_ok.one())
                        split_lo(dve, 1)
                        dve.wait_ge(*rstd_ok.at(1))

                        def low_parts(k):
                            for p, (a, b) in enumerate(parts):
                                dve.wait_ge(*high.at(np_ * k + p + 1))
                                x, hi, lo = sq[:, k % 2, a:b], as_f32(dst[0][:, k, a:b]), dst[1][:, k, a:b]
                                if shift_of is None:
                                    mm = nc.vector.tensor_tensor(lo, x, hi, ALU.subtract)
                                else:
                                    mm = nc.vector.scalar_tensor_tensor(out=lo, in0=x, scalar=shift_of(k, p),
                                                                        in1=hi, op0=ALU.add, op1=ALU.subtract)
                                mm.then_inc(*low.one())

                        for k in range(KD):
                            if split and k >= 2:
                                if k > 1:
                                    dve.wait_ge(*low.at(np_ * (k - 1)))
                            for p, (a, b) in enumerate(parts):
                                y = sq[:, k % 2, a:b] if split else dst[:, k, a:b]
                                nc.vector.scalar_tensor_tensor(
                                    out=y, in0=src[:, k, a:b], scalar=scale_of(k, p),
                                    in1=root[:, a:b], op0=ALU.mult, op1=ALU.mult).then_inc(*scaled.one())
                            if split and k >= 1:
                                low_parts(k - 1)
                        if split:
                            low_parts(KD - 1)
            stage_end()

        norm_in = [sig(f"norm_in{k}") for k in range(KD)]

        def stage_attn_inputs(h, q, kk, vtok):
            evac = sig("gemm_evac")
            rope_in, sq_ok, ss_ok, root_ok = sig("rope_in"), sig("qk_sq"), sig("qk_ss"), sig("qk_root")
            rs_ok, n_ok, rot_ok = sig("qk_rstd"), sig("qk_normed"), sig("qk_rot")
            cos_ok, sin_ok, done = sig("qk_cos"), sig("qk_sin"), sig("qk_done")
            items = [(q[:, i, :], LAT, "q_norm") for i in range(HEADS)] + \
                    [(kk[:, i, :], TOK, "k_norm") for i in range(KV_HEADS)]
            n_items = len(items)
            with ExitStack() as s:
                sq = sb(s, "qk_sq_buf", 2, TOK)
                root = sb(s, "qk_root_buf", 2, TOK)
                t1 = sb(s, "qk_t1", 2, LAT)
                rope = sb(s, "rope", 2 * LAT)
                with nc.Block() as block:
                    @block.sync
                    def _(sp):
                        sp.dma_start(rope[:], t_rope).then_inc(*rope_in.dma())
                        stream_weights(sp, 12)

                    @block.tensor
                    def _(pe):
                        for n in range(12):
                            w = unit(pe)
                            if n - 3 > 0:
                                pe.wait_ge(*evac.at(n - 3))
                            if n < 2:
                                mm = product(pe, w, h, pair(n), TOK)
                            elif n < 4:
                                mm = product_tok(pe, w, h, pair(n), TT, P)
                            else:
                                mm = product(pe, w, h, pair(n), LAT)
                            mm.then_inc(*unit_used.one())
                        pe.wait_ge(*evac.at(12))

                        def sums(i):
                            pe.wait_ge(*sq_ok.at(i + 1))
                            if i - 1 > 0:
                                pe.wait_ge(*root_ok.at(i - 1))
                            n = items[i][1]
                            for a, b in ((0, LAT), (LAT, n)):
                                if a < b:
                                    mm = nc.tensor.matmul(pair(i % 2)[:, a:b], ones, sq[:, i % 2, a:b],
                                                          start=True, stop=True)
                            mm.then_inc(*ss_ok.one())

                        sums(0)
                        for i in range(n_items):
                            if i + 1 < n_items:
                                sums(i + 1)
                            pe.wait_ge(*n_ok.at(i + 1))
                            if i - 1 > 0:
                                pe.wait_ge(*sin_ok.at(i - 1))
                            nc.tensor.matmul(ps[:, 4 + 2 * (i % 2), :], tab("rot"), items[i][0][:, 0:LAT],
                                             start=True, stop=True).then_inc(*rot_ok.one())

                    @block.scalar
                    def _(act):
                        split_hi(act, 1)
                        for n in range(12):
                            act.wait_ge(*unit_used.at(n + 1))
                            split_hi(act, n + 2)
                            if n < 2:
                                nc.scalar.copy(kk[:, n, :], pair(n)[:, 0:TOK]).then_inc(*evac.one())
                            elif n < 4:
                                c = (n - 2) * P
                                nc.scalar.copy(vtok[:, :, c:c + P],
                                               pair(n)[:, 0:TOK].rearrange("p (t c) -> p t c", c=P)
                                               ).then_inc(*evac.one())
                            else:
                                nc.scalar.copy(q[:, n - 4, :], pair(n)[:, 0:LAT]).then_inc(*evac.one())
                        act.wait_ge(*evac.at(12))

                        def square(i):
                            src, n, _ = items[i]
                            if i - 1 > 0:
                                act.wait_ge(*ss_ok.at(i - 1))
                            nc.scalar.activation(sq[:, i % 2, 0:n], src, ACT.Square).then_inc(*sq_ok.one())

                        square(0)
                        for i in range(n_items):
                            if i + 1 < n_items:
                                square(i + 1)
                            n = items[i][1]
                            act.wait_ge(*ss_ok.at(i + 1))
                            if i - 1 > 0:
                                act.wait_ge(*n_ok.at(i - 1))
                            nc.scalar.activation(root[:, i % 2, 0:n], pair(i % 2)[:, 0:n], ACT.Sqrt,
                                                 scale=1.0 / HD, bias=tab("eps", 0, 1)).then_inc(*root_ok.one())

                    @block.vector
                    def _(dve):
                        for n in range(12):
                            split_lo(dve, n)
                        for i in range(n_items):
                            src, n, gain = items[i]
                            dve.wait_ge(*root_ok.at(i + 1))
                            nc.vector.reciprocal(root[:, i % 2, 0:n], root[:, i % 2, 0:n]).then_inc(*rs_ok.one())
                            dve.wait_ge(*rs_ok.at(i + 1))
                            nc.vector.scalar_tensor_tensor(out=src, in0=src, scalar=vec(gain), in1=root[:, i % 2, 0:n],
                                                           op0=ALU.mult, op1=ALU.mult).then_inc(*n_ok.one())
                            dve.wait_ge(*rot_ok.at(i + 1))
                            if i - 1 > 0:
                                dve.wait_ge(*done.at(i - 1))
                            dve.wait_ge(*rope_in.at(16))
                            nc.vector.tensor_tensor(t1[:, i % 2, :], ps[:, 4 + 2 * (i % 2), :], rope[:, LAT:],
                                                    ALU.mult).then_inc(*sin_ok.one())

                    @block.gpsimd
                    def _(pool):
                        pool.wait_ge(*rope_in.at(16))
                        for i in range(n_items):
                            x = items[i][0][:, 0:LAT]
                            pool.wait_ge(*rot_ok.at(i + 1))
                            nc.gpsimd.tensor_tensor(x, x, rope[:, 0:LAT], ALU.mult).then_inc(*cos_ok.one())
                            pool.wait_ge(*cos_ok.at(i + 1))
                            pool.wait_ge(*sin_ok.at(i + 1))
                            nc.gpsimd.tensor_tensor(x, x, t1[:, i % 2, :], ALU.add).then_inc(*done.one())
            stage_end()

        def stage_attention(q, kk, vtok, pt, spill):
            s_ok, max_ok, nmax_ok, exp_ok, rinv_ok = (sig("score_done"), sig("max_done"), sig("nmax_done"),
                                                      sig("exp_done"), sig("rinv_done"))
            p_ok, t_ok, tev, pv_ok, o_ok = (sig("prob_done"), sig("probT_done"), sig("probT_evac"),
                                            sig("pv_done"), sig("pv_evac"))
            spilled = [sig("attn_spilled0"), sig("attn_spilled1")]
            mod_b = sig("mod_b")
            n_rest = 6 * KD - MOD_FIRST
            n_items = HEADS * TL
            scale = HD ** -0.5
            with ExitStack() as s:
                pr = sb(s, "probs", 2, TOK)
                o = sb(s, "attn_out", 2, LAT)
                mx = sb(s, "row_max", n_items)
                nmx = sb(s, "neg_max", n_items)
                rsum = sb(s, "row_sum", n_items)
                rinv = sb(s, "row_inv", n_items)
                pt_bank = ps[:, 4:6, :].rearrange("p b n -> p (b n)")
                with nc.Block() as block:
                    @block.sync
                    def _(sp):
                        per = n_rest // HEADS
                        for h in range(HEADS):
                            stream_weights(sp, per * (h + 1))
                            sp.wait_ge(*o_ok.at(h + 1))
                            sp.dma_start(spill[h], o[:, h % 2, :]).then_inc(*spilled[h % 2].dma())
                        for c in range(2):
                            sp.wait_ge(*spilled[c].at(8 * HEADS))

                    @block.tensor
                    def _(pe):
                        def scores(i):
                            h, t = divmod(i, TL)
                            if i - 1 > 0:
                                pe.wait_ge(*exp_ok.at(i - 1))
                            for a, b in ((0, LAT), (LAT, TOK)):
                                mm = nc.tensor.matmul(pair(i % 2)[:, a:b], q[:, h, t * P:(t + 1) * P],
                                                      kk[:, h // GROUP, a:b], start=True, stop=True)
                            mm.then_inc(*s_ok.one())

                        scores(0)
                        for i in range(n_items):
                            h, t = divmod(i, TL)
                            if i + 1 < n_items:
                                scores(i + 1)
                            mod_unit(pe, MOD_FIRST + i, 7)
                            pe.wait_ge(*p_ok.at(i + 1))
                            if i > 0:
                                pe.wait_ge(*tev.at(i))
                            for k in range(TT):
                                mm = nc.tensor.transpose(pt_bank[:, k * P:(k + 1) * P],
                                                         pr[:, i % 2, k * P:(k + 1) * P], ident)
                            mm.then_inc(*t_ok.one())
                            if t == TL - 1:
                                pe.wait_ge(*tev.at(i + 1))
                                if h > 0:
                                    pe.wait_ge(*o_ok.at(h))
                                for k in range(TT):
                                    c = (h // GROUP) * P
                                    mm = nc.tensor.matmul(ps[:, 6, :], vtok[:, k, c:c + P],
                                                          pt[:, k, :], start=k == 0, stop=k == TT - 1)
                                mm.then_inc(*pv_ok.one())

                    @block.vector
                    def _(dve):
                        def maximum(i):
                            dve.wait_ge(*s_ok.at(i + 1))
                            nc.vector.reduce_max(mx[:, i:i + 1], pair(i % 2)[:, 0:TOK], AX_X).then_inc(*max_ok.one())
                            dve.wait_ge(*max_ok.at(i + 1))
                            nc.vector.tensor_scalar(nmx[:, i:i + 1], mx[:, i:i + 1], -scale, None,
                                                    ALU.mult).then_inc(*nmax_ok.one())

                        maximum(0)
                        for i in range(n_items):
                            h, t = divmod(i, TL)
                            dve.wait_ge(*exp_ok.at(i + 1))
                            nc.vector.reciprocal(rinv[:, i:i + 1], rsum[:, i:i + 1]).then_inc(*rinv_ok.one())
                            dve.wait_ge(*rinv_ok.at(i + 1))
                            nc.vector.tensor_scalar(pr[:, i % 2, :], pr[:, i % 2, :], rinv[:, i:i + 1], None,
                                                    ALU.mult).then_inc(*p_ok.one())
                            if i + 1 < n_items:
                                maximum(i + 1)
                            dve.wait_ge(*t_ok.at(i + 1))
                            if h > 0:
                                dve.wait_ge(*pv_ok.at(h))
                            nc.vector.tensor_copy(pt[:, :, t * P:(t + 1) * P],
                                                  pt_bank[:, 0:TOK].rearrange("p (k c) -> p k c", c=P)
                                                  ).then_inc(*tev.one())
                        dve.wait_ge(*unit_used.at(n_rest))
                        mod_bias(dve, MOD_FIRST, 6 * KD, 7, mod_b)

                    @block.scalar
                    def _(act):
                        for i in range(n_items):
                            act.wait_ge(*nmax_ok.at(i + 1))
                            if i - 1 > 0:
                                act.wait_ge(*t_ok.at(i - 1))
                            nc.scalar.activation(pr[:, i % 2, :], pair(i % 2)[:, 0:TOK], ACT.Exp, scale=scale,
                                                 bias=nmx[:, i:i + 1],
                                                 accum_out=rsum[:, i:i + 1]).then_inc(*exp_ok.one())
                            if i % TL == TL - 1:
                                h = i // TL
                                act.wait_ge(*pv_ok.at(h + 1))
                                if h >= 2:
                                    if 16 * (h // 2) > 0:
                                        act.wait_ge(*spilled[h % 2].at(16 * (h // 2)))
                                nc.scalar.copy(o[:, h % 2, :], ps[:, 6, :]).then_inc(*o_ok.one())
            stage_end()

        def stage_gdn_inputs(h, q, kk, v, beta, log_a, spill):
            evac, taps, conv_ok, silu_ok = (sig("gemm_evac"), sig("conv_tap"), sig("conv_done"),
                                            sig("silu_done"))
            pad_ok, ga_ok, gd_ok = sig("pad_zero"), sig("gate_act"), sig("gate_dve")
            spilled, whole_ok = [sig("h_spilled0"), sig("h_spilled1")], sig("h_whole")
            dst = [q[:, i, :] for i in range(GH)] + [kk[:, i, :] for i in range(GH)] + \
                  [v[:, i, :] for i in range(GH)]
            n_items = len(dst)
            wide = TOK + 4
            c0 = LAT + 3
            with ExitStack() as s:
                cb = sb(s, "conv_in", 2, wide)
                cv = sb(s, "conv_out", 2, wide)
                gt = sb(s, "gate_tmp", 6, 96)
                hw = sb(s, "h_whole_buf", 2, LAT)
                with nc.Block() as block:
                    @block.sync
                    def _(sp):
                        stream_weights(sp, n_items + 1)
                        for k in range(KD):
                            sp.wait_ge(*whole_ok.at(k + 1))
                            sp.dma_start(spill[k], hw[:, k % 2, :]).then_inc(*spilled[k % 2].dma())
                        for c in range(2):
                            sp.wait_ge(*spilled[c].at(8 * KD))

                    @block.gpsimd
                    def _(pool):
                        nc.gpsimd.memset(cb[:], 0.0).then_inc(*pad_ok.one())
                        for k in range(KD):
                            if k >= 2:
                                if 16 * (k // 2) > 0:
                                    pool.wait_ge(*spilled[k % 2].at(16 * (k // 2)))
                            nc.gpsimd.tensor_tensor(hw[:, k % 2, :], as_f32(h[0][:, k, 0:LAT]),
                                                    as_f32(h[1][:, k, 0:LAT]), ALU.add).then_inc(*whole_ok.one())

                    @block.tensor
                    def _(pe):
                        w = unit(pe)
                        product_tok(pe, w, h, ps[:, 7, :], TT, 32).then_inc(*unit_used.one())
                        for n in range(n_items):
                            w = unit(pe)
                            if n - 2 > 0:
                                pe.wait_ge(*evac.at(n - 2))
                            product(pe, w, h, pair(n % 3), LAT if n < GH else TOK).then_inc(*unit_used.one())

                    @block.scalar
                    def _(act):
                        split_hi(act, 2)
                        act.wait_ge(*unit_used.at(1))
                        raw = ps[:, 7, 0:192].rearrange("p (t s c) -> p s t c", s=2, c=16)
                        gv = [gt[:, i, :].rearrange("p (t c) -> p t c", c=16) for i in range(6)]
                        nc.scalar.activation(beta[:].rearrange("p d t h -> p t d h"),
                                             raw[:, 0].rearrange("p t (d h) -> p t d h", d=2),
                                             ACT.Sigmoid).then_inc(*ga_ok.one())
                        act.wait_ge(*gd_ok.at(2))
                        nc.scalar.activation(gt[:, 2, :], gt[:, 1, :], ACT.Exp, scale=-1.0).then_inc(*ga_ok.one())
                        nc.scalar.activation(gt[:, 5, 0:16], vec("a_log", 0, 16), ACT.Exp).then_inc(*ga_ok.one())
                        act.wait_ge(*ga_ok.at(3))
                        nc.scalar.activation(gt[:, 3, :], gt[:, 2, :], ACT.Ln, bias=1.0).then_inc(*ga_ok.one())
                        act.wait_ge(*pad_ok.at(1))

                        def silu(n):
                            act.wait_ge(*conv_ok.at(n + 1))
                            mm = nc.scalar.activation(dst[n][:, 0:LAT], cv[:, n % 2, 0:LAT], ACT.Silu)
                            if n >= GH:
                                mm = nc.scalar.activation(dst[n][:, LAT:TOK], cv[:, n % 2, LAT + 2:TOK + 2],
                                                          ACT.Silu)
                            mm.then_inc(*silu_ok.one())

                        for n in range(n_items):
                            act.wait_ge(*unit_used.at(n + 2))
                            split_hi(act, n + 3)
                            if n - 1 > 0:
                                act.wait_ge(*conv_ok.at(n - 1))
                            mm = nc.scalar.copy(cb[:, n % 2, 1:1 + LAT], pair(n % 3)[:, 0:LAT])
                            if n >= GH:
                                mm = nc.scalar.copy(cb[:, n % 2, c0:c0 + CTX], pair(n % 3)[:, LAT:TOK])
                            mm.then_inc(*evac.one())
                            if n >= 1:
                                silu(n - 1)
                        silu(n_items - 1)

                    @block.vector
                    def _(dve):
                        split_lo(dve, 2)
                        dve.wait_ge(*ga_ok.at(1))
                        raw = ps[:, 7, 0:192].rearrange("p (t s c) -> p s t c", s=2, c=16)
                        gv = [gt[:, i, :].rearrange("p (t c) -> p t c", c=16) for i in range(6)]
                        nc.vector.tensor_tensor(gv[0], raw[:, 1], vec("dt_bias", 0, 16).unsqueeze(1)
                                                .to_broadcast([P, TT, 16]), ALU.add).then_inc(*gd_ok.one())
                        dve.wait_ge(*gd_ok.at(1))
                        nc.vector.scalar_tensor_tensor(out=gt[:, 1, :], in0=gt[:, 0, :], scalar=-1.0,
                                                       in1=gt[:, 0, :], op0=ALU.mult,
                                                       op1=ALU.max).then_inc(*gd_ok.one())
                        nc.vector.tensor_scalar(gt[:, 4, :], gt[:, 0, :], 0.0, None, ALU.max).then_inc(*gd_ok.one())
                        dve.wait_ge(*gd_ok.at(3))
                        dve.wait_ge(*ga_ok.at(4))
                        nc.vector.tensor_tensor(gt[:, 4, :], gt[:, 4, :], gt[:, 3, :],
                                                ALU.add).then_inc(*gd_ok.one())
                        dve.wait_ge(*gd_ok.at(4))
                        for d in range(2):
                            nc.vector.scalar_tensor_tensor(
                                out=log_a[:, d], in0=gv[4][:, :, 8 * d:8 * d + 8], scalar=-1.0,
                                in1=gt[:, 5, 8 * d:8 * d + 8].unsqueeze(1).to_broadcast([P, TT, 8]),
                                op0=ALU.mult, op1=ALU.mult).then_inc(*gd_ok.one())
                        for n in range(n_items):
                            m = LAT if n < GH else TOK + 2
                            split_lo(dve, n + 3)
                            dve.wait_ge(*evac.at(n + 1))
                            if n - 1 > 0:
                                dve.wait_ge(*silu_ok.at(n - 1))
                            x, y, c = cb[:, n % 2, :], cv[:, n % 2, 0:m], VEC["conv_qkv"] + 3 * n
                            nc.vector.tensor_scalar(y, x[:, 0:m], vecs[:, c:c + 1], None,
                                                    ALU.mult).then_inc(*taps.one())
                            dve.wait_ge(*taps.at(2 * n + 1))
                            nc.vector.scalar_tensor_tensor(out=y, in0=x[:, 1:1 + m], scalar=vecs[:, c + 1:c + 2],
                                                           in1=y, op0=ALU.mult, op1=ALU.add).then_inc(*taps.one())
                            dve.wait_ge(*taps.at(2 * n + 2))
                            nc.vector.scalar_tensor_tensor(out=y, in0=x[:, 2:2 + m], scalar=vecs[:, c + 2:c + 3],
                                                           in1=y, op0=ALU.mult,
                                                           op1=ALU.add).then_inc(*conv_ok.one())
            stage_end()

        def stage_l2(q, kk):
            sq_ok, ss_ok, root_ok, rs_ok, done = (sig("qk_sq"), sig("qk_ss"), sig("qk_root"),
                                                  sig("qk_rstd"), sig("qk_normed"))
            items = [(q[:, i, :], LAT, HD ** -0.5) for i in range(GH)] + \
                    [(kk[:, i, :], TOK, 1.0) for i in range(GH)]
            n_items = len(items)
            with ExitStack() as s:
                sq = sb(s, "l2_sq", 2, TOK)
                root = sb(s, "l2_root", 2, TOK)
                with nc.Block() as block:
                    @block.sync
                    def _(sp):
                        stream_weights(sp, 0)

                    @block.tensor
                    def _(pe):
                        for i in range(n_items):
                            n = items[i][1]
                            pe.wait_ge(*sq_ok.at(i + 1))
                            if i - 1 > 0:
                                pe.wait_ge(*root_ok.at(i - 1))
                            for a, b in ((0, LAT), (LAT, n)):
                                if a < b:
                                    mm = nc.tensor.matmul(pair(i % 2)[:, a:b], ones, sq[:, i % 2, a:b],
                                                          start=True, stop=True)
                            mm.then_inc(*ss_ok.one())

                    @block.scalar
                    def _(act):
                        def square(i):
                            src, n, _ = items[i]
                            if i - 1 > 0:
                                act.wait_ge(*ss_ok.at(i - 1))
                            nc.scalar.activation(sq[:, i % 2, 0:n], src, ACT.Square).then_inc(*sq_ok.one())

                        square(0)
                        for i in range(n_items):
                            if i + 1 < n_items:
                                square(i + 1)
                            n = items[i][1]
                            act.wait_ge(*ss_ok.at(i + 1))
                            if i - 1 > 0:
                                act.wait_ge(*done.at(i - 1))
                            nc.scalar.activation(root[:, i % 2, 0:n], pair(i % 2)[:, 0:n], ACT.Sqrt,
                                                 bias=tab("eps", 0, 1)).then_inc(*root_ok.one())

                    @block.vector
                    def _(dve):
                        for i in range(n_items):
                            src, n, c = items[i]
                            dve.wait_ge(*root_ok.at(i + 1))
                            nc.vector.reciprocal(root[:, i % 2, 0:n], root[:, i % 2, 0:n]).then_inc(*rs_ok.one())
                            dve.wait_ge(*rs_ok.at(i + 1))
                            nc.vector.scalar_tensor_tensor(out=src, in0=src, scalar=c, in1=root[:, i % 2, 0:n],
                                                           op0=ALU.mult, op1=ALU.mult).then_inc(*done.one())
            stage_end()

        def stage_gdn(q, kk, v, beta, log_a, o_tok):
            def S1(name):
                return sig("gdn_" + name)

            sums_ok, exp_ok, be_ok, zero_ok = S1("sums"), S1("exps"), S1("beta_eg"), S1("zero")
            pD, pKK, pQK, pKT, pVT, pPT, pUI = (S1("pe_decay"), S1("pe_kk"), S1("pe_qk"), S1("pe_ktok"),
                                                S1("pe_vtok"), S1("pe_attnT"), S1("pe_u0"))
            pY, pU, pT = S1("pe_y"), S1("pe_u"), S1("pe_t")
            pKS, pO1, pDL, pS, pO2 = S1("pe_ks"), S1("pe_qs"), S1("pe_delta"), S1("pe_state"), S1("pe_attn_v")
            aE, aT, aDL = S1("act_decay"), S1("act_t"), S1("act_delta")
            dN, dU0, dP, dPT, dKD, dBV = (S1("dve_n"), S1("dve_u0"), S1("dve_attn"), S1("dve_attnT"),
                                          S1("dve_kdec"), S1("dve_bv"))
            dY, dU, dR, dS, dO1, dO2 = (S1("dve_y"), S1("dve_u"), S1("dve_rhs"), S1("dve_state"),
                                        S1("dve_o1"), S1("dve_o2"))
            lAu, lT1, lTI, lO = S1("pool_au"), S1("pool_t1"), S1("pool_t0"), S1("pool_o")
            G, STEPS, CS = 4, TT, CTX // P
            HALF = QUAD * P // 2
            order = [[TL + i for i in range(CS)] + list(range(TL)),
                     [TL + CS - 1 - i for i in range(CS)] + list(range(TL - 1, -1, -1))]

            def n_of(t, g):
                return G * t + g + 1

            def l_of(t, lev, g):
                return (LEVELS * t + lev) * G + g + 1

            def t_of(t, lev, g):
                return ((LEVELS - 1) * t + lev) * G + g + 1

            with ExitStack() as s:
                buf = {n: sb(s, "gdn_" + n, G, QUAD * P) for n in
                       ("E", "N", "T", "U", "Y", "kd", "bv", "St", "Pt")}
                fac = sb(s, "gdn_fac", 3, 2 * TT * GH)
                be = sb(s, "gdn_be", 2, TT, GH)
                la = log_a[:].rearrange("p d t h -> p d (t h)")

                def B(name, g):
                    return buf[name][:, g, :]

                def Bh(name, g):
                    return buf[name][:, g, :].rearrange("p (h s) -> p h s", h=QUAD)

                def joined(a, g, lev):
                    b = 2 << lev
                    return a.rearrange("p (n two b) -> p n two b", two=2, b=b)[:, :, 1 if g < 2 else 0, :]

                def packed(a, lev):
                    return a.rearrange("p (n b) -> p n b", b=2 << lev)

                def bank(g, b):
                    return ps[:, 4 * b + g, :]

                def bankh(g, b):
                    return bank(g, b).rearrange("p (h s) -> p h s", h=QUAD)

                def col(a, t, g):
                    d, h0, tile = g // 2, QUAD * (g % 2), order[g // 2][t]
                    return a[:, d, tile, h0:h0 + QUAD].unsqueeze(2).to_broadcast([P, QUAD, P])

                def one_col(a, t, g, h):
                    d = g // 2
                    i = QUAD * (g % 2) + h
                    return a[:, d, order[d][t], i:i + 1]

                def facs(i):
                    return fac[:, i, :].rearrange("p (d t h) -> p d t h", d=2, h=GH)

                def rows(m):
                    return m.unsqueeze(1).to_broadcast([P, QUAD, P])

                def chunk(x, t, g, h):
                    c = order[g // 2][t] * P
                    return x[:, QUAD * (g % 2) + h, c:c + P]

                with nc.Block() as block:
                    @block.sync
                    def _(sp):
                        stream_weights(sp, 0)

                    @block.gpsimd
                    def _(pool):
                        def decay_operand(t, g):
                            nc.gpsimd.tensor_tensor(Bh("T", g), rows(tab("gt" if g < 2 else "lt")),
                                                    col(log_a, t, g), ALU.mult).then_inc(*lAu.one())

                        nc.gpsimd.memset(buf["St"][:], 0.0).then_inc(*zero_ok.one())
                        nc.gpsimd.memset(o_tok[:], 0.0).then_inc(*zero_ok.one())
                        pool.wait_ge(*zero_ok.at(2))
                        for g in range(G):
                            decay_operand(0, g)
                        for t in range(STEPS):
                            for g in range(G):
                                pool.wait_ge(*dN.at(n_of(t, g)))
                                nc.gpsimd.tensor_tensor(Bh("T", g), Bh("N", g),
                                                        rows(tab("lo" if g < 2 else "up")),
                                                        ALU.mult).then_inc(*lT1.one())
                            for g in range(G):
                                pool.wait_ge(*lT1.at(n_of(t, g)))
                                pool.wait_ge(*pUI.at(n_of(t, g)))
                                nc.gpsimd.tensor_tensor(Bh("T", g), rows(ident), Bh("T", g),
                                                        ALU.add).then_inc(*lTI.one())
                            if t + 1 < STEPS:
                                for g in range(G):
                                    pool.wait_ge(*pU.at(l_of(t, LEVELS - 1, g)))
                                    decay_operand(t + 1, g)
                            if t >= CS:
                                for g in range(G):
                                    d, tile, h0 = g // 2, order[g // 2][t], QUAD * (g % 2)
                                    dst = o_tok[:, tile, h0 * P:(h0 + QUAD) * P]
                                    pool.wait_ge(*dO2.at(n_of(t - CS, g)))
                                    if t > CS or g:
                                        pool.wait_ge(*lO.at(n_of(t - CS, g) - 1))
                                    nc.gpsimd.tensor_tensor(dst, dst, B("Y", g), ALU.add).then_inc(*lO.one())

                    @block.scalar
                    def _(act):
                        act.wait_ge(*sums_ok.at(1))
                        nc.scalar.activation(fac[:].rearrange("p a b -> p (a b)"), ps[:, 7, 0:6 * TT * GH],
                                             ACT.Exp).then_inc(*exp_ok.one())
                        for t in range(STEPS):
                            for g in range(G):
                                act.wait_ge(*pD.at(n_of(t, g)))
                                if t > 0:
                                    act.wait_ge(*pS.at(n_of(t - 1, g)))
                                if t > CS:
                                    act.wait_ge(*pO2.at(n_of(t - CS - 1, g)))
                                nc.scalar.activation(B("E", g), bank(g, 0), ACT.Exp).then_inc(*aE.one())
                            for lev in range(LEVELS - 1):
                                for g in range(G):
                                    act.wait_ge(*pT.at(t_of(t, lev, g)))
                                    nc.scalar.copy(B("T", g), bank(g, 1)).then_inc(*aT.one())
                            for g in range(G):
                                act.wait_ge(*pDL.at(n_of(t, g)))
                                nc.scalar.copy(B("E", g), bank(g, 1)).then_inc(*aDL.one())

                    @block.vector
                    def _(dve):
                        def beside_level(t, lev, g):
                            if lev == 0:
                                dve.wait_ge(*pVT.at(n_of(t, g)))
                                if t > 0:
                                    dve.wait_ge(*pDL.at(n_of(t - 1, g)))
                                nc.vector.tensor_tensor(Bh("bv", g), bankh(g, 0), col(beta, t, g),
                                                        ALU.mult).then_inc(*dBV.one())
                            elif lev == 1:
                                dve.wait_ge(*pKT.at(n_of(t, g)))
                                if t > 0:
                                    dve.wait_ge(*pS.at(n_of(t - 1, g)))
                                nc.vector.tensor_tensor(Bh("kd", g), bankh(g, 0), col(facs(1), t, g),
                                                        ALU.mult).then_inc(*dKD.one())
                            elif lev == 2 and t >= CS:
                                dve.wait_ge(*pQK.at(n_of(t - CS, g)))
                                nc.vector.tensor_tensor(B("E", g), B("E", g), bank(g, 0),
                                                        ALU.mult).then_inc(*dP.one())
                            elif lev == 3 and t >= CS:
                                dve.wait_ge(*pPT.at(n_of(t - CS, g)))
                                if t > CS:
                                    dve.wait_ge(*pO2.at(n_of(t - CS - 1, g)))
                                nc.vector.tensor_tensor(Bh("Pt", g), bankh(g, 0),
                                                        rows(tab("le" if g < 2 else "ge")),
                                                        ALU.mult).then_inc(*dPT.one())

                        dve.wait_ge(*exp_ok.at(1))
                        nc.vector.scalar_tensor_tensor(out=be[:], in0=beta[:], scalar=-1.0, in1=facs(0),
                                                       op0=ALU.mult, op1=ALU.mult).then_inc(*be_ok.one())
                        dve.wait_ge(*be_ok.at(1))
                        for t in range(STEPS):
                            for g in range(G):
                                dve.wait_ge(*aE.at(n_of(t, g)))
                                dve.wait_ge(*pKK.at(n_of(t, g)))
                                for h in range(QUAD):
                                    mm = nc.vector.scalar_tensor_tensor(
                                        out=Bh("N", g)[:, h, :], in0=bankh(g, 1)[:, h, :],
                                        scalar=one_col(beta, t, g, h), in1=Bh("E", g)[:, h, :],
                                        op0=ALU.mult, op1=ALU.mult)
                                mm.then_inc(*dN.one())
                            for g in range(G):
                                dve.wait_ge(*pUI.at(n_of(t, g)))
                                if t > 0:
                                    dve.wait_ge(*pDL.at(n_of(t - 1, g)))
                                nc.vector.tensor_tensor(Bh("U", g), bankh(g, 1), rows(ident),
                                                        ALU.add).then_inc(*dU0.one())
                            for lev in range(LEVELS):
                                for g in range(G):
                                    m = tab("join_up" if g < 2 else "join_lo", lev * P // 2, P // 2)
                                    dve.wait_ge(*pY.at(l_of(t, lev, g)))
                                    if lev == 0 and t > CS:
                                        dve.wait_ge(*lO.at(n_of(t - CS - 1, g)))
                                    nc.vector.tensor_tensor(
                                        B("Y", g)[:, 0:HALF].rearrange("p (h s) -> p h s", h=QUAD),
                                        bank(g, 0)[:, 0:HALF].rearrange("p (h s) -> p h s", h=QUAD),
                                        m.unsqueeze(1).to_broadcast([P, QUAD, P // 2]), ALU.mult).then_inc(*dY.one())
                                for g in range(G):
                                    dve.wait_ge(*pU.at(l_of(t, lev, g)))
                                    nc.vector.tensor_tensor(joined(B("U", g), g, lev), joined(B("U", g), g, lev),
                                                            packed(bank(g, 1)[:, 0:HALF], lev),
                                                            ALU.subtract).then_inc(*dU.one())
                                    beside_level(t, lev, g)
                            for g in range(G):
                                dve.wait_ge(*pKS.at(n_of(t, g)))
                                dve.wait_ge(*dBV.at(n_of(t, g)))
                                for h in range(QUAD):
                                    mm = nc.vector.scalar_tensor_tensor(
                                        out=Bh("bv", g)[:, h, :], in0=bankh(g, 0)[:, h, :],
                                        scalar=one_col(be, t, g, h), in1=Bh("bv", g)[:, h, :],
                                        op0=ALU.mult, op1=ALU.add)
                                mm.then_inc(*dR.one())
                                if t >= CS:
                                    dve.wait_ge(*pO1.at(n_of(t - CS, g)))
                                    nc.vector.tensor_tensor(Bh("Y", g), bankh(g, 1), col(facs(0), t, g),
                                                            ALU.mult).then_inc(*dO1.one())
                            for g in range(G):
                                dve.wait_ge(*pS.at(n_of(t, g)))
                                if t > 0:
                                    dve.wait_ge(*dS.at(n_of(t - 1, g)))
                                for h in range(QUAD):
                                    mm = nc.vector.scalar_tensor_tensor(
                                        out=Bh("St", g)[:, h, :], in0=Bh("St", g)[:, h, :],
                                        scalar=one_col(facs(2), t, g, h), in1=bankh(g, 0)[:, h, :],
                                        op0=ALU.mult, op1=ALU.add)
                                mm.then_inc(*dS.one())
                            if t >= CS:
                                for g in range(G):
                                    dve.wait_ge(*pO2.at(n_of(t - CS, g)))
                                    dve.wait_ge(*dO1.at(n_of(t - CS, g)))
                                    nc.vector.tensor_tensor(B("Y", g), B("Y", g), bank(g, 0),
                                                            ALU.add).then_inc(*dO2.one())

                    @block.tensor
                    def _(pe):
                        for d in range(2):
                            for i, m in enumerate((tab("le" if d == 0 else "ge"), tab("gt" if d == 0 else "lt"),
                                                   ones)):
                                c = (2 * i + d) * TT * GH
                                mm = nc.tensor.matmul(ps[:, 7, c:c + TT * GH], m, la[:, d, :],
                                                      start=True, stop=True)
                        mm.then_inc(*sums_ok.one())
                        pe.wait_ge(*exp_ok.at(1))
                        pe.wait_ge(*zero_ok.at(1))

                        def four(dst, lhs, rhs, done):
                            for h in range(QUAD):
                                mm = nc.tensor.matmul(dst[:, h * P:(h + 1) * P], lhs(h), rhs(h),
                                                      start=True, stop=True)
                            mm.then_inc(*done.one())

                        def half_four(dst, lhs, rhs, lev, done):
                            for h in range(QUAD):
                                mm = nc.tensor.matmul(packed(dst[:, h * P // 2:(h + 1) * P // 2], lev), lhs(h),
                                                      rhs(h), start=True, stop=True)
                            mm.then_inc(*done.one())

                        def four_t(dst, src, done):
                            for h in range(QUAD):
                                mm = nc.tensor.transpose(dst[:, h * P:(h + 1) * P], src(h), ident)
                            mm.then_inc(*done.one())

                        def part(name, g):
                            return lambda h: buf[name][:, g, h * P:(h + 1) * P]

                        for t in range(STEPS):
                            for g in range(G):
                                pe.wait_ge(*lAu.at(n_of(t, g)))
                                if t > 0:
                                    pe.wait_ge(*dS.at(n_of(t - 1, g)))
                                if t > CS:
                                    pe.wait_ge(*dO2.at(n_of(t - CS - 1, g)))
                                nc.tensor.matmul(bank(g, 0), tab("le" if g < 2 else "ge"), B("T", g),
                                                 start=True, stop=True).then_inc(*pD.one())
                                if t > 0:
                                    pe.wait_ge(*aDL.at(n_of(t - 1, g)))
                                four(bank(g, 1), lambda h: chunk(kk, t, g, h), lambda h: chunk(kk, t, g, h), pKK)
                            for g in range(G):
                                pe.wait_ge(*lT1.at(n_of(t, g)))
                                four_t(bank(g, 1), part("T", g), pUI)
                            for lev in range(LEVELS):
                                for g in range(G):
                                    if lev == 0:
                                        pe.wait_ge(*dU0.at(n_of(t, g)))
                                    else:
                                        pe.wait_ge(*dU.at(l_of(t, lev - 1, g)))
                                        four_t(bank(g, 1), part("U", g), pT)
                                    if lev == 1:
                                        pe.wait_ge(*dBV.at(n_of(t, g)))
                                    elif lev == 2:
                                        pe.wait_ge(*dKD.at(n_of(t, g)))
                                    elif lev == 3 and t >= CS:
                                        pe.wait_ge(*dP.at(n_of(t - CS, g)))
                                    elif lev == 4 and t >= CS:
                                        pe.wait_ge(*dPT.at(n_of(t - CS, g)))
                                    half_four(bank(g, 0), part("N", g),
                                              lambda h: joined(B("U", g)[:, h * P:(h + 1) * P], g, lev), lev, pY)
                                for g in range(G):
                                    pe.wait_ge(*dY.at(l_of(t, lev, g)))
                                    if lev == 0:
                                        pe.wait_ge(*lTI.at(n_of(t, g)))
                                    else:
                                        pe.wait_ge(*aT.at(t_of(t, lev - 1, g)))
                                    half_four(bank(g, 1), part("T", g),
                                              lambda h: packed(B("Y", g)[:, h * P // 2:(h + 1) * P // 2], lev),
                                              lev, pU)
                                    if lev == 0:
                                        four_t(bank(g, 0), lambda h: chunk(v, t, g, h), pVT)
                                    elif lev == 1:
                                        four_t(bank(g, 0), lambda h: chunk(kk, t, g, h), pKT)
                                    elif lev == 2 and t >= CS:
                                        four(bank(g, 0), lambda h: chunk(q, t, g, h), lambda h: chunk(kk, t, g, h),
                                             pQK)
                                    elif lev == 3 and t >= CS:
                                        four_t(bank(g, 0), part("E", g), pPT)
                            for g in range(G):
                                if t > 0:
                                    pe.wait_ge(*dS.at(n_of(t - 1, g)))
                                four(bank(g, 0), lambda h: chunk(kk, t, g, h), part("St", g), pKS)
                                pe.wait_ge(*dU.at(l_of(t, LEVELS - 1, g)))
                                if t >= CS:
                                    four(bank(g, 1), lambda h: chunk(q, t, g, h), part("St", g), pO1)
                            for g in range(G):
                                pe.wait_ge(*dR.at(n_of(t, g)))
                                if t >= CS:
                                    pe.wait_ge(*dO1.at(n_of(t - CS, g)))
                                four(bank(g, 1), part("U", g), part("bv", g), pDL)
                            for g in range(G):
                                pe.wait_ge(*aDL.at(n_of(t, g)))
                                four(bank(g, 0), part("kd", g), part("E", g), pS)
                            if t >= CS:
                                for g in range(G):
                                    pe.wait_ge(*dS.at(n_of(t, g)))
                                    four(bank(g, 0), part("Pt", g), part("E", g), pO2)
            stage_end()

        def stage_gdn_out(h, o_tok, gdn, attn, y, mats, spill_h, spill_attn):
            z_ok, sq_ok, ss_ok, root_ok = sig("z_silu"), sig("o_sq"), sig("o_ss"), sig("o_root")
            rs_ok, on_ok, tr_ok, done = sig("o_rstd"), sig("o_normed"), sig("o_tr"), sig("gdn_done")
            high, low, mats_in = sig("gdn_hi"), sig("gdn_lo"), sig("mats_landed")
            h_hi, h_lo, a_hi, a_lo = sig("h_hi"), sig("h_lo"), sig("attn_hi"), sig("attn_lo")
            ov = o_tok[:].rearrange("p t (h e) -> p (t h) e", e=P)
            with ExitStack() as s:
                sq = sb(s, "o_sq_buf", TL * GH // 2, P)
                ss = sb(s, "o_ss_buf", TL * GH)
                zs = sb(s, "z_buf", 2, LAT)
                go = sb(s, "gdn_f32", 2, LAT)
                with nc.Block() as block:
                    @block.sync
                    def _(sp):
                        for k in range(KD):
                            sp.dma_start(y[:, k, :], spill_h[k]).then_inc(*norm_in[k].dma())
                        for k in range(KD):
                            sp.wait_ge(*h_lo.at(k + 1))
                            sp.dma_start(y[:, k, :], spill_attn[k]).then_inc(*norm_in[k].dma())
                        stream_weights(sp, GH)
                        sp.dma_start(mats[:], t_mats).then_inc(*mats_in.dma())
                        sp.wait_ge(*mats_in.at(16))

                    @block.tensor
                    def _(pe):
                        pe.wait_ge(*h_lo.at(KD))
                        for n in range(GH):
                            w = unit(pe)
                            if n - 1 > 0:
                                pe.wait_ge(*z_ok.at(n - 1))
                            product(pe, w, h, ps[:, n % 2, :], LAT).then_inc(*unit_used.one())
                            pe.wait_ge(*on_ok.at(1))
                            if n - 1 > 0:
                                pe.wait_ge(*done.at(n - 1))
                            for t in range(TL):
                                mm = nc.tensor.transpose(ps[:, 2 + n % 2, t * P:(t + 1) * P],
                                                         o_tok[:, t, n * P:(n + 1) * P], ident)
                            mm.then_inc(*tr_ok.one())

                    @block.scalar
                    def _(act):
                        split_hi(act, 1)
                        for k in range(KD):
                            act.wait_ge(*norm_in[k].at(16))
                            nc.scalar.copy(h[0][:, k, :], y[:, k, :]).then_inc(*h_hi.one())
                        act.wait_ge(*ss_ok.at(2))
                        nc.scalar.activation(ss[:], ss[:], ACT.Sqrt, scale=1.0 / HD,
                                             bias=tab("eps", 0, 1)).then_inc(*root_ok.one())
                        for n in range(GH):
                            act.wait_ge(*unit_used.at(n + 1))
                            split_hi(act, n + 2)
                            if n - 1 > 0:
                                act.wait_ge(*done.at(n - 1))
                            nc.scalar.activation(zs[:, n % 2, :], ps[:, n % 2, :], ACT.Silu).then_inc(*z_ok.one())
                            act.wait_ge(*done.at(n + 1))
                            nc.scalar.copy(gdn[0][:, n, :], go[:, n % 2, :]).then_inc(*high.one())
                            act.wait_ge(*norm_in[n].at(32))
                            nc.scalar.copy(attn[0][:, n, :], y[:, n, :]).then_inc(*a_hi.one())

                    @block.vector
                    def _(dve):
                        split_lo(dve, 1)
                        for k in range(KD):
                            dve.wait_ge(*h_hi.at(k + 1))
                            nc.vector.tensor_tensor(h[1][:, k, :], y[:, k, :], as_f32(h[0][:, k, :]),
                                                    ALU.subtract).then_inc(*h_lo.one())
                        for c in range(2):
                            half = slice(c * TL * GH // 2, (c + 1) * TL * GH // 2)
                            if c > 0:
                                dve.wait_ge(*ss_ok.at(c))
                            nc.vector.tensor_tensor(sq[:], ov[:, half], ov[:, half], ALU.mult).then_inc(*sq_ok.one())
                            dve.wait_ge(*sq_ok.at(c + 1))
                            nc.vector.reduce_sum(ss[:, half], sq[:], AX_X).then_inc(*ss_ok.one())
                        dve.wait_ge(*root_ok.at(1))
                        nc.vector.reciprocal(ss[:], ss[:]).then_inc(*rs_ok.one())
                        dve.wait_ge(*rs_ok.at(1))
                        nc.vector.tensor_tensor(ov, ov, ss[:].unsqueeze(2).to_broadcast([P, TL * GH, P]),
                                                ALU.mult).then_inc(*on_ok.one())
                        for n in range(GH):
                            split_lo(dve, n + 2)
                            dve.wait_ge(*tr_ok.at(n + 1))
                            dve.wait_ge(*z_ok.at(n + 1))
                            if n - 1 > 0:
                                dve.wait_ge(*low.at(n - 1))
                            nc.vector.scalar_tensor_tensor(out=go[:, n % 2, :], in0=ps[:, 2 + n % 2, :],
                                                           scalar=vec("gdn_norm"), in1=zs[:, n % 2, :],
                                                           op0=ALU.mult, op1=ALU.mult).then_inc(*done.one())
                            dve.wait_ge(*high.at(n + 1))
                            nc.vector.tensor_tensor(gdn[1][:, n, :], go[:, n % 2, :], as_f32(gdn[0][:, n, :]),
                                                    ALU.subtract).then_inc(*low.one())
                            dve.wait_ge(*a_hi.at(n + 1))
                            nc.vector.tensor_tensor(attn[1][:, n, :], y[:, n, :], as_f32(attn[0][:, n, :]),
                                                    ALU.subtract).then_inc(*a_lo.one())
            stage_end()

        def stage_merge(h, attn, gdn, y):
            gate_ok, prod_ok, done = sig("merge_gate"), sig("merge_prod"), sig("merged")
            with ExitStack() as s:
                gate = sb(s, "merge_gates", 2, LAT)
                with nc.Block() as block:
                    @block.sync
                    def _(sp):
                        stream_weights(sp, 4 * KD)

                    @block.tensor
                    def _(pe):
                        for n in range(2 * KD):
                            w = unit(pe)
                            if n - 1 > 0:
                                pe.wait_ge(*gate_ok.at(n - 1))
                            product(pe, w, h, ps[:, n % 2, :], LAT).then_inc(*unit_used.one())
                            w = unit(pe)
                            if n - 1 > 0:
                                pe.wait_ge(*prod_ok.at(n - 1))
                            product(pe, w, (attn, gdn)[n % 2], ps[:, 2 + n % 2, :],
                                    LAT).then_inc(*unit_used.one())

                    @block.scalar
                    def _(act):
                        split_hi(act, 1)
                        for n in range(2 * KD):
                            act.wait_ge(*unit_used.at(2 * n + 1))
                            split_hi(act, 2 * n + 2)
                            if n - 1 > 0:
                                act.wait_ge(*prod_ok.at(n - 1))
                            if n % 2:
                                if n // 2 > 0:
                                    act.wait_ge(*done.at(n // 2))
                            nc.scalar.activation(gate[:, n % 2, :], ps[:, n % 2, :],
                                                 ACT.Sigmoid).then_inc(*gate_ok.one())
                            split_hi(act, 2 * n + 3)

                    @block.vector
                    def _(dve):
                        split_lo(dve, 1)
                        for n in range(2 * KD):
                            split_lo(dve, 2 * n + 2)
                            dve.wait_ge(*gate_ok.at(n + 1))
                            split_lo(dve, 2 * n + 3)
                            dve.wait_ge(*unit_used.at(2 * n + 2))
                            dst = y[:, n // 2, :] if n % 2 == 0 else gate[:, 1, :]
                            nc.vector.tensor_tensor(dst, gate[:, n % 2, :], ps[:, 2 + n % 2, :],
                                                    ALU.mult).then_inc(*prod_ok.one())
                            if n % 2:
                                dve.wait_ge(*prod_ok.at(n + 1))
                                nc.vector.tensor_tensor(y[:, n // 2, :], y[:, n // 2, :], gate[:, 1, :],
                                                        ALU.add).then_inc(*done.one())
            stage_end()

        def stage_project(src, x, nk, gain_of=None, load=None):
            done, high, low = sig("gemm_evac"), sig("src_hi"), sig("src_lo")
            per = -(-nk // 8)
            given = isinstance(src, tuple)
            with ExitStack() as s:
                xs = src if given else (sbr(s, "src_hi_buf", nk, LAT), sbr(s, "src_lo_buf", nk, LAT))
                with nc.Block() as block:
                    @block.sync
                    def _(sp):
                        if load is not None:
                            for k in range(KD):
                                sp.dma_start(x[:, k, :], load[k][:, 0:LAT]).then_inc(*norm_in[k].dma())
                        stream_weights(sp, KD * per)

                    @block.tensor
                    def _(pe):
                        for n in range(KD):
                            if n - 3 > 0:
                                pe.wait_ge(*done.at(n - 3))
                            for u in range(per):
                                w = unit(pe)
                                if given or n:
                                    mm = product(pe, w, xs, ps[:, n % 4, :], LAT, k0=8 * u,
                                                 nk=min(8, nk - 8 * u), start=u == 0, stop=u == per - 1)
                                else:
                                    for k in range(nk):
                                        pe.wait_ge(*low.at(k + 1))
                                        mm = product(pe, tuple(p[:, k * P:(k + 1) * P] for p in w), xs,
                                                     ps[:, 0, :], LAT, k0=k, nk=1, start=k == 0,
                                                     stop=k == nk - 1)
                                mm.then_inc(*unit_used.one())

                    @block.scalar
                    def _(act):
                        split_hi(act, 1)
                        if not given:
                            for k in range(nk):
                                nc.scalar.copy(xs[0][:, k, :], src[:, k, :]).then_inc(*high.one())
                        for j in range(KD * per):
                            act.wait_ge(*unit_used.at(j + 1))
                            split_hi(act, j + 2)

                    @block.vector
                    def _(dve):
                        split_lo(dve, 1)
                        if not given:
                            for k in range(nk):
                                dve.wait_ge(*high.at(k + 1))
                                nc.vector.tensor_tensor(xs[1][:, k, :], src[:, k, :], as_f32(xs[0][:, k, :]),
                                                        ALU.subtract).then_inc(*low.one())
                        for n in range(KD):
                            if load is not None:
                                dve.wait_ge(*norm_in[n].at(16))
                            for u in range(per):
                                split_lo(dve, per * n + u + 2)
                            dve.wait_ge(*unit_used.at(per * (n + 1)))
                            if gain_of is None:
                                nc.vector.tensor_tensor(x[:, n, :], x[:, n, :], ps[:, n % 4, :],
                                                        ALU.add).then_inc(*done.one())
                            else:
                                nc.vector.scalar_tensor_tensor(out=x[:, n, :], in0=ps[:, n % 4, :],
                                                               scalar=gain_of(n), in1=x[:, n, :], op0=ALU.mult,
                                                               op1=ALU.add).then_inc(*done.one())
            stage_end()

        def stage_up(h, mid):
            evac, taps, conv_ok, silu_ok, done = (sig("gemm_evac"), sig("conv_tap"), sig("conv_done"),
                                                  sig("silu_done"), sig("up_done"))
            pad_ok = sig("pad_zero")
            n_items = 2 * KF
            with ExitStack() as s:
                cb = sb(s, "up_in", 2, LAT + 2)
                cv = sb(s, "up_conv", 4, LAT)
                hi_done, lo_done = sig("mid_hi"), sig("mid_lo")
                with nc.Block() as block:
                    @block.sync
                    def _(sp):
                        stream_weights(sp, n_items)

                    @block.gpsimd
                    def _(pool):
                        nc.gpsimd.memset(cb[:], 0.0).then_inc(*pad_ok.one())
                        for j in range(KF):
                            pool.wait_ge(*silu_ok.at(j + 1))
                            pool.wait_ge(*conv_ok.at(2 * j + 2))
                            val = cv[:, (2 * j + 1) % 4, :]
                            nc.gpsimd.tensor_tensor(val, cv[:, (2 * j) % 4, :], val, ALU.mult).then_inc(*done.one())

                    @block.tensor
                    def _(pe):
                        for n in range(n_items):
                            w = unit(pe)
                            if n - 3 > 0:
                                pe.wait_ge(*evac.at(n - 3))
                            product(pe, w, h, ps[:, n % 4, :], LAT).then_inc(*unit_used.one())

                    @block.scalar
                    def _(act):
                        act.wait_ge(*pad_ok.at(1))
                        split_hi(act, 1)

                        def high(j):
                            act.wait_ge(*done.at(j + 1))
                            nc.scalar.copy(mid[0][:, j, :], cv[:, (2 * j + 1) % 4, :]).then_inc(*hi_done.one())

                        for n in range(n_items):
                            act.wait_ge(*unit_used.at(n + 1))
                            split_hi(act, n + 2)
                            if n - 1 > 0:
                                act.wait_ge(*conv_ok.at(n - 1))
                            nc.scalar.copy(cb[:, n % 2, 1:1 + LAT], ps[:, n % 4, :]).then_inc(*evac.one())
                            if n % 2 == 0 and n >= 4:
                                high(n // 2 - 2)
                            if n % 2:
                                act.wait_ge(*conv_ok.at(n))
                                g = cv[:, (n - 1) % 4, :]
                                nc.scalar.activation(g, g, ACT.Silu).then_inc(*silu_ok.one())
                        high(KF - 2)
                        high(KF - 1)

                    @block.vector
                    def _(dve):
                        split_lo(dve, 1)

                        def low(j):
                            dve.wait_ge(*hi_done.at(j + 1))
                            nc.vector.tensor_tensor(mid[1][:, j, :], cv[:, (2 * j + 1) % 4, :], as_f32(mid[0][:, j, :]),
                                                    ALU.subtract).then_inc(*lo_done.one())

                        for n in range(n_items):
                            tile = n // 2 + KF * (n % 2)
                            x, y = cb[:, n % 2, :], cv[:, n % 4, :]
                            c, b = VEC["ffn_w"] + 3 * tile, VEC["ffn_b"] + tile
                            split_lo(dve, n + 2)
                            dve.wait_ge(*evac.at(n + 1))
                            if n // 2 - 1 > 0:
                                dve.wait_ge(*done.at(n // 2 - 1))
                            if n % 2:
                                if n // 2 - 1 > 0:
                                    dve.wait_ge(*lo_done.at(n // 2 - 1))
                            nc.vector.tensor_scalar(y, x[:, 0:LAT], vecs[:, c:c + 1], vecs[:, b:b + 1], ALU.mult,
                                                    ALU.add).then_inc(*taps.one())
                            dve.wait_ge(*taps.at(2 * n + 1))
                            nc.vector.scalar_tensor_tensor(out=y, in0=x[:, 1:1 + LAT], scalar=vecs[:, c + 1:c + 2],
                                                           in1=y, op0=ALU.mult, op1=ALU.add).then_inc(*taps.one())
                            dve.wait_ge(*taps.at(2 * n + 2))
                            nc.vector.scalar_tensor_tensor(out=y, in0=x[:, 2:2 + LAT], scalar=vecs[:, c + 2:c + 3],
                                                           in1=y, op0=ALU.mult,
                                                           op1=ALU.add).then_inc(*conv_ok.one())
                            if n % 2 == 0 and n >= 4:
                                low(n // 2 - 2)
                        low(KF - 2)
                        low(KF - 1)
            stage_end()

        def stage_mixer_inputs(u, pin, gq, gk, gr, gg, qz, dk, dv, gv):
            evac, zeroed = sig("gemm_evac"), sig("pad_zero")
            kinds = [("pin", i) for i in range(2)] + [("gq", 0), ("gk", 0)] + [("gr", i) for i in range(2)] + \
                    [("gg", 0)] + [("dq", i) for i in range(DH2)] + [("dk", i) for i in range(DH2)] + \
                    [("dv", i) for i in range(DH2)] + [("gv", i) for i in range(2)]
            with nc.Block() as block:
                @block.sync
                def _(sp):
                    stream_weights(sp, len(kinds))

                @block.gpsimd
                def _(pool):
                    nc.gpsimd.memset(qz[:], 0.0).then_inc(*zeroed.one())

                @block.tensor
                def _(pe):
                    for n, (kind, i) in enumerate(kinds):
                        w = unit(pe)
                        if n - 3 > 0:
                            pe.wait_ge(*evac.at(n - 3))
                        dst = ps[:, n % 4, :]
                        if kind in ("dv", "gv"):
                            mm = product_tok(pe, w, u, dst, TL, P)
                        else:
                            mm = product(pe, w, u, dst, LAT)
                        mm.then_inc(*unit_used.one())

                @block.scalar
                def _(act):
                    act.wait_ge(*zeroed.at(1))
                    split_hi(act, 1)
                    for n, (kind, i) in enumerate(kinds):
                        act.wait_ge(*unit_used.at(n + 1))
                        split_hi(act, n + 2)
                        b = ps[:, n % 4, :]
                        if kind == "gr":
                            mm = nc.scalar.activation(gr[:, i, :], b, ACT.Silu)
                        elif kind == "gg":
                            mm = nc.scalar.copy(gg[0:16, :], b[0:16, :])
                        elif kind == "dq":
                            for m in range(2):
                                mm = nc.scalar.copy(qz[64 * m:64 * m + 64, m, i, :], b[64 * m:64 * m + 64, :])
                        elif kind in ("dv", "gv"):
                            mm = nc.scalar.copy((dv if kind == "dv" else gv)[:, :, i * P:(i + 1) * P],
                                                b.rearrange("p (t c) -> p t c", c=P))
                        else:
                            dst = {"pin": pin, "gq": gq, "gk": gk, "dk": dk}[kind]
                            mm = nc.scalar.copy(dst[:, i, :] if kind in ("pin", "dk") else dst[:], b)
                        mm.then_inc(*evac.one())

                @block.vector
                def _(dve):
                    for n in range(len(kinds)):
                        split_lo(dve, n)
            stage_end()

        def stage_pool_gla(layer, mats, pin, gq, gk, gr, gg, gv, mix):
            a_ok, d_ok, l_ok, p_ok = sig("gla_act"), sig("gla_dve"), sig("gla_pool"), sig("gla_pe")
            with ExitStack() as s:
                cs_ = sb(s, "pool_csum", 2, 16 + LAT)
                pw = sb(s, "pool_mean", 2, LAT)
                x = sb(s, "gla_x", 3, LAT)
                bc = sb(s, "gla_cum", LAT)
                ex = sb(s, "gla_exp", 3, LAT)
                qd = sb(s, "gla_qdec", LAT)
                ke = x[:, 0, :]
                kp = sb(s, "gla_kinv", 4, LAT)
                vp = sb(s, "gla_vpad", TL, 4, P)
                kt = sb(s, "gla_kend_tok", 2, TL, P)
                at_ = sb(s, "gla_att", TL, 4, P)
                kv = sb(s, "gla_kv", NCH, 256)
                st = sb(s, "gla_state", NCH, 256)
                og = mix[:, 2:4, :]
                rt = mix[:, 4:6, :]
                chunks = lambda a: a.rearrange("p (c i) -> p c i", i=GLA_C)
                with nc.Block() as block:
                    @block.sync
                    def _(sp):
                        stream_weights(sp, 0)

                    @block.gpsimd
                    def _(pool):
                        nc.gpsimd.memset(kp[:], 0.0).then_inc(*l_ok.one())
                        nc.gpsimd.memset(cs_[:], 0.0).then_inc(*l_ok.one())
                        nc.gpsimd.memset(vp[:], 0.0).then_inc(*l_ok.one())
                        nc.gpsimd.memset(st[:, 0, :], 0.0).then_inc(*l_ok.one())
                        pool.wait_ge(*l_ok.at(4))
                        for h in range(4):
                            c = 64 * (h % 2)
                            nc.gpsimd.tensor_copy(vp[:, :, h, c:c + 64],
                                                  gv[:, :, 64 * h:64 * h + 64]).then_inc(*l_ok.one())
                        pool.wait_ge(*d_ok.at(2))
                        for tile in range(2):
                            for half in range(2):
                                w, r = POOL_WINDOWS[2 * tile + half], slice(64 * half, 64 * half + 64)
                                pool.wait_ge(*l_ok.at(8 + 2 * tile + half))
                                nc.gpsimd.tensor_tensor(pw[r, tile, :], cs_[r, tile, 16:16 + LAT],
                                                        cs_[r, tile, 16 - w:16 - w + LAT],
                                                        ALU.subtract).then_inc(*l_ok.one())
                        pool.wait_ge(*l_ok.at(12))
                        nc.gpsimd.tensor_tensor(pw[:].rearrange("p a b -> p (a b)"),
                                                pw[:].rearrange("p a b -> p (a b)"), tab("inv_count", 0, 2 * LAT),
                                                ALU.mult).then_inc(*l_ok.one())
                        pool.wait_ge(*l_ok.at(13))
                        nc.gpsimd.tensor_tensor(pw[:], pw[:], pin[:], ALU.subtract).then_inc(*l_ok.one())

                    @block.scalar
                    def _(act):
                        act.wait_ge(*d_ok.at(4))
                        nc.scalar.activation(x[:, 1, :], x[:, 1, :], ACT.Exp, scale=-1.0).then_inc(*a_ok.one())
                        act.wait_ge(*a_ok.at(1))
                        nc.scalar.activation(x[:, 1, :], x[:, 1, :], ACT.Ln, bias=1.0).then_inc(*a_ok.one())
                        act.wait_ge(*d_ok.at(8))
                        nc.scalar.activation(ex[:, 0, :], bc[:], ACT.Exp).then_inc(*a_ok.one())
                        nc.scalar.activation(ex[:, 1, :], bc[:], ACT.Exp, scale=-1.0).then_inc(*a_ok.one())
                        act.wait_ge(*d_ok.at(9))
                        nc.scalar.activation(ex[:, 2, :], x[:, 2, :], ACT.Exp).then_inc(*a_ok.one())
                        act.wait_ge(*p_ok.at(3))
                        for tile in range(2):
                            nc.scalar.activation(mix[:, tile, :], ps[:, 1 + tile, :], ACT.Copy,
                                                 scale=vec("pool_scale", 2 * layer + tile)).then_inc(*a_ok.one())
                        for p in range(2):
                            act.wait_ge(*p_ok.at(13 + p))
                            nc.scalar.copy(og[:, p, :], ps[:, 4 + p, :]).then_inc(*a_ok.one())
                        act.wait_ge(*a_ok.at(9))
                        for p in range(2):
                            nc.scalar.activation(rt[:, p, :], og[:, p, :], ACT.Square).then_inc(*a_ok.one())
                        for p in range(2):
                            act.wait_ge(*p_ok.at(15 + p))
                            nc.scalar.activation(rt[:, p, :], ps[:, 6 + p, :], ACT.Sqrt, scale=1.0 / 64,
                                                 bias=tab("eps", 0, 1)).then_inc(*a_ok.one())

                    @block.vector
                    def _(dve):
                        dve.wait_ge(*l_ok.at(4))
                        for tile in range(2):
                            nc.vector.tensor_tensor_scan(cs_[:, tile, 16:16 + LAT],
                                                         ones[:, 0:1].to_broadcast([P, LAT]), pin[:, tile, :], 0.0,
                                                         ALU.mult, ALU.add).then_inc(*d_ok.one())
                        dve.wait_ge(*p_ok.at(1))
                        nc.vector.tensor_scalar(x[:, 0, :], ps[:, 0, :], vec("gla_b", layer), None,
                                                ALU.add).then_inc(*d_ok.one())
                        dve.wait_ge(*d_ok.at(3))
                        nc.vector.scalar_tensor_tensor(out=x[:, 1, :], in0=x[:, 0, :], scalar=-1.0,
                                                       in1=x[:, 0, :], op0=ALU.mult,
                                                       op1=ALU.max).then_inc(*d_ok.one())
                        nc.vector.tensor_scalar(x[:, 0, :], x[:, 0, :], 0.0, None, ALU.min).then_inc(*d_ok.one())
                        dve.wait_ge(*d_ok.at(5))
                        dve.wait_ge(*a_ok.at(2))
                        nc.vector.tensor_tensor(x[:, 0, :], x[:, 0, :], x[:, 1, :],
                                                ALU.subtract).then_inc(*d_ok.one())
                        dve.wait_ge(*d_ok.at(6))
                        nc.vector.tensor_scalar(x[:, 0, :], x[:, 0, :], 1.0 / 16, None,
                                                ALU.mult).then_inc(*d_ok.one())
                        dve.wait_ge(*d_ok.at(7))
                        nc.vector.tensor_tensor_scan(bc[:], tab("keep", 0, LAT), x[:, 0, :], 0.0, ALU.mult,
                                                     ALU.add).then_inc(*d_ok.one())
                        dve.wait_ge(*d_ok.at(8))
                        nc.vector.tensor_tensor(chunks(x[:, 2, :]),
                                                chunks(bc[:])[:, :, GLA_C - 1:GLA_C].to_broadcast([P, NCH, GLA_C]),
                                                chunks(bc[:]), ALU.subtract).then_inc(*d_ok.one())
                        dve.wait_ge(*a_ok.at(5))
                        nc.vector.scalar_tensor_tensor(out=qd[:], in0=gq[:], scalar=32 ** -0.5, in1=ex[:, 0, :],
                                                       op0=ALU.mult, op1=ALU.mult).then_inc(*d_ok.one())
                        nc.vector.tensor_tensor(ke, gk[:], ex[:, 2, :], ALU.mult).then_inc(*d_ok.one())
                        for h in range(4):
                            r = slice(32 * h, 32 * h + 32)
                            nc.vector.tensor_tensor(kp[r, h, :], gk[r, :], ex[r, 1, :], ALU.mult).then_inc(*d_ok.one())
                        dve.wait_ge(*p_ok.at(4))
                        for half in range(2):
                            nc.vector.tensor_scalar(kt[:, half, :, :].rearrange("p t c -> p (t c)"), ps[:, 3, :],
                                                    tab("half", half, 1), None, ALU.mult).then_inc(*d_ok.one())
                        for t in range(TL):
                            dve.wait_ge(*p_ok.at(5 + t))
                            nc.vector.tensor_tensor(at_[:, t], ps[:, 4 + t, :].rearrange("p (h c) -> p h c", h=4),
                                                    tab("causal64").unsqueeze(1).to_broadcast([P, 4, P]),
                                                    ALU.mult).then_inc(*d_ok.one())
                        for t in range(TL):
                            dve.wait_ge(*p_ok.at(9 + t))
                            dve.wait_ge(*a_ok.at(7))
                            nc.vector.tensor_tensor(kv[:, 2 * t:2 * t + 2, :],
                                                    ps[:, t, :].rearrange("p (c n) -> p c n", c=2),
                                                    tab("blockdiag", 0, 256).unsqueeze(1).to_broadcast([P, 2, 256]),
                                                    ALU.mult).then_inc(*d_ok.one())
                        for c in range(NCH - 1):
                            dve.wait_ge(*d_ok.at(25 + c))
                            e = ex[:, 0, c * GLA_C + GLA_C - 1:c * GLA_C + GLA_C]
                            nc.vector.scalar_tensor_tensor(out=st[:, c + 1, :], in0=st[:, c, :], scalar=e,
                                                           in1=kv[:, c, :], op0=ALU.mult,
                                                           op1=ALU.add).then_inc(*d_ok.one())
                        for p in range(2):
                            dve.wait_ge(*a_ok.at(12 + p))
                            nc.vector.reciprocal(rt[:, p, :], rt[:, p, :]).then_inc(*d_ok.one())
                            dve.wait_ge(*d_ok.at(33 + 3 * p))
                            nc.vector.scalar_tensor_tensor(out=og[:, p, :], in0=og[:, p, :],
                                                           scalar=vec("gla_norm", 2 * layer + p), in1=rt[:, p, :],
                                                           op0=ALU.mult, op1=ALU.mult).then_inc(*d_ok.one())
                            dve.wait_ge(*d_ok.at(34 + 3 * p))
                            nc.vector.tensor_tensor(mix[:, 6 + p, :], og[:, p, :], gr[:, p, :],
                                                    ALU.mult).then_inc(*d_ok.one())

                    @block.tensor
                    def _(pe):
                        nc.tensor.matmul(ps[:, 0, :], mats[0:16, layer * P:(layer + 1) * P], gg[0:16, :],
                                         start=True, stop=True).then_inc(*p_ok.one())
                        pe.wait_ge(*l_ok.at(14))
                        for tile in range(2):
                            c = (2 + 2 * layer + tile) * P
                            nc.tensor.matmul(ps[:, 1 + tile, :], mats[:, c:c + P], pw[:, tile, :],
                                             start=True, stop=True).then_inc(*p_ok.one())
                        pe.wait_ge(*d_ok.at(15))
                        for t in range(TL):
                            mm = nc.tensor.transpose(ps[:, 3, t * P:(t + 1) * P], ke[:, t * P:(t + 1) * P], ident)
                        mm.then_inc(*p_ok.one())
                        for t in range(TL):
                            for h in range(4):
                                mm = nc.tensor.matmul(ps[:, 4 + t, h * P:(h + 1) * P], kp[:, h, t * P:(t + 1) * P],
                                                      qd[:, t * P:(t + 1) * P], start=True, stop=True)
                            mm.then_inc(*p_ok.one())
                        pe.wait_ge(*d_ok.at(17))
                        pe.wait_ge(*a_ok.at(7))
                        for t in range(TL):
                            for half in range(2):
                                mm = nc.tensor.matmul(ps[:, t, 256 * half:256 * half + 256], kt[:, half, t, :],
                                                      gv[:, t, :], start=True, stop=True)
                            mm.then_inc(*p_ok.one())
                        pe.wait_ge(*d_ok.at(32))
                        for p in range(2):
                            for t in range(TL):
                                o = ps[:, 4 + p, t * P:(t + 1) * P]
                                for i in range(2):
                                    nc.tensor.matmul(o, vp[:, t, 2 * p + i, :], at_[:, t, 2 * p + i, :],
                                                     start=i == 0, stop=False)
                                for half in range(2):
                                    c = 2 * t + half
                                    mm = nc.tensor.matmul(o[:, 64 * half:64 * half + 64],
                                                          st[:, c, p * P:(p + 1) * P],
                                                          qd[:, c * GLA_C:(c + 1) * GLA_C], start=False,
                                                          stop=half == 1)
                            mm.then_inc(*p_ok.one())
                        for p in range(2):
                            pe.wait_ge(*a_ok.at(10 + p))
                            nc.tensor.matmul(ps[:, 6 + p, :], tab("ones64"), rt[:, p, :], start=True,
                                             stop=True).then_inc(*p_ok.one())
            stage_end()

        def stage_diff(layer, qz, dk, dv, mix):
            lam0 = 0.8 - 0.6 * float(np.exp(-0.3 * layer))
            scale = 64 ** -0.5
            s_ok, max_ok, nmax_ok, exp_ok, rinv_ok = (sig("score_done"), sig("max_done"), sig("nmax_done"),
                                                      sig("exp_done"), sig("rinv_done"))
            w_ok, t1_ok, p_ok, t_ok, tev = (sig("weight_done"), sig("map1_done"), sig("prob_done"),
                                            sig("probT_done"), sig("probT_evac"))
            pv_ok, o_ok, lam_ok, lame_ok, lams_ok = (sig("pv_done"), sig("pv_evac"), sig("lam_dve"),
                                                     sig("lam_exp"), sig("lam_sum"))
            sq_ok, ss_ok, root_ok, rs_ok, done = (sig("qk_sq"), sig("qk_ss"), sig("qk_root"), sig("qk_rstd"),
                                                  sig("qk_normed"))
            n_items = DH2 * TL
            with ExitStack() as s:
                pr = sb(s, "diff_probs", 2, 2, LAT)
                pt = sb(s, "diff_probsT", 2, TL, LAT)
                mx = sb(s, "diff_max", n_items, 2)
                nmx = sb(s, "diff_nmax", n_items, 2)
                rsum = sb(s, "diff_sum", n_items, 2)
                rinv = sb(s, "diff_inv", n_items, 2)
                lam = sb(s, "diff_lam", 8)
                gain = sb(s, "diff_gain", DH2)
                o = sb(s, "diff_o", DH2, LAT)
                rt = sb(s, "diff_root", DH2, LAT)
                with nc.Block() as block:
                    @block.sync
                    def _(sp):
                        stream_weights(sp, 0)

                    @block.tensor
                    def _(pe):
                        pe.wait_ge(*lam_ok.at(1))
                        nc.tensor.matmul(ps[:, 7, 0:2], ones, lam[:, 0:2], start=True,
                                         stop=True).then_inc(*lams_ok.one())

                        def scores(i):
                            h, t = divmod(i, TL)
                            if 2 * (i - 1) > 0:
                                pe.wait_ge(*exp_ok.at(2 * (i - 1)))
                            for m in range(2):
                                b = ps[:, 2 * (i % 2) + m, :]
                                nc.tensor.matmul(b[:, 0:(t + 1) * P], qz[:, m, h, t * P:(t + 1) * P],
                                                 dk[:, h, 0:(t + 1) * P], start=True, stop=False)
                                mm = nc.tensor.matmul(b[:, t * P:(t + 1) * P], tab("mask_q"), tab("mask_k"),
                                                      start=False, stop=True)
                            mm.then_inc(*s_ok.one())

                        scores(0)
                        for i in range(n_items):
                            h, t = divmod(i, TL)
                            if i + 1 < n_items:
                                scores(i + 1)
                            pe.wait_ge(*p_ok.at(i + 1))
                            if i - 1 > 0:
                                pe.wait_ge(*tev.at(i - 1))
                            for k in range(t + 1):
                                mm = nc.tensor.transpose(ps[:, 4 + i % 2, k * P:(k + 1) * P],
                                                         pr[:, i % 2, 0, k * P:(k + 1) * P], ident)
                            mm.then_inc(*t_ok.one())
                            if t == TL - 1:
                                pe.wait_ge(*tev.at(i + 1))
                                if h - 1 > 0:
                                    pe.wait_ge(*o_ok.at(h - 1))
                                if h == 1:
                                    pe.wait_ge(*lame_ok.at(1))
                                for k in range(TL):
                                    mm = nc.tensor.matmul(ps[:, 6 + h % 2, k * P:LAT],
                                                          dv[:, k, h * P:(h + 1) * P], pt[:, h % 2, k, k * P:LAT],
                                                          start=k == 0, stop=k == TL - 1)
                                mm.then_inc(*pv_ok.one())
                        for h in range(DH2):
                            pe.wait_ge(*sq_ok.at(h + 1))
                            nc.tensor.matmul(ps[:, h, :], ones, rt[:, h, :], start=True,
                                             stop=True).then_inc(*ss_ok.one())

                    @block.scalar
                    def _(act):
                        act.wait_ge(*lams_ok.at(1))
                        nc.scalar.activation(lam[:, 2:4], ps[:, 7, 0:2], ACT.Exp).then_inc(*lame_ok.one())
                        for i in range(n_items):
                            h, t = divmod(i, TL)
                            act.wait_ge(*nmax_ok.at(i + 1))
                            if i - 1 > 0:
                                act.wait_ge(*t_ok.at(i - 1))
                            for m in range(2):
                                nc.scalar.activation(pr[:, i % 2, m, 0:(t + 1) * P],
                                                     ps[:, 2 * (i % 2) + m, 0:(t + 1) * P], ACT.Exp, scale=scale,
                                                     bias=nmx[:, i, m:m + 1],
                                                     accum_out=rsum[:, i, m:m + 1]).then_inc(*exp_ok.one())
                            act.wait_ge(*t_ok.at(i + 1))
                            if h - 1 > 0:
                                act.wait_ge(*pv_ok.at(h - 1))
                            nc.scalar.copy(pt[:, h % 2, 0:t + 1, t * P:(t + 1) * P],
                                           ps[:, 4 + i % 2, 0:(t + 1) * P].rearrange("p (k c) -> p k c", c=P)
                                           ).then_inc(*tev.one())
                            if t == TL - 1:
                                act.wait_ge(*pv_ok.at(h + 1))
                                nc.scalar.copy(o[:, h, :], ps[:, 6 + h % 2, :]).then_inc(*o_ok.one())
                        for h in range(DH2):
                            act.wait_ge(*o_ok.at(h + 1))
                            nc.scalar.activation(rt[:, h, :], o[:, h, :], ACT.Square).then_inc(*sq_ok.one())
                        for h in range(DH2):
                            act.wait_ge(*ss_ok.at(h + 1))
                            nc.scalar.activation(rt[:, h, :], ps[:, h, :], ACT.Sqrt, scale=1.0 / P,
                                                 bias=tab("eps", 0, 1)).then_inc(*root_ok.one())

                    @block.vector
                    def _(dve):
                        lv = vec("lam", 4 * layer, 4).rearrange("p (m w) -> p w m", w=2)
                        nc.vector.tensor_tensor(lam[:, 0:2], lv[:, 0], lv[:, 1], ALU.mult).then_inc(*lam_ok.one())
                        dve.wait_ge(*lame_ok.at(1))
                        nc.vector.scalar_tensor_tensor(out=lam[:, 4:5], in0=lam[:, 3:4], scalar=lam0,
                                                       in1=lam[:, 2:3], op0=ALU.subtract,
                                                       op1=ALU.subtract).then_inc(*lam_ok.one())
                        nc.vector.tensor_scalar(gain[:], vec("diff_norm", DH2 * layer, DH2), 1.0 - lam0, None,
                                                ALU.mult).then_inc(*lam_ok.one())
                        dve.wait_ge(*lam_ok.at(3))

                        def maximum(i):
                            n = (i % TL + 1) * P
                            b = 2 * (i % 2)
                            dve.wait_ge(*s_ok.at(i + 1))
                            nc.vector.reduce_max(mx[:, i, :], ps[:, b:b + 2, 0:n], AX_X).then_inc(*max_ok.one())
                            dve.wait_ge(*max_ok.at(i + 1))
                            nc.vector.tensor_scalar(nmx[:, i, :], mx[:, i, :], -scale, None,
                                                    ALU.mult).then_inc(*nmax_ok.one())

                        maximum(0)
                        for i in range(n_items):
                            n = (i % TL + 1) * P
                            if i + 1 < n_items:
                                maximum(i + 1)
                            dve.wait_ge(*exp_ok.at(2 * i + 2))
                            nc.vector.reciprocal(rinv[:, i, :], rsum[:, i, :]).then_inc(*rinv_ok.one())
                            dve.wait_ge(*rinv_ok.at(i + 1))
                            nc.vector.tensor_tensor(mx[:, i, 1:2], rinv[:, i, 1:2], lam[:, 4:5],
                                                    ALU.mult).then_inc(*w_ok.one())
                            dve.wait_ge(*w_ok.at(i + 1))
                            nc.vector.tensor_scalar(pr[:, i % 2, 1, 0:n], pr[:, i % 2, 1, 0:n], mx[:, i, 1:2], None,
                                                    ALU.mult).then_inc(*t1_ok.one())
                            dve.wait_ge(*t1_ok.at(i + 1))
                            nc.vector.scalar_tensor_tensor(out=pr[:, i % 2, 0, 0:n], in0=pr[:, i % 2, 0, 0:n],
                                                           scalar=rinv[:, i, 0:1], in1=pr[:, i % 2, 1, 0:n],
                                                           op0=ALU.mult, op1=ALU.add).then_inc(*p_ok.one())
                        for h in range(DH2):
                            dve.wait_ge(*root_ok.at(h + 1))
                            nc.vector.reciprocal(rt[:, h, :], rt[:, h, :]).then_inc(*rs_ok.one())
                            dve.wait_ge(*rs_ok.at(h + 1))
                            nc.vector.scalar_tensor_tensor(out=mix[:, 2 + h, :], in0=o[:, h, :],
                                                           scalar=gain[:, h:h + 1], in1=rt[:, h, :],
                                                           op0=ALU.mult, op1=ALU.mult).then_inc(*done.one())
            stage_end()

        def stage_mlp1(z, mid, n_tiles):
            evac, high, squared, low = sig("gemm_evac"), sig("mid_hi"), sig("mid_sq"), sig("mid_lo")
            with ExitStack() as s:
                r = sb(s, "relu", 2, LAT)
                r2 = sb(s, "relu_sq", 2, LAT)
                with nc.Block() as block:
                    @block.sync
                    def _(sp):
                        stream_weights(sp, n_tiles)

                    @block.tensor
                    def _(pe):
                        for n in range(n_tiles):
                            w = unit(pe)
                            if n - 3 > 0:
                                pe.wait_ge(*evac.at(n - 3))
                            product(pe, w, z, ps[:, n % 4, :], LAT).then_inc(*unit_used.one())

                    @block.scalar
                    def _(act):
                        split_hi(act, 1)
                        for n in range(n_tiles):
                            act.wait_ge(*unit_used.at(n + 1))
                            split_hi(act, n + 2)
                            if n - 1 > 0:
                                act.wait_ge(*squared.at(n - 1))
                            nc.scalar.activation(r[:, n % 2, :], ps[:, n % 4, :], ACT.Relu).then_inc(*evac.one())
                            act.wait_ge(*evac.at(n + 1))
                            nc.scalar.activation(mid[0][:, n, :], r[:, n % 2, :],
                                                 ACT.Square).then_inc(*high.one())

                    @block.vector
                    def _(dve):
                        split_lo(dve, 1)
                        for n in range(n_tiles):
                            split_lo(dve, n + 2)
                            dve.wait_ge(*evac.at(n + 1))
                            nc.vector.tensor_tensor(r2[:, n % 2, :], r[:, n % 2, :], r[:, n % 2, :],
                                                    ALU.mult).then_inc(*squared.one())
                            dve.wait_ge(*squared.at(n + 1))
                            dve.wait_ge(*high.at(n + 1))
                            nc.vector.tensor_tensor(mid[1][:, n, :], r2[:, n % 2, :], as_f32(mid[0][:, n, :]),
                                                    ALU.subtract).then_inc(*low.one())
            stage_end()

        def lat_mod(j):
            return lambda k, part: mod[:, j * KD + k, part:part + 1]

        def spill(name):
            return nc.dram_tensor(name, (KD, P, LAT), F32, kind="Internal").ap()

        def split_pair(ctx, name, *shape):
            return sbr(ctx, name + "_hi", *shape), sbr(ctx, name + "_lo", *shape)

        spill_h, spill_attn = spill("spill_h"), spill("spill_attn")
        with ExitStack() as s:
            o_tok = sb(s, "o_tok", TL, GH * P)
            with ExitStack() as s2:
                gk_ = sb(s2, "gdn_k", GH, TOK)
                gv_ = sb(s2, "gdn_v", GH, TOK)
                gq_ = sb(s2, "gdn_q", GH, LAT)
                beta = sb(s2, "gdn_beta", 2, TT, GH)
                log_a = sb(s2, "gdn_log_a", 2, TT, GH)
                with ExitStack() as s3:
                    h = split_pair(s3, "h", KD, TOK)
                    cs = sb(s3, "silu_c_buf", 16)
                    stage_modulation()
                    stage_norm(gk_, h, TOK, lat_mod(1), lat_mod(0), load=t_x)
                    vtok = gv_[:, 0:2, :].rearrange("p a n -> p (a n)").rearrange("p (t c) -> p t c", t=TT)
                    stage_attn_inputs(h, gq_, gk_, vtok)
                    probs_t = o_tok[:].rearrange("p t n -> p (t n)")[:, 0:TT * LAT].rearrange("p (t n) -> p t n", t=TT)
                    stage_attention(gq_, gk_, vtok, probs_t, spill_attn)
                    stage_gdn_inputs(h, gq_, gk_, gv_, beta, log_a, spill_h)
                stage_l2(gq_, gk_)
                stage_gdn(gq_, gk_, gv_, beta, log_a, o_tok)
            mats = sb(s, "mats", 6 * P)
            with ExitStack() as s2:
                y = sb(s2, "y", KD, LAT)
                with ExitStack() as s3:
                    h = split_pair(s3, "h_lat", KD, LAT)
                    attn = split_pair(s3, "attn_back", KD, LAT)
                    gdn = split_pair(s3, "gdn_o", GH, LAT)
                    stage_gdn_out(h, o_tok, gdn, attn, y, mats, spill_h, spill_attn)
                    stage_merge(h, attn, gdn, y)
                x = o_tok[:].rearrange("p t n -> p (t n)").rearrange("p (k n) -> p k n", k=KD)
                stage_project(y, x, KD, gain_of=lambda n: mod[:, 2 * KD + n, 0:1], load=t_x)
            with ExitStack() as s2:
                mid = split_pair(s2, "mid", KF, LAT)
                with ExitStack() as s3:
                    h = split_pair(s3, "h_ffn", KD, LAT)
                    stage_norm(x, h, LAT, lat_mod(4), lat_mod(3))
                    stage_up(h, mid)
                stage_project(mid, x, KF, gain_of=lambda n: mod[:, 5 * KD + n, 0:1])
            stage_norm(x, x, LAT, lambda k, part: vec("final", k))

            for layer in range(DEPTH2):
                with ExitStack() as s2:
                    mix = sb(s2, "mix", KD, LAT)
                    pin = sb(s2, "pool_in", 2, LAT)
                    gq, gk = sb(s2, "gla_q", LAT), sb(s2, "gla_k", LAT)
                    gr, gg = sb(s2, "gla_r", 2, LAT), sb(s2, "gla_g", LAT)
                    gv = sb(s2, "gla_v", TL, 256)
                    qz, dk = sb(s2, "diff_q", 2, DH2, LAT), sb(s2, "diff_k", DH2, LAT)
                    dv = sb(s2, "diff_v", TL, DH2 * P)
                    with ExitStack() as s3:
                        u = split_pair(s3, "u", KD, LAT)
                        stage_norm(x, u, LAT, lambda k, part: vec("norm1", KD * layer + k))
                        stage_mixer_inputs(u, pin, gq, gk, gr, gg, qz, dk, dv, gv)
                    stage_pool_gla(layer, mats, pin, gq, gk, gr, gg, gv, mix)
                    stage_diff(layer, qz, dk, dv, mix)
                    stage_project(mix, x, KD)
                with ExitStack() as s2:
                    z = split_pair(s2, "z_mlp", KD, LAT)
                    mid = split_pair(s2, "mid2", KF2 // 2, LAT)
                    stage_norm(x, z, LAT, lambda k, part: vec("norm2", KD * layer + k))
                    for _half in range(2):
                        stage_mlp1(z, mid, KF2 // 2)
                        stage_project(mid, x, KF2 // 2)
            stage_norm(x, x, LAT, lambda k, part: vec("final2", k), store=out)
        assert at["used"] == len(units)


def _units(w, cols=P, kt=8):
    k, n = w.shape
    out = []
    for j in range(n // cols):
        for a in range(0, k // P, kt):
            b = min(kt, k // P - a)
            t = w[a * P:(a + b) * P, j * cols:(j + 1) * cols].reshape(b, P, cols).transpose(1, 0, 2)
            out.append(t.reshape(P, b * cols))
    return out


def _columns(a):
    return np.asarray(a).reshape(-1, P).T


def kernel(**inputs):
    import concourse.bacc as bacc
    from concourse.bass_utils import run_bass_kernel_spmd

    i = {k: np.asarray(v) for k, v in inputs.items()}
    f32 = np.float32
    xt = np.concatenate([i["x"][0].T, i["ctx"][0].T], 1).reshape(KD, P, TOK)

    vecs = np.zeros((P, NVEC), f32)

    def put(name, a, at=0):
        c = VEC[name] + at
        vecs[:a.shape[0], c:c + a.shape[1]] = a

    put("c", np.stack([_columns(i["c"][0]), _columns(i["c_ctx"])], 2).reshape(P, 16))
    put("b_mod", _columns(i["b_mod"][0]))
    put("q_norm", _columns(i["q_norm_w"][0]))
    put("k_norm", _columns(i["k_norm_w"][0]))
    put("conv_qkv", i["conv_qkv_w"][0].reshape(3, 24, P).transpose(2, 1, 0).reshape(P, 72))
    put("gdn_norm", _columns(i["gdn_norm_w"][0]))
    put("ffn_w", i["ffn_conv_w"][0].reshape(3, 44, P).transpose(2, 1, 0).reshape(P, 132))
    put("ffn_b", _columns(i["ffn_conv_b"][0]))
    put("final", _columns(i["final_norm_w"]))
    put("a_log", np.broadcast_to(i["a_log"].reshape(1, 16), (P, 16)))
    put("dt_bias", np.broadcast_to(i["dt_bias"].reshape(1, 16), (P, 16)))
    put("final2", _columns(i["final_norm_g_2"]))
    mats = np.zeros((P, 6 * P), f32)
    for l in range(DEPTH2):
        put("norm1", _columns(i["norm1_g_2"][l]), KD * l)
        put("norm2", _columns(i["norm2_g_2"][l]), KD * l)
        put("diff_norm", _columns(i["diff_norm_g_2"][l]), DH2 * l)
        put("gla_norm", _columns(i["gla_norm_g_2"][l]), 2 * l)
        put("gla_b", _columns(i["gla_b_gate_2"][l]), l)
        put("pool_scale", _columns(i["pool_scale_2"][l]), 2 * l)
        put("lam", np.stack([i[f"diff_{n}_2"][l] for n in ("lq1", "lk1", "lq2", "lk2")], 1), 4 * l)
        mats[0:16, l * P:(l + 1) * P] = i["gla_w_gate2_2"][l]
        for g in range(4):
            r, c = 64 * (g % 2), (2 + 2 * l + g // 2) * P + 64 * (g % 2)
            mats[r:r + 64, c:c + 64] = i["pool_w_2"][l, g]
    tabs, rope = shape_tables()

    w = i["w_in"][0]
    o = np.cumsum([0, 256, 256, 3072, 16, 16, 1024, 1024, 2048])
    ak, av, qkv, db, da, aq, z, gates = [w[:, o[n]:o[n + 1]] for n in range(8)]
    ga, gd = _units(gates[:, :D]), _units(gates[:, D:])
    pa, pd = _units(i["w_pa"][0]), _units(i["w_pd"][0])
    up = _units(i["w_up"][0])
    mod = _units(i["w_mod"][0])
    weights = {
        "mod_first": mod[:MOD_FIRST],
        "mod_rest": mod[MOD_FIRST:],
        "attn_in": _units(ak) + _units(av) + _units(aq),
        "gates": _units(np.concatenate([db, da], 1), 32),
        "gdn_in": _units(qkv),
        "z": _units(z),
        "merge": [u for j in range(KD) for u in (ga[j], pa[j], gd[j], pd[j])],
        "out": _units(i["w_out"][0]),
        "up": [up[j + KF * s] for j in range(KF) for s in range(2)],
        "down": _units(i["w_down"][0]),
    }
    for l in range(DEPTH2):
        w = i["w_in_2"][l]
        o = np.cumsum([0, 256, 512, 512, 512, 128, 128, 256, 256, 16])
        p_in, dq, dk, dv, gq, gk, gv, gr, gg = [w[:, o[n]:o[n + 1]] for n in range(9)]
        gg = np.pad(gg, ((0, 0), (0, P - gg.shape[1])))
        weights[f"in2_{l}"] = [u for m in (p_in, gq, gk, gr, gg, dq, dk, dv, gv) for u in _units(m)]
        weights[f"out2_{l}"] = _units(i["w_out_2"][l])
        up, down = _units(i["w_mlp1_2"][l]), _units(i["w_mlp2_2"][l])
        for s, half in enumerate("ab"):
            weights[f"mlp1{half}_{l}"] = up[s * KF2 // 2:(s + 1) * KF2 // 2]
            weights[f"mlp2{half}_{l}"] = [u for j in range(KD) for u in down[4 * j + 2 * s:4 * j + 2 * s + 2]]

    nc = bacc.Bacc("TRN2", target_bir_lowering=False, num_devices=1)
    arrays = {}

    def dram(name, a):
        a = arrays[f"in_{name}"] = np.ascontiguousarray(a)
        return nc.dram_tensor(f"in_{name}", a.shape, F32, kind="ExternalInput").ap()

    t_w = {}
    for name, us in weights.items():
        widths = sorted({u.shape[1] for u in us})
        if len(widths) == 1:
            t = dram(f"w_{name}", np.stack(us))
            t_w[name] = [t[n] for n in range(len(us))]
        else:
            t = {c: dram(f"w_{name}_{c}", np.stack([u for u in us if u.shape[1] == c])) for c in widths}
            at = dict.fromkeys(widths, 0)
            t_w[name] = []
            for u in us:
                c = u.shape[1]
                t_w[name].append(t[c][at[c]])
                at[c] += 1
    out = nc.dram_tensor("out", (KD, P, LAT), F32, kind="ExternalOutput").ap()
    build(nc, dram("vecs", vecs), dram("mats", mats), dram("tabs", tabs), dram("rope", rope),
          dram("xt", xt), t_w, out)
    r = run_bass_kernel_spmd(nc, [arrays], core_ids=[0])
    got = np.asarray(r.results[0]["out"])
    return np.ascontiguousarray(got.reshape(D, LAT).T)[None]
```

```python
from contextlib import ExitStack

import concourse.bass as bass
import numpy as np
from concourse import mybir

F32 = mybir.dt.float32
F32R = mybir.dt.float32r
ALU = mybir.AluOpType
ACT = mybir.ActivationFunctionType
AX_X = mybir.AxisListType.X

P = 128
D = 1024
KD = D // P
LAT, CTX = 512, 256
TOK = LAT + CTX
TT, TL = TOK // P, LAT // P
EPS = 1e-6
HD = 128
HEADS, KV_HEADS = 8, 2
GROUP = HEADS // KV_HEADS
GH = 8
FF = 2816
KF = FF // P
GRID_W = 64
ROPE_THETA = 10000.0
QUAD = 4
LEVELS = 6
DEPTH2 = 2
FF2 = 4096
KF2 = FF2 // P
DH2 = 4
GLA_C = 64
NCH = LAT // GLA_C
RING = 4
UNIT = 8 * P
MOD_FIRST = 16
BIG = -1.0e30
POOL_WINDOWS = (2, 4, 8, 16)

VEC = {}


def _vec_columns():
    at = 0
    for name, n in (("c", 16), ("b_mod", 48), ("q_norm", 1), ("k_norm", 1), ("conv_qkv", 72),
                    ("gdn_norm", 1), ("ffn_w", 132), ("ffn_b", 44), ("final", 8), ("a_log", 16),
                    ("dt_bias", 16), ("norm1", 16), ("norm2", 16), ("final2", 8), ("diff_norm", 8),
                    ("gla_norm", 4), ("gla_b", 2), ("pool_scale", 4), ("lam", 8)):
        VEC[name] = at
        at += n
    return at


NVEC = _vec_columns()

TAB = {}


def _table_columns():
    at = 0
    for name, n in (("ident", P), ("ones", P), ("le", P), ("ge", P), ("lt", P), ("gt", P),
                    ("up", P), ("lo", P), ("join_up", LEVELS * P // 2), ("join_lo", LEVELS * P // 2),
                    ("rot", P), ("ones64", P), ("causal64", P),
                    ("blockdiag", 256), ("half", 2), ("keep", LAT), ("inv_count", 2 * LAT),
                    ("mask_q", P), ("mask_k", P), ("eps", 1)):
        TAB[name] = at
        at += n
    return at


NTAB = _table_columns()


def shape_tables():
    r, c = np.arange(P)[:, None], np.arange(P)[None, :]
    t = np.zeros((P, NTAB), np.float32)

    def put(name, a):
        t[:, TAB[name]:TAB[name] + a.shape[1]] = a

    put("ident", (r == c) * 1.0)
    put("ones", np.ones((P, P)))
    put("le", (r <= c) * 1.0)
    put("ge", (r >= c) * 1.0)
    put("lt", (r < c) * 1.0)
    put("gt", (r > c) * 1.0)
    up = [((r // b) % 2 == 0) & (c // b == r // b + 1) for b in (1, 2, 4, 8, 16, 32, 64)]
    put("up", up[0] * -1.0)
    put("lo", up[0].T * -1.0)
    odd = [np.arange(P) // b % 2 == 1 for b in (2, 4, 8, 16, 32, 64)]
    put("join_up", np.concatenate([u[:, o] for u, o in zip(up[1:], odd)], 1) * 1.0)
    put("join_lo", np.concatenate([u.T[:, ~o] for u, o in zip(up[1:], odd)], 1) * 1.0)
    rot = np.zeros((P, P))
    for a in range(2):
        for i in range(32):
            rot[a * 64 + 32 + i, a * 64 + i] = -1.0
            rot[a * 64 + i, a * 64 + 32 + i] = 1.0
    put("rot", rot)
    put("ones64", (r // 64 == c // 64) * 1.0)
    put("causal64", ((r // 64 == c // 64) & (r <= c)) * 1.0)
    put("blockdiag", (np.arange(P)[:, None] // 32 == np.arange(256)[None, :] // 64) * 1.0)
    put("half", (r // 64 == np.arange(2)[None, :]) * 1.0)
    put("keep", np.broadcast_to((np.arange(LAT) % GLA_C != 0)[None, :] * 1.0, (P, LAT)))
    win = np.array([[POOL_WINDOWS[2 * tile + (p // 64)] for p in range(P)] for tile in range(2)])
    cnt = np.minimum(np.arange(LAT)[None, None, :] + 1, win[:, :, None])
    put("inv_count", (1.0 / cnt).transpose(1, 0, 2).reshape(P, 2 * LAT))
    put("mask_q", np.where(r == 0, (c < 64) * BIG, 0.0))
    put("mask_k", np.where(r == 0, (c >= 64) * 1.0, 0.0))
    put("eps", np.full((P, 1), EPS))
    tok = np.arange(LAT, dtype=np.float32)
    inv = np.float32(ROPE_THETA) ** (-np.arange(0, 64, 2, dtype=np.float32) / np.float32(64))
    row, col = np.floor(tok / GRID_W), tok % GRID_W
    ang = np.stack([(row[None, :] * inv[:, None]), (col[None, :] * inv[:, None])]).astype(np.float32)
    ang = np.repeat(ang[:, None], 2, 1).reshape(P, LAT)
    rope = np.concatenate([np.cos(ang), np.sin(ang)], 1).astype(np.float32)
    return t, rope


class Signal:

    def __init__(self, sem):
        self.sem, self.base, self.total = sem, 0, 0

    def one(self):
        self.total += 1
        return self.sem, 1

    def dma(self):
        self.total += 16
        return self.sem, 16

    def at(self, n):
        return self.sem, self.base + n


def build(nc, t_vecs, t_mats, t_tabs, t_rope, t_x, t_w, out):
    with ExitStack() as top:
        signals = {}

        def sig(name):
            if name not in signals:
                signals[name] = Signal(top.enter_context(nc.semaphore(name)))
            return signals[name]

        def stage_end():
            for s in signals.values():
                s.base = s.total

        taken = {}

        def sb(ctx, name, *shape):
            taken[name] = taken.get(name, 0) + 1
            name = name if taken[name] == 1 else f"{name}_{taken[name]}"
            return ctx.enter_context(nc.sbuf_tensor(name, [P, *shape], F32))

        def sbr(ctx, name, *shape):
            taken[name] = taken.get(name, 0) + 1
            name = name if taken[name] == 1 else f"{name}_{taken[name]}"
            return ctx.enter_context(nc.sbuf_tensor(name, [P, *shape], F32R))

        def as_f32(a):
            return a.bitcast(F32)

        ring = sb(top, "ring", RING, UNIT)
        w_hi, w_lo = sbr(top, "w_hi", 2, UNIT), sbr(top, "w_lo", 2, UNIT)
        vecs = sb(top, "vecs", NVEC)
        tabs = sb(top, "tabs", NTAB)
        mod = sb(top, "mod", 48, 2)
        ps = top.enter_context(nc.psum_tensor("ps", [P, 8, 512], F32))

        def vec(name, i=0, n=1):
            return vecs[:, VEC[name] + i:VEC[name] + i + n]

        def tab(name, i=0, n=P):
            return tabs[:, TAB[name] + i:TAB[name] + i + n]

        ident, ones = tab("ident"), tab("ones")

        units, whole = [], []

        def add(name, split=True):
            units.extend(t_w[name])
            whole.extend([not split] * len(t_w[name]))

        add("mod_first", split=False)
        add("attn_in")
        add("mod_rest", split=False)
        for name in ("gates", "gdn_in", "z", "merge", "out", "up", "down"):
            add(name)
        for layer in range(DEPTH2):
            for name in ("in2", "out2", "mlp1a", "mlp2a", "mlp1b", "mlp2b"):
                add(f"{name}_{layer}")
        n_split = [n - sum(whole[:n]) for n in range(len(units))]
        loaded = [top.enter_context(nc.semaphore(f"unit_loaded{s}")) for s in range(RING)]
        unit_used, hi_ok, lo_ok = sig("unit_used"), sig("w_hi_made"), sig("w_lo_made")
        at = {"issued": 0, "used": 0, "hi": 0, "lo": 0}

        def stream_weights(sp, n_stage):
            at["stage_end"] = unit_used.base + max(n_stage, 1)
            last = min(at["used"] + n_stage + RING, len(units))
            for n in range(at["issued"], last):
                m = n - RING
                if m >= 0 and whole[m]:
                    sp.wait_ge(unit_used.sem, m + 1)
                elif m >= 0:
                    sp.wait_ge(lo_ok.sem, n_split[m] + 1)
                w = units[n]
                sp.dma_start(ring[:, n % RING, 0:w.shape[1]], w).then_inc(loaded[n % RING], 16)
            at["issued"] = last

        def ready_to_split(which, j):
            at[which] = max(at[which], unit_used.base)
            while at[which] <= min(unit_used.base + j, at["stage_end"]) and at[which] < len(units) and not whole[at[which]]:
                n = at[which]
                at[which] += 1
                yield n, n_split[n] % 2, units[n].shape[1]

        def split_hi(act, j):
            for n, slot, width in ready_to_split("hi", j):
                act.wait_ge(loaded[n % RING], 16 * (n // RING + 1))
                if n >= 2:
                    act.wait_ge(unit_used.sem, n - 1)
                nc.scalar.copy(w_hi[:, slot, 0:width], ring[:, n % RING, 0:width]).then_inc(*hi_ok.one())

        def split_lo(dve, j):
            for n, slot, width in ready_to_split("lo", j):
                dve.wait_ge(hi_ok.sem, n_split[n] + 1)
                if n >= 2:
                    dve.wait_ge(unit_used.sem, n - 1)
                nc.vector.tensor_tensor(w_lo[:, slot, 0:width], ring[:, n % RING, 0:width],
                                        as_f32(w_hi[:, slot, 0:width]), ALU.subtract).then_inc(*lo_ok.one())

        def unit(pe):
            n = at["used"]
            at["used"] += 1
            if whole[n]:
                pe.wait_ge(loaded[n % RING], 16 * (n // RING + 1))
                return ring[:, n % RING, :]
            pe.wait_ge(lo_ok.sem, n_split[n] + 1)
            return w_hi[:, n_split[n] % 2, :], w_lo[:, n_split[n] % 2, :]

        def pair(n):
            return ps[:, 2 * (n % 4):2 * (n % 4) + 2, :].rearrange("p b n -> p (b n)")

        def product(pe, w, src, dst, n_tok, k0=0, nk=KD, start=True, stop=True):
            for k in range(nk):
                for wi, xi in ((0, 0), (0, 1), (1, 0)):
                    for a, b in ((0, min(n_tok, LAT)), (LAT, n_tok)):
                        if a < b:
                            mm = nc.tensor.matmul(dst[:, a:b], w[wi][:, k * P:(k + 1) * P],
                                                  src[xi][:, k0 + k, a:b], start=start and k == wi == xi == 0,
                                                  stop=stop and k == nk - 1 and wi == 1)
            return mm

        def product_tok(pe, w, src, dst_of, n_tiles, cols, k0=0, nk=KD, start=True, stop=True):
            for t in range(n_tiles):
                for k in range(nk):
                    for xi, wi in ((0, 0), (0, 1), (1, 0)):
                        mm = nc.tensor.matmul(dst_of(t), src[xi][:, k0 + k, t * P:(t + 1) * P],
                                              w[wi][:, k * cols:(k + 1) * cols],
                                              start=start and k == wi == xi == 0,
                                              stop=stop and k == nk - 1 and xi == 1)
            return mm

        def mod_rows(pe, half, dst):
            cv = cs[:].rearrange("p (k v) -> p k v", v=2)
            w = unit(pe)
            for k in range(4):
                mm = nc.tensor.matmul(dst, cv[:, 4 * half + k, :], w[:, k * 2 * P:(k + 1) * 2 * P],
                                      start=half == 0 and k == 0, stop=half == 1 and k == 3)
            mm.then_inc(*unit_used.one())

        def mod_columns(g, rows, bank, turned):
            for c in range(2):
                j = 2 * g + c
                mm = nc.tensor.transpose(ps[:, bank, 2 * j:2 * j + 2], rows[:, c * P:(c + 1) * P], ident[0:2, 0:2])
            mm.then_inc(*turned.one())

        def mod_bias(dve, a, b, bank, mod_b):
            nc.vector.tensor_tensor(mod[:, a:b, :], ps[:, bank, 2 * a:2 * b].rearrange("p (j v) -> p j v", v=2),
                                    vec("b_mod", a, b - a).unsqueeze(2).to_broadcast([P, b - a, 2]),
                                    ALU.add).then_inc(*mod_b.one())
            dve.wait_ge(*mod_b.at(1))
            c = KD if a == 0 else 4 * KD
            nc.vector.tensor_scalar(mod[:, c:c + KD, :], mod[:, c:c + KD, :], 1.0, None,
                                    ALU.add).then_inc(*mod_b.one())

        norm_in = [sig(f"norm_in{k}") for k in range(KD)]

        def stage_modulation(x, scratch, sq_scratch):
            sq_ok, sum_ok = sig("norm_sq"), sig("norm_sum")
            sq = sq_scratch[:].rearrange("p h n -> p (h n)")[:, 0:2 * TOK].rearrange("p (b n) -> p b n", b=2)
            landed, tabs_in, silu_c, mod_b = sig("vecs_landed"), sig("tabs_landed"), sig("silu_c"), sig("mod_b")
            rows_ok, turned = sig("mod_rows"), sig("mod_turned")
            rows = scratch[0:2, :, 0:2 * P]
            with nc.Block() as block:
                @block.sync
                def _(sp):
                    sp.dma_start(vecs[:], t_vecs).then_inc(*landed.dma())
                    for n in range(MOD_FIRST + RING):
                        if n >= RING:
                            sp.wait_ge(*unit_used.at(n - RING + 1))
                        sp.dma_start(ring[:, n % RING, 0:units[n].shape[1]], units[n]).then_inc(loaded[n % RING], 16)
                        if n == RING - 1:
                            sp.dma_start(tabs[:], t_tabs).then_inc(*tabs_in.dma())
                        if 0 <= n - RING < KD:
                            k = n - RING
                            sp.dma_start(x[:, k, :], t_x[k]).then_inc(*norm_in[k].dma())
                    at["issued"] = MOD_FIRST + RING

                @block.scalar
                def _(act):
                    act.wait_ge(*landed.at(16))
                    nc.scalar.activation(cs[:], vec("c", 0, 16), ACT.Silu).then_inc(*silu_c.one())
                    for k in range(KD):
                        act.wait_ge(*norm_in[k].at(16))
                        if k > 1:
                            act.wait_ge(*sum_ok.at(k - 1))
                        nc.scalar.activation(sq[:, k % 2, :], x[:, k, :], ACT.Square).then_inc(*sq_ok.one())

                @block.tensor
                def _(pe):
                    pe.wait_ge(*silu_c.at(1))
                    for g in range(MOD_FIRST // 2):
                        if g > 1:
                            pe.wait_ge(*rows_ok.at(g - 1))
                        for half in range(2):
                            mod_rows(pe, half, ps[0:2, 1 + g % 2, 0:2 * P])
                        for k in (2 * g - 4, 2 * g - 3):
                            if 0 <= k < KD:
                                pe.wait_ge(*tabs_in.at(16))
                                pe.wait_ge(*sq_ok.at(k + 1))
                                for a, b in ((0, LAT), (LAT, TOK)):
                                    mm = nc.tensor.matmul(pair(2)[:, a:b], ones, sq[:, k % 2, a:b],
                                                          start=k == 0, stop=k == KD - 1)
                                mm.then_inc(*sum_ok.one())
                    for g in range(MOD_FIRST // 2):
                        pe.wait_ge(*rows_ok.at(g + 1))
                        mod_columns(g, rows[:, g], 0, turned)

                @block.vector
                def _(dve):
                    for g in range(MOD_FIRST // 2):
                        dve.wait_ge(*unit_used.at(2 * g + 2))
                        nc.vector.tensor_copy(rows[:, g], ps[0:2, 1 + g % 2, 0:2 * P]).then_inc(*rows_ok.one())
                    dve.wait_ge(*turned.at(MOD_FIRST // 2))
                    mod_bias(dve, 0, MOD_FIRST, 0, mod_b)
            stage_end()

        def norm_steps(ctx, src, dst, n_tok, scale_of, shift_of=None, summed=False):
            sq_ok, sum_ok, root_ok, rstd_ok = (sig("norm_sq"), sig("norm_sum"), sig("norm_root"),
                                               sig("norm_rstd"))
            scaled, high, low = sig("norm_scaled"), sig("norm_hi"), sig("norm_low")
            parts = [(0, LAT)] + ([(LAT, TOK)] if n_tok > LAT else [])
            np_ = len(parts)
            split = dst is not src
            sq = sb(ctx, "norm_sq_buf", 2, n_tok)
            root = sb(ctx, "norm_root_buf", n_tok)
            acc = pair(2)

            def norm_act(act):
                if not summed:
                    for k in range(KD):
                        if k > 1:
                            act.wait_ge(*sum_ok.at(k - 1))
                        nc.scalar.activation(sq[:, k % 2, :], src[:, k, 0:n_tok], ACT.Square).then_inc(*sq_ok.one())
                    act.wait_ge(*sum_ok.at(KD))
                nc.scalar.activation(root[:], acc[:, 0:n_tok], ACT.Sqrt, scale=1.0 / D,
                                     bias=tab("eps", 0, 1)).then_inc(*root_ok.one())
                split_hi(act, 1)
                if split:
                    for k in range(KD):
                        for p, (a, b) in enumerate(parts):
                            act.wait_ge(*scaled.at(np_ * k + p + 1))
                            x, y = sq[:, k % 2, a:b], dst[0][:, k, a:b]
                            if shift_of is None:
                                mm = nc.scalar.copy(y, x)
                            else:
                                mm = nc.scalar.activation(y, x, ACT.Identity, bias=shift_of(k, p))
                            mm.then_inc(*high.one())

            def norm_pe(pe):
                if not summed:
                    for k in range(KD):
                        pe.wait_ge(*sq_ok.at(k + 1))
                        for a, b in parts:
                            mm = nc.tensor.matmul(acc[:, a:b], ones, sq[:, k % 2, a:b],
                                                  start=k == 0, stop=k == KD - 1)
                        mm.then_inc(*sum_ok.one())

            def norm_dve(dve):
                def low_parts(k):
                    for p, (a, b) in enumerate(parts):
                        dve.wait_ge(*high.at(np_ * k + p + 1))
                        x, hi, lo = sq[:, k % 2, a:b], as_f32(dst[0][:, k, a:b]), dst[1][:, k, a:b]
                        if shift_of is None:
                            mm = nc.vector.tensor_tensor(lo, x, hi, ALU.subtract)
                        else:
                            mm = nc.vector.scalar_tensor_tensor(out=lo, in0=x, scalar=shift_of(k, p),
                                                                in1=hi, op0=ALU.add, op1=ALU.subtract)
                        mm.then_inc(*low.one())

                dve.wait_ge(*root_ok.at(1))
                nc.vector.reciprocal(root[:], root[:]).then_inc(*rstd_ok.one())
                split_lo(dve, 1)
                dve.wait_ge(*rstd_ok.at(1))
                for k in range(KD):
                    if split and k > 1:
                        dve.wait_ge(*low.at(np_ * (k - 1)))
                    for p, (a, b) in enumerate(parts):
                        y = sq[:, k % 2, a:b] if split else dst[:, k, a:b]
                        nc.vector.scalar_tensor_tensor(
                            out=y, in0=src[:, k, a:b], scalar=scale_of(k, p),
                            in1=root[:, a:b], op0=ALU.mult, op1=ALU.mult).then_inc(*scaled.one())
                    if split and k >= 1:
                        low_parts(k - 1)
                if split:
                    low_parts(KD - 1)

            return norm_act, norm_pe, norm_dve

        def product_of_norm(pe, w, src, dst):
            low = sig("norm_low")
            for k in range(KD):
                pe.wait_ge(*low.at(k + 1))
                mm = product(pe, tuple(p[:, k * P:(k + 1) * P] for p in w), src, dst, LAT, k0=k, nk=1,
                             start=k == 0, stop=k == KD - 1)
            return mm

        def stage_norm(src, dst, n_tok, *args, store=None, **kwargs):
            scaled, stored = sig("norm_scaled"), sig("norm_stored")
            with ExitStack() as s:
                norm_act, norm_pe, norm_dve = norm_steps(s, src, dst, n_tok, *args, **kwargs)
                with nc.Block() as block:
                    @block.sync
                    def _(sp):
                        stream_weights(sp, 0)
                        if store is not None:
                            for k in range(KD):
                                sp.wait_ge(*scaled.at(k + 1))
                                sp.dma_start(store[k], dst[:, k, :]).then_inc(*stored.dma())
                            sp.wait_ge(*stored.at(16 * KD))

                    @block.scalar
                    def _(act):
                        norm_act(act)

                    @block.tensor
                    def _(pe):
                        norm_pe(pe)

                    @block.vector
                    def _(dve):
                        norm_dve(dve)
            stage_end()

        def stage_attn_inputs(h, norm, q, kk, vtok, spare):
            evac = sig("gemm_evac")
            rope_in, sq_ok, ss_ok, root_ok = sig("rope_in"), sig("qk_sq"), sig("qk_ss"), sig("qk_root")
            rs_ok, n_ok, rot_ok = sig("qk_rstd"), sig("qk_normed"), sig("qk_rot")
            cos_ok, sin_ok, done = sig("qk_cos"), sig("qk_sin"), sig("qk_done")
            items = [(kk[:, i, :], TOK, "k_norm") for i in range(KV_HEADS)] + \
                    [(q[:, i, :], LAT, "q_norm") for i in range(HEADS)]
            n_items = len(items)
            with ExitStack() as s:
                norm_act, norm_pe, norm_dve = norm_steps(s, *norm, summed=True)
                h_low = sig("norm_low")
                sq, root = (spare[:].rearrange("p t n -> p (t n)")[:, a * 2 * TOK:(a + 1) * 2 * TOK]
                            .rearrange("p (b n) -> p b n", b=2) for a in range(2))
                t1 = sb(s, "qk_t1", 2, LAT)
                rope = sb(s, "rope", 2 * LAT)
                with nc.Block() as block:
                    @block.sync
                    def _(sp):
                        sp.dma_start(rope[:], t_rope).then_inc(*rope_in.dma())
                        stream_weights(sp, 2 + n_items)

                    @block.tensor
                    def _(pe):
                        norm_pe(pe)
                        for a in range(2):
                            w = unit(pe)
                            pe.wait_ge(*h_low.at(2 * 4 * (a + 1)))
                            product_tok(pe, w, h, lambda t: ps[:, 2 + t, 0:KV_HEADS * P], TT, KV_HEADS * P, k0=4 * a,
                                        nk=4, start=a == 0, stop=a == 1).then_inc(*unit_used.one())
                        for n in range(n_items + 2):
                            if n < n_items:
                                w = unit(pe)
                                if n > 0:
                                    pe.wait_ge(*evac.at(n))
                                product(pe, w, h, pair(n % 2), items[n][1]).then_inc(*unit_used.one())
                            if 1 <= n <= n_items:
                                i = n - 1
                                pe.wait_ge(*sq_ok.at(i + 1))
                                if i > 0:
                                    pe.wait_ge(*root_ok.at(i))
                                for a, b in ((0, LAT), (LAT, items[i][1])):
                                    if a < b:
                                        mm = nc.tensor.matmul(pair(2)[:, a:b], ones, sq[:, i % 2, a:b],
                                                              start=True, stop=True)
                                mm.then_inc(*ss_ok.one())
                            if n >= 2:
                                i = n - 2
                                pe.wait_ge(*n_ok.at(i + 1))
                                if i > 1:
                                    pe.wait_ge(*sin_ok.at(i - 1))
                                nc.tensor.matmul(ps[:, 6 + i % 2, :], tab("rot"), items[i][0][:, 0:LAT],
                                                 start=True, stop=True).then_inc(*rot_ok.one())

                    @block.scalar
                    def _(act):
                        norm_act(act)
                        split_hi(act, 1)
                        act.wait_ge(*unit_used.at(1))
                        split_hi(act, 2)
                        act.wait_ge(*unit_used.at(2))
                        split_hi(act, 3)
                        nc.scalar.copy(vtok, ps[:, 2:2 + TT, 0:KV_HEADS * P]).then_inc(*evac.one())
                        for n in range(n_items + 1):
                            if n < n_items:
                                src, m, _ = items[n]
                                act.wait_ge(*unit_used.at(n + 3))
                                split_hi(act, n + 4)
                                nc.scalar.copy(src, pair(n % 2)[:, 0:m]).then_inc(*evac.one())
                                if n > 1:
                                    act.wait_ge(*ss_ok.at(n - 1))
                                act.wait_ge(*evac.at(n + 2))
                                nc.scalar.activation(sq[:, n % 2, 0:m], src, ACT.Square).then_inc(*sq_ok.one())
                            if n > 0:
                                i = n - 1
                                m = items[i][1]
                                act.wait_ge(*ss_ok.at(i + 1))
                                if i > 1:
                                    act.wait_ge(*n_ok.at(i - 1))
                                nc.scalar.activation(root[:, i % 2, 0:m], pair(2)[:, 0:m], ACT.Sqrt,
                                                     scale=1.0 / HD, bias=tab("eps", 0, 1)).then_inc(*root_ok.one())

                    @block.vector
                    def _(dve):
                        norm_dve(dve)
                        for j in range(4):
                            split_lo(dve, j)
                        for n in range(n_items + 2):
                            if n < n_items:
                                split_lo(dve, n + 4)
                            if 1 <= n <= n_items:
                                i = n - 1
                                src, m, gain = items[i]
                                dve.wait_ge(*root_ok.at(i + 1))
                                nc.vector.reciprocal(root[:, i % 2, 0:m], root[:, i % 2, 0:m]).then_inc(*rs_ok.one())
                                dve.wait_ge(*rs_ok.at(i + 1))
                                nc.vector.scalar_tensor_tensor(out=src, in0=src, scalar=vec(gain),
                                                               in1=root[:, i % 2, 0:m], op0=ALU.mult,
                                                               op1=ALU.mult).then_inc(*n_ok.one())
                            if n >= 2:
                                i = n - 2
                                dve.wait_ge(*rot_ok.at(i + 1))
                                if i > 1:
                                    dve.wait_ge(*done.at(i - 1))
                                dve.wait_ge(*rope_in.at(16))
                                nc.vector.tensor_tensor(t1[:, i % 2, :], ps[:, 6 + i % 2, :], rope[:, LAT:],
                                                        ALU.mult).then_inc(*sin_ok.one())

                    @block.gpsimd
                    def _(pool):
                        pool.wait_ge(*rope_in.at(16))
                        for i in range(n_items):
                            x = items[i][0][:, 0:LAT]
                            pool.wait_ge(*rot_ok.at(i + 1))
                            nc.gpsimd.tensor_tensor(x, x, rope[:, 0:LAT], ALU.mult).then_inc(*cos_ok.one())
                            pool.wait_ge(*cos_ok.at(i + 1))
                            pool.wait_ge(*sin_ok.at(i + 1))
                            nc.gpsimd.tensor_tensor(x, x, t1[:, i % 2, :], ALU.add).then_inc(*done.one())
            stage_end()

        def stage_attention(q, kk, vtok, pt, spill):
            s_ok, max_ok, nmax_ok, exp_ok, rinv_ok = (sig("score_done"), sig("max_done"), sig("nmax_done"),
                                                      sig("exp_done"), sig("rinv_done"))
            p_ok, t_ok, tev, pv_ok, o_ok = (sig("prob_done"), sig("probT_done"), sig("probT_evac"),
                                            sig("pv_done"), sig("pv_evac"))
            spilled = [sig("attn_spilled0"), sig("attn_spilled1")]
            mod_b, rows_ok, turned = sig("mod_b"), sig("mod_rows"), sig("mod_turned")
            n_rest = 6 * KD - MOD_FIRST
            n_items = HEADS * TL
            scale = HD ** -0.5
            with ExitStack() as s:
                pr = sb(s, "probs", 2, TOK)
                o = sb(s, "attn_out", 2, LAT)
                rows = sb(s, "mod_rows_buf", 2, 2 * P)
                row_bank = ps[0:2, 7, 2 * P:4 * P]
                mx = sb(s, "row_max", n_items)
                nmx = sb(s, "neg_max", n_items)
                rsum = sb(s, "row_sum", n_items)
                rinv = sb(s, "row_inv", n_items)
                pt_bank = ps[:, 4:6, :].rearrange("p b n -> p (b n)")
                with nc.Block() as block:
                    @block.sync
                    def _(sp):
                        per = n_rest // HEADS
                        for h in range(HEADS):
                            stream_weights(sp, per * (h + 1))
                            sp.wait_ge(*o_ok.at(h + 1))
                            sp.dma_start(spill[h], o[:, h % 2, :]).then_inc(*spilled[h % 2].dma())
                        for c in range(2):
                            sp.wait_ge(*spilled[c].at(8 * HEADS))

                    @block.tensor
                    def _(pe):
                        def scores(i):
                            h, t = divmod(i, TL)
                            if i > 1:
                                pe.wait_ge(*exp_ok.at(i - 1))
                            for a, b in ((0, LAT), (LAT, TOK)):
                                mm = nc.tensor.matmul(pair(i % 2)[:, a:b], q[:, h, t * P:(t + 1) * P],
                                                      kk[:, h // GROUP, a:b], start=True, stop=True)
                            mm.then_inc(*s_ok.one())

                        scores(0)
                        scores(1)
                        for i in range(n_items):
                            h, t = divmod(i, TL)
                            if i + 2 < n_items:
                                scores(i + 2)
                            if i % 2 == 0 and i > 0:
                                pe.wait_ge(*rows_ok.at(i // 2))
                                mod_columns((MOD_FIRST + i) // 2 - 1, rows[0:2, (i // 2 - 1) % 2], 7, turned)
                            mod_rows(pe, i % 2, row_bank)
                            pe.wait_ge(*p_ok.at(i + 1))
                            if i > 0:
                                pe.wait_ge(*tev.at(i))
                            for k in range(TT):
                                mm = nc.tensor.transpose(pt_bank[:, k * P:(k + 1) * P],
                                                         pr[:, i % 2, k * P:(k + 1) * P], ident)
                            mm.then_inc(*t_ok.one())
                            if t == TL - 1:
                                pe.wait_ge(*tev.at(i + 1))
                                if h > 0:
                                    pe.wait_ge(*o_ok.at(h))
                                for k in range(TT):
                                    c = (h // GROUP) * P
                                    mm = nc.tensor.matmul(ps[:, 6, :], vtok[:, k, c:c + P],
                                                          pt[:, k, :], start=k == 0, stop=k == TT - 1)
                                mm.then_inc(*pv_ok.one())
                        pe.wait_ge(*rows_ok.at(n_rest // 2))
                        mod_columns(3 * KD - 1, rows[0:2, (n_rest // 2 - 1) % 2], 7, turned)

                    @block.vector
                    def _(dve):
                        def maximum(i):
                            dve.wait_ge(*s_ok.at(i + 1))
                            nc.vector.reduce_max(mx[:, i:i + 1], pair(i % 2)[:, 0:TOK], AX_X).then_inc(*max_ok.one())
                            dve.wait_ge(*max_ok.at(i + 1))
                            nc.vector.tensor_scalar(nmx[:, i:i + 1], mx[:, i:i + 1], -scale, None,
                                                    ALU.mult).then_inc(*nmax_ok.one())

                        maximum(0)
                        maximum(1)
                        for i in range(n_items):
                            dve.wait_ge(*exp_ok.at(i + 1))
                            nc.vector.reciprocal(rinv[:, i:i + 1], rsum[:, i:i + 1]).then_inc(*rinv_ok.one())
                            dve.wait_ge(*rinv_ok.at(i + 1))
                            nc.vector.tensor_scalar(pr[:, i % 2, :], pr[:, i % 2, :], rinv[:, i:i + 1], None,
                                                    ALU.mult).then_inc(*p_ok.one())
                            if i + 2 < n_items:
                                maximum(i + 2)
                            if i % 2:
                                dve.wait_ge(*unit_used.at(i + 1))
                                nc.vector.tensor_copy(rows[0:2, (i // 2) % 2], row_bank).then_inc(*rows_ok.one())
                        dve.wait_ge(*turned.at(n_rest // 2))
                        mod_bias(dve, MOD_FIRST, 6 * KD, 7, mod_b)

                    @block.scalar
                    def _(act):
                        def exponentials(i):
                            act.wait_ge(*nmax_ok.at(i + 1))
                            if i > 1:
                                act.wait_ge(*t_ok.at(i - 1))
                            nc.scalar.activation(pr[:, i % 2, :], pair(i % 2)[:, 0:TOK], ACT.Exp, scale=scale,
                                                 bias=nmx[:, i:i + 1],
                                                 accum_out=rsum[:, i:i + 1]).then_inc(*exp_ok.one())

                        exponentials(0)
                        for i in range(n_items):
                            h, t = divmod(i, TL)
                            if i + 1 < n_items:
                                exponentials(i + 1)
                            act.wait_ge(*t_ok.at(i + 1))
                            if h > 0:
                                act.wait_ge(*pv_ok.at(h))
                            nc.scalar.copy(pt[:, :, t * P:(t + 1) * P],
                                           pt_bank[:, 0:TOK].rearrange("p (k c) -> p k c", c=P)).then_inc(*tev.one())
                            if t == TL - 1:
                                act.wait_ge(*pv_ok.at(h + 1))
                                if h >= 2:
                                    act.wait_ge(*spilled[h % 2].at(16 * (h // 2)))
                                nc.scalar.copy(o[:, h % 2, :], ps[:, 6, :]).then_inc(*o_ok.one())
            stage_end()

        def stage_gdn_inputs(h, q, kk, v, beta, log_a, spare, spill):
            sq_ok, ss_ok, root_ok, rs_ok, scaled = (sig("qk_sq"), sig("qk_ss"), sig("qk_root"),
                                                    sig("qk_rstd"), sig("qk_normed"))
            sq, root = (spare[:].rearrange("p t n -> p (t n)")[:, a * 2 * TOK:(a + 1) * 2 * TOK]
                        .rearrange("p (b n) -> p b n", b=2) for a in range(2))
            evac, taps, conv_ok, silu_ok = (sig("gemm_evac"), sig("conv_tap"), sig("conv_done"),
                                            sig("silu_done"))
            pad_ok, ga_ok, gd_ok = sig("pad_zero"), sig("gate_act"), sig("gate_dve")
            spilled, whole_ok = [sig("h_spilled0"), sig("h_spilled1")], sig("h_whole")
            dst = [q[:, i, :] for i in range(GH)] + [kk[:, i, :] for i in range(GH)] + \
                  [v[:, i, :] for i in range(GH)]
            n_items = len(dst)
            n_unit = 2 * GH

            def width(i):
                return LAT if i < GH else TOK

            wide = TOK + 4
            c0 = LAT + 3
            with ExitStack() as s:
                cb = sb(s, "conv_in", 2, wide)
                cv = sb(s, "conv_out", 2, wide)
                gt = sb(s, "gate_tmp", 6, 96)
                hw = sb(s, "h_whole_buf", 2, LAT)
                with nc.Block() as block:
                    @block.sync
                    def _(sp):
                        stream_weights(sp, n_items + 1)
                        for k in range(KD):
                            sp.wait_ge(*whole_ok.at(k + 1))
                            sp.dma_start(spill[k], hw[:, k % 2, :]).then_inc(*spilled[k % 2].dma())
                        for c in range(2):
                            sp.wait_ge(*spilled[c].at(8 * KD))

                    @block.gpsimd
                    def _(pool):
                        nc.gpsimd.memset(cb[:], 0.0).then_inc(*pad_ok.one())
                        for k in range(KD):
                            if k >= 2:
                                pool.wait_ge(*spilled[k % 2].at(16 * (k // 2)))
                            nc.gpsimd.tensor_tensor(hw[:, k % 2, :], as_f32(h[0][:, k, 0:LAT]),
                                                    as_f32(h[1][:, k, 0:LAT]), ALU.add).then_inc(*whole_ok.one())

                    @block.tensor
                    def _(pe):
                        w = unit(pe)
                        product_tok(pe, w, h, lambda t: ps[:, 7, t * 32:(t + 1) * 32], TT, 32).then_inc(*unit_used.one())
                        for n in range(n_items):
                            w = unit(pe)
                            if n > 2:
                                pe.wait_ge(*evac.at(n - 2))
                            product(pe, w, h, pair(n % 3), width(n)).then_inc(*unit_used.one())
                            i = n - 2
                            if 0 <= i < n_unit:
                                pe.wait_ge(*sq_ok.at(i + 1))
                                if i == 0:
                                    pe.wait_ge(*gd_ok.at(1))
                                else:
                                    pe.wait_ge(*root_ok.at(i))
                                for a, b in ((0, LAT), (LAT, width(i))):
                                    if a < b:
                                        mm = nc.tensor.matmul(pair(3)[:, a:b], ones, sq[:, i % 2, a:b],
                                                              start=True, stop=True)
                                mm.then_inc(*ss_ok.one())

                    @block.scalar
                    def _(act):
                        split_hi(act, 2)
                        act.wait_ge(*unit_used.at(1))
                        raw = ps[:, 7, 0:192].rearrange("p (t s c) -> p s t c", s=2, c=16)
                        gv = [gt[:, i, :].rearrange("p (t c) -> p t c", c=16) for i in range(6)]
                        nc.scalar.activation(beta[:].rearrange("p d t h -> p t d h"),
                                             raw[:, 0].rearrange("p t (d h) -> p t d h", d=2),
                                             ACT.Sigmoid).then_inc(*ga_ok.one())
                        act.wait_ge(*gd_ok.at(2))
                        nc.scalar.activation(gt[:, 2, :], gt[:, 1, :], ACT.Exp, scale=-1.0).then_inc(*ga_ok.one())
                        nc.scalar.activation(gt[:, 5, 0:16], vec("a_log", 0, 16), ACT.Exp).then_inc(*ga_ok.one())
                        act.wait_ge(*ga_ok.at(3))
                        nc.scalar.activation(gt[:, 3, :], gt[:, 2, :], ACT.Ln, bias=1.0).then_inc(*ga_ok.one())
                        act.wait_ge(*pad_ok.at(1))

                        def silu(n):
                            act.wait_ge(*conv_ok.at(n + 1))
                            mm = nc.scalar.activation(dst[n][:, 0:LAT], cv[:, n % 2, 0:LAT], ACT.Silu)
                            if n >= GH:
                                mm = nc.scalar.activation(dst[n][:, LAT:TOK], cv[:, n % 2, LAT + 2:TOK + 2],
                                                          ACT.Silu)
                            mm.then_inc(*silu_ok.one())

                        for n in range(n_items):
                            act.wait_ge(*unit_used.at(n + 2))
                            split_hi(act, n + 3)
                            if n > 1:
                                act.wait_ge(*conv_ok.at(n - 1))
                            mm = nc.scalar.copy(cb[:, n % 2, 1:1 + LAT], pair(n % 3)[:, 0:LAT])
                            if n >= GH:
                                mm = nc.scalar.copy(cb[:, n % 2, c0:c0 + CTX], pair(n % 3)[:, LAT:TOK])
                            mm.then_inc(*evac.one())
                            if n >= 1:
                                silu(n - 1)
                            i = n - 2
                            if 0 <= i < n_unit:
                                act.wait_ge(*ss_ok.at(i + 1))
                                if i > 1:
                                    act.wait_ge(*scaled.at(i - 1))
                                nc.scalar.activation(root[:, i % 2, 0:width(i)], pair(3)[:, 0:width(i)], ACT.Sqrt,
                                                     bias=tab("eps", 0, 1)).then_inc(*root_ok.one())
                            i = n - 1
                            if 0 <= i < n_unit:
                                if i > 1:
                                    act.wait_ge(*ss_ok.at(i - 1))
                                act.wait_ge(*silu_ok.at(i + 1))
                                nc.scalar.activation(sq[:, i % 2, 0:width(i)], dst[i][:, 0:width(i)],
                                                     ACT.Square).then_inc(*sq_ok.one())
                        silu(n_items - 1)

                    @block.vector
                    def _(dve):
                        split_lo(dve, 2)
                        dve.wait_ge(*ga_ok.at(1))
                        raw = ps[:, 7, 0:192].rearrange("p (t s c) -> p s t c", s=2, c=16)
                        gv = [gt[:, i, :].rearrange("p (t c) -> p t c", c=16) for i in range(6)]
                        nc.vector.tensor_tensor(gv[0], raw[:, 1], vec("dt_bias", 0, 16).unsqueeze(1)
                                                .to_broadcast([P, TT, 16]), ALU.add).then_inc(*gd_ok.one())
                        dve.wait_ge(*gd_ok.at(1))
                        nc.vector.scalar_tensor_tensor(out=gt[:, 1, :], in0=gt[:, 0, :], scalar=-1.0,
                                                       in1=gt[:, 0, :], op0=ALU.mult,
                                                       op1=ALU.max).then_inc(*gd_ok.one())
                        nc.vector.tensor_scalar(gt[:, 4, :], gt[:, 0, :], 0.0, None, ALU.max).then_inc(*gd_ok.one())
                        dve.wait_ge(*gd_ok.at(3))
                        dve.wait_ge(*ga_ok.at(4))
                        nc.vector.tensor_tensor(gt[:, 4, :], gt[:, 4, :], gt[:, 3, :],
                                                ALU.add).then_inc(*gd_ok.one())
                        dve.wait_ge(*gd_ok.at(4))
                        for d in range(2):
                            nc.vector.scalar_tensor_tensor(
                                out=log_a[:, d], in0=gv[4][:, :, 8 * d:8 * d + 8], scalar=-1.0,
                                in1=gt[:, 5, 8 * d:8 * d + 8].unsqueeze(1).to_broadcast([P, TT, 8]),
                                op0=ALU.mult, op1=ALU.mult).then_inc(*gd_ok.one())
                        for n in range(n_items):
                            m = LAT if n < GH else TOK + 2
                            split_lo(dve, n + 3)
                            dve.wait_ge(*evac.at(n + 1))
                            if n > 1:
                                dve.wait_ge(*silu_ok.at(n - 1))
                            x, y, c = cb[:, n % 2, :], cv[:, n % 2, 0:m], VEC["conv_qkv"] + 3 * n
                            nc.vector.tensor_scalar(y, x[:, 0:m], vecs[:, c:c + 1], None,
                                                    ALU.mult).then_inc(*taps.one())
                            dve.wait_ge(*taps.at(2 * n + 1))
                            nc.vector.scalar_tensor_tensor(out=y, in0=x[:, 1:1 + m], scalar=vecs[:, c + 1:c + 2],
                                                           in1=y, op0=ALU.mult, op1=ALU.add).then_inc(*taps.one())
                            dve.wait_ge(*taps.at(2 * n + 2))
                            nc.vector.scalar_tensor_tensor(out=y, in0=x[:, 2:2 + m], scalar=vecs[:, c + 2:c + 3],
                                                           in1=y, op0=ALU.mult,
                                                           op1=ALU.add).then_inc(*conv_ok.one())
                            i = n - 2
                            if 0 <= i < n_unit:
                                x, r = dst[i][:, 0:width(i)], root[:, i % 2, 0:width(i)]
                                dve.wait_ge(*root_ok.at(i + 1))
                                nc.vector.reciprocal(r, r).then_inc(*rs_ok.one())
                                dve.wait_ge(*rs_ok.at(i + 1))
                                nc.vector.scalar_tensor_tensor(out=x, in0=x, scalar=HD ** -0.5 if i < GH else 1.0,
                                                               in1=r, op0=ALU.mult,
                                                               op1=ALU.mult).then_inc(*scaled.one())
            stage_end()

        def stage_gdn(q, kk, v, beta, log_a, o_tok):
            def S1(name):
                return sig("gdn_" + name)

            sums_ok, exp_ok, be_ok, zero_ok = S1("sums"), S1("exps"), S1("beta_eg"), S1("zero")
            pD, pKK, pQK, pKT, pVT, pPT, pUI = (S1("pe_decay"), S1("pe_kk"), S1("pe_qk"), S1("pe_ktok"),
                                                S1("pe_vtok"), S1("pe_attnT"), S1("pe_u0"))
            pY, pU, pT = S1("pe_y"), S1("pe_u"), S1("pe_t")
            pKS, pO1, pDL, pS, pO2 = S1("pe_ks"), S1("pe_qs"), S1("pe_delta"), S1("pe_state"), S1("pe_attn_v")
            aE, aT, aDL = S1("act_decay"), S1("act_t"), S1("act_delta")
            dN, dU0, dP, dPT, dKD, dBV = (S1("dve_n"), S1("dve_u0"), S1("dve_attn"), S1("dve_attnT"),
                                          S1("dve_kdec"), S1("dve_bv"))
            dY, dU, dR, dS, dO1, dO2 = (S1("dve_y"), S1("dve_u"), S1("dve_rhs"), S1("dve_state"),
                                        S1("dve_o1"), S1("dve_o2"))
            lAu, lT1, lTI, lO = S1("pool_au"), S1("pool_t1"), S1("pool_t0"), S1("pool_o")
            G, STEPS, CS = 4, TT, CTX // P
            HALF = QUAD * P // 2
            order = [[TL + i for i in range(CS)] + list(range(TL)),
                     [TL + CS - 1 - i for i in range(CS)] + list(range(TL - 1, -1, -1))]

            def n_of(t, g):
                return G * t + g + 1

            def l_of(t, lev, g):
                return (LEVELS * t + lev) * G + g + 1

            def t_of(t, lev, g):
                return ((LEVELS - 1) * t + lev) * G + g + 1

            with ExitStack() as s:
                buf = {n: sb(s, "gdn_" + n, G, QUAD * P) for n in
                       ("E", "N", "T", "U", "Y", "kd", "bv", "St", "Pt")}
                fac = sb(s, "gdn_fac", 3, 2 * TT * GH)
                be = sb(s, "gdn_be", 2, TT, GH)
                la = log_a[:].rearrange("p d t h -> p d (t h)")

                def B(name, g):
                    return buf[name][:, g, :]

                def Bh(name, g):
                    return buf[name][:, g, :].rearrange("p (h s) -> p h s", h=QUAD)

                def joined(a, g, lev):
                    b = 2 << lev
                    return a.rearrange("p (n two b) -> p n two b", two=2, b=b)[:, :, 1 if g < 2 else 0, :]

                def packed(a, lev):
                    return a.rearrange("p (n b) -> p n b", b=2 << lev)

                def bank(g, b):
                    return ps[:, 4 * b + g, :]

                def bankh(g, b):
                    return bank(g, b).rearrange("p (h s) -> p h s", h=QUAD)

                def col(a, t, g):
                    d, h0, tile = g // 2, QUAD * (g % 2), order[g // 2][t]
                    return a[:, d, tile, h0:h0 + QUAD].unsqueeze(2).to_broadcast([P, QUAD, P])

                def one_col(a, t, g, h):
                    d = g // 2
                    i = QUAD * (g % 2) + h
                    return a[:, d, order[d][t], i:i + 1]

                def facs(i):
                    return fac[:, i, :].rearrange("p (d t h) -> p d t h", d=2, h=GH)

                def rows(m):
                    return m.unsqueeze(1).to_broadcast([P, QUAD, P])

                def chunk(x, t, g, h):
                    c = order[g // 2][t] * P
                    return x[:, QUAD * (g % 2) + h, c:c + P]

                with nc.Block() as block:
                    @block.sync
                    def _(sp):
                        stream_weights(sp, 0)

                    @block.gpsimd
                    def _(pool):
                        def decay_operand(t, g):
                            nc.gpsimd.tensor_tensor(Bh("T", g), rows(tab("gt" if g < 2 else "lt")),
                                                    col(log_a, t, g), ALU.mult).then_inc(*lAu.one())

                        nc.gpsimd.memset(buf["St"][:], 0.0).then_inc(*zero_ok.one())
                        nc.gpsimd.memset(o_tok[:], 0.0).then_inc(*zero_ok.one())
                        pool.wait_ge(*zero_ok.at(2))
                        for g in range(G):
                            decay_operand(0, g)
                        for t in range(STEPS):
                            for g in range(G):
                                pool.wait_ge(*dN.at(n_of(t, g)))
                                nc.gpsimd.tensor_tensor(Bh("T", g), Bh("N", g),
                                                        rows(tab("lo" if g < 2 else "up")),
                                                        ALU.mult).then_inc(*lT1.one())
                            for g in range(G):
                                pool.wait_ge(*lT1.at(n_of(t, g)))
                                pool.wait_ge(*pUI.at(n_of(t, g)))
                                nc.gpsimd.tensor_tensor(Bh("T", g), rows(ident), Bh("T", g),
                                                        ALU.add).then_inc(*lTI.one())
                            if t + 1 < STEPS:
                                for g in range(G):
                                    pool.wait_ge(*pU.at(l_of(t, LEVELS - 1, g)))
                                    decay_operand(t + 1, g)
                            if t >= CS:
                                for g in range(G):
                                    d, tile, h0 = g // 2, order[g // 2][t], QUAD * (g % 2)
                                    dst = o_tok[:, tile, h0 * P:(h0 + QUAD) * P]
                                    pool.wait_ge(*dO2.at(n_of(t - CS, g)))
                                    if t > CS or g:
                                        pool.wait_ge(*lO.at(n_of(t - CS, g) - 1))
                                    nc.gpsimd.tensor_tensor(dst, dst, B("Y", g), ALU.add).then_inc(*lO.one())

                    @block.scalar
                    def _(act):
                        act.wait_ge(*sums_ok.at(1))
                        nc.scalar.activation(fac[:].rearrange("p a b -> p (a b)"), ps[:, 7, 0:6 * TT * GH],
                                             ACT.Exp).then_inc(*exp_ok.one())
                        for t in range(STEPS):
                            for g in range(G):
                                act.wait_ge(*pD.at(n_of(t, g)))
                                if t > 0:
                                    act.wait_ge(*pS.at(n_of(t - 1, g)))
                                if t > CS:
                                    act.wait_ge(*pO2.at(n_of(t - CS - 1, g)))
                                nc.scalar.activation(B("E", g), bank(g, 0), ACT.Exp).then_inc(*aE.one())
                            for lev in range(LEVELS - 1):
                                for g in range(G):
                                    act.wait_ge(*pT.at(t_of(t, lev, g)))
                                    nc.scalar.copy(B("T", g), bank(g, 1)).then_inc(*aT.one())
                            for g in range(G):
                                act.wait_ge(*pDL.at(n_of(t, g)))
                                nc.scalar.copy(B("E", g), bank(g, 1)).then_inc(*aDL.one())

                    @block.vector
                    def _(dve):
                        def beside_level(t, lev, g):
                            if lev == 0:
                                dve.wait_ge(*pVT.at(n_of(t, g)))
                                if t > 0:
                                    dve.wait_ge(*pDL.at(n_of(t - 1, g)))
                                nc.vector.tensor_tensor(Bh("bv", g), bankh(g, 0), col(beta, t, g),
                                                        ALU.mult).then_inc(*dBV.one())
                            elif lev == 1:
                                dve.wait_ge(*pKT.at(n_of(t, g)))
                                if t > 0:
                                    dve.wait_ge(*pS.at(n_of(t - 1, g)))
                                nc.vector.tensor_tensor(Bh("kd", g), bankh(g, 0), col(facs(1), t, g),
                                                        ALU.mult).then_inc(*dKD.one())
                            elif lev == 2 and t >= CS:
                                dve.wait_ge(*pQK.at(n_of(t - CS, g)))
                                nc.vector.tensor_tensor(B("E", g), B("E", g), bank(g, 0),
                                                        ALU.mult).then_inc(*dP.one())
                            elif lev == 3 and t >= CS:
                                dve.wait_ge(*pPT.at(n_of(t - CS, g)))
                                if t > CS:
                                    dve.wait_ge(*pO2.at(n_of(t - CS - 1, g)))
                                nc.vector.tensor_tensor(Bh("Pt", g), bankh(g, 0),
                                                        rows(tab("le" if g < 2 else "ge")),
                                                        ALU.mult).then_inc(*dPT.one())

                        dve.wait_ge(*exp_ok.at(1))
                        nc.vector.scalar_tensor_tensor(out=be[:], in0=beta[:], scalar=-1.0, in1=facs(0),
                                                       op0=ALU.mult, op1=ALU.mult).then_inc(*be_ok.one())
                        dve.wait_ge(*be_ok.at(1))
                        for t in range(STEPS):
                            for g in range(G):
                                dve.wait_ge(*aE.at(n_of(t, g)))
                                dve.wait_ge(*pKK.at(n_of(t, g)))
                                for h in range(QUAD):
                                    mm = nc.vector.scalar_tensor_tensor(
                                        out=Bh("N", g)[:, h, :], in0=bankh(g, 1)[:, h, :],
                                        scalar=one_col(beta, t, g, h), in1=Bh("E", g)[:, h, :],
                                        op0=ALU.mult, op1=ALU.mult)
                                mm.then_inc(*dN.one())
                            for g in range(G):
                                dve.wait_ge(*pUI.at(n_of(t, g)))
                                if t > 0:
                                    dve.wait_ge(*pDL.at(n_of(t - 1, g)))
                                nc.vector.tensor_tensor(Bh("U", g), bankh(g, 1), rows(ident),
                                                        ALU.add).then_inc(*dU0.one())
                            for lev in range(LEVELS):
                                for g in range(G):
                                    m = tab("join_up" if g < 2 else "join_lo", lev * P // 2, P // 2)
                                    dve.wait_ge(*pY.at(l_of(t, lev, g)))
                                    if lev == 0 and t > CS:
                                        dve.wait_ge(*lO.at(n_of(t - CS - 1, g)))
                                    nc.vector.tensor_tensor(
                                        B("Y", g)[:, 0:HALF].rearrange("p (h s) -> p h s", h=QUAD),
                                        bank(g, 0)[:, 0:HALF].rearrange("p (h s) -> p h s", h=QUAD),
                                        m.unsqueeze(1).to_broadcast([P, QUAD, P // 2]), ALU.mult).then_inc(*dY.one())
                                for g in range(G):
                                    dve.wait_ge(*pU.at(l_of(t, lev, g)))
                                    nc.vector.tensor_tensor(joined(B("U", g), g, lev), joined(B("U", g), g, lev),
                                                            packed(bank(g, 1)[:, 0:HALF], lev),
                                                            ALU.subtract).then_inc(*dU.one())
                                    beside_level(t, lev, g)
                            for g in range(G):
                                dve.wait_ge(*pKS.at(n_of(t, g)))
                                dve.wait_ge(*dBV.at(n_of(t, g)))
                                for h in range(QUAD):
                                    mm = nc.vector.scalar_tensor_tensor(
                                        out=Bh("bv", g)[:, h, :], in0=bankh(g, 0)[:, h, :],
                                        scalar=one_col(be, t, g, h), in1=Bh("bv", g)[:, h, :],
                                        op0=ALU.mult, op1=ALU.add)
                                mm.then_inc(*dR.one())
                                if t >= CS:
                                    dve.wait_ge(*pO1.at(n_of(t - CS, g)))
                                    nc.vector.tensor_tensor(Bh("Y", g), bankh(g, 1), col(facs(0), t, g),
                                                            ALU.mult).then_inc(*dO1.one())
                            for g in range(G):
                                dve.wait_ge(*pS.at(n_of(t, g)))
                                if t > 0:
                                    dve.wait_ge(*dS.at(n_of(t - 1, g)))
                                for h in range(QUAD):
                                    mm = nc.vector.scalar_tensor_tensor(
                                        out=Bh("St", g)[:, h, :], in0=Bh("St", g)[:, h, :],
                                        scalar=one_col(facs(2), t, g, h), in1=bankh(g, 0)[:, h, :],
                                        op0=ALU.mult, op1=ALU.add)
                                mm.then_inc(*dS.one())
                            if t >= CS:
                                for g in range(G):
                                    dve.wait_ge(*pO2.at(n_of(t - CS, g)))
                                    dve.wait_ge(*dO1.at(n_of(t - CS, g)))
                                    nc.vector.tensor_tensor(B("Y", g), B("Y", g), bank(g, 0),
                                                            ALU.add).then_inc(*dO2.one())

                    @block.tensor
                    def _(pe):
                        for d in range(2):
                            for i, m in enumerate((tab("le" if d == 0 else "ge"), tab("gt" if d == 0 else "lt"),
                                                   ones)):
                                c = (2 * i + d) * TT * GH
                                mm = nc.tensor.matmul(ps[:, 7, c:c + TT * GH], m, la[:, d, :],
                                                      start=True, stop=True)
                        mm.then_inc(*sums_ok.one())
                        pe.wait_ge(*exp_ok.at(1))
                        pe.wait_ge(*zero_ok.at(1))

                        def four(dst, lhs, rhs, done):
                            for h in range(QUAD):
                                mm = nc.tensor.matmul(dst[:, h * P:(h + 1) * P], lhs(h), rhs(h),
                                                      start=True, stop=True)
                            mm.then_inc(*done.one())

                        def half_four(dst, lhs, rhs, lev, done):
                            for h in range(QUAD):
                                mm = nc.tensor.matmul(packed(dst[:, h * P // 2:(h + 1) * P // 2], lev), lhs(h),
                                                      rhs(h), start=True, stop=True)
                            mm.then_inc(*done.one())

                        def four_t(dst, src, done):
                            for h in range(QUAD):
                                mm = nc.tensor.transpose(dst[:, h * P:(h + 1) * P], src(h), ident)
                            mm.then_inc(*done.one())

                        def part(name, g):
                            return lambda h: buf[name][:, g, h * P:(h + 1) * P]

                        for t in range(STEPS):
                            for g in range(G):
                                pe.wait_ge(*lAu.at(n_of(t, g)))
                                if t > 0:
                                    pe.wait_ge(*dS.at(n_of(t - 1, g)))
                                if t > CS:
                                    pe.wait_ge(*dO2.at(n_of(t - CS - 1, g)))
                                nc.tensor.matmul(bank(g, 0), tab("le" if g < 2 else "ge"), B("T", g),
                                                 start=True, stop=True).then_inc(*pD.one())
                                if t > 0:
                                    pe.wait_ge(*aDL.at(n_of(t - 1, g)))
                                four(bank(g, 1), lambda h: chunk(kk, t, g, h), lambda h: chunk(kk, t, g, h), pKK)
                            for g in range(G):
                                pe.wait_ge(*lT1.at(n_of(t, g)))
                                four_t(bank(g, 1), part("T", g), pUI)
                            for lev in range(LEVELS):
                                for g in range(G):
                                    if lev == 0:
                                        pe.wait_ge(*dU0.at(n_of(t, g)))
                                    else:
                                        pe.wait_ge(*dU.at(l_of(t, lev - 1, g)))
                                        four_t(bank(g, 1), part("U", g), pT)
                                    if lev == 1:
                                        pe.wait_ge(*dBV.at(n_of(t, g)))
                                    elif lev == 2:
                                        pe.wait_ge(*dKD.at(n_of(t, g)))
                                    elif lev == 3 and t >= CS:
                                        pe.wait_ge(*dP.at(n_of(t - CS, g)))
                                    elif lev == 4 and t >= CS:
                                        pe.wait_ge(*dPT.at(n_of(t - CS, g)))
                                    half_four(bank(g, 0), part("N", g),
                                              lambda h: joined(B("U", g)[:, h * P:(h + 1) * P], g, lev), lev, pY)
                                for g in range(G):
                                    pe.wait_ge(*dY.at(l_of(t, lev, g)))
                                    if lev == 0:
                                        pe.wait_ge(*lTI.at(n_of(t, g)))
                                    else:
                                        pe.wait_ge(*aT.at(t_of(t, lev - 1, g)))
                                    half_four(bank(g, 1), part("T", g),
                                              lambda h: packed(B("Y", g)[:, h * P // 2:(h + 1) * P // 2], lev),
                                              lev, pU)
                                    if lev == 0:
                                        four_t(bank(g, 0), lambda h: chunk(v, t, g, h), pVT)
                                    elif lev == 1:
                                        four_t(bank(g, 0), lambda h: chunk(kk, t, g, h), pKT)
                                    elif lev == 2 and t >= CS:
                                        four(bank(g, 0), lambda h: chunk(q, t, g, h), lambda h: chunk(kk, t, g, h),
                                             pQK)
                                    elif lev == 3 and t >= CS:
                                        four_t(bank(g, 0), part("E", g), pPT)
                            for g in range(G):
                                if t > 0:
                                    pe.wait_ge(*dS.at(n_of(t - 1, g)))
                                four(bank(g, 0), lambda h: chunk(kk, t, g, h), part("St", g), pKS)
                                pe.wait_ge(*dU.at(l_of(t, LEVELS - 1, g)))
                                if t >= CS:
                                    four(bank(g, 1), lambda h: chunk(q, t, g, h), part("St", g), pO1)
                            for g in range(G):
                                pe.wait_ge(*dR.at(n_of(t, g)))
                                if t >= CS:
                                    pe.wait_ge(*dO1.at(n_of(t - CS, g)))
                                four(bank(g, 1), part("U", g), part("bv", g), pDL)
                            for g in range(G):
                                pe.wait_ge(*aDL.at(n_of(t, g)))
                                four(bank(g, 0), part("kd", g), part("E", g), pS)
                            if t >= CS:
                                for g in range(G):
                                    pe.wait_ge(*dS.at(n_of(t, g)))
                                    four(bank(g, 0), part("Pt", g), part("E", g), pO2)
            stage_end()

        def stage_gdn_out(h, o_tok, gdn, attn, y, mats, spill_h, spill_attn):
            z_ok, sq_ok, ss_ok, root_ok = sig("z_silu"), sig("o_sq"), sig("o_ss"), sig("o_root")
            rs_ok, on_ok, tr_ok, done = sig("o_rstd"), sig("o_normed"), sig("o_tr"), sig("gdn_done")
            high, low, mats_in = sig("gdn_hi"), sig("gdn_lo"), sig("mats_landed")
            h_hi, h_lo, a_hi, a_lo = sig("h_hi"), sig("h_lo"), sig("attn_hi"), sig("attn_lo")
            ov = o_tok[:].rearrange("p t (h e) -> p (t h) e", e=P)
            with ExitStack() as s:
                sq = sb(s, "o_sq_buf", TL * GH // 2, P)
                ss = sb(s, "o_ss_buf", TL * GH)
                zs = sb(s, "z_buf", 2, LAT)
                go = sb(s, "gdn_f32", 2, LAT)
                with nc.Block() as block:
                    @block.sync
                    def _(sp):
                        for k in range(KD):
                            sp.dma_start(y[:, k, :], spill_h[k]).then_inc(*norm_in[k].dma())
                        for k in range(KD):
                            sp.wait_ge(*h_lo.at(k + 1))
                            sp.dma_start(y[:, k, :], spill_attn[k]).then_inc(*norm_in[k].dma())
                        stream_weights(sp, GH)
                        sp.dma_start(mats[:], t_mats).then_inc(*mats_in.dma())
                        sp.wait_ge(*mats_in.at(16))

                    @block.tensor
                    def _(pe):
                        for n in range(GH + 1):
                            if n < GH:
                                w = unit(pe)
                                if n > 1:
                                    pe.wait_ge(*z_ok.at(n - 1))
                                for a in range(KD if n == 0 else 1):
                                    if n == 0:
                                        pe.wait_ge(*h_lo.at(a + 1))
                                        mm = product(pe, tuple(p[:, a * P:(a + 1) * P] for p in w), h, ps[:, 0, :],
                                                     LAT, k0=a, nk=1, start=a == 0, stop=a == KD - 1)
                                    else:
                                        mm = product(pe, w, h, ps[:, n % 2, :], LAT)
                                mm.then_inc(*unit_used.one())
                            if n > 0:
                                m = n - 1
                                pe.wait_ge(*on_ok.at(1))
                                if m > 1:
                                    pe.wait_ge(*done.at(m - 1))
                                for t in range(TL):
                                    mm = nc.tensor.transpose(ps[:, 2 + m % 2, t * P:(t + 1) * P],
                                                             o_tok[:, t, m * P:(m + 1) * P], ident)
                                mm.then_inc(*tr_ok.one())

                    @block.scalar
                    def _(act):
                        split_hi(act, 1)
                        for k in range(KD):
                            act.wait_ge(*norm_in[k].at(16))
                            nc.scalar.copy(h[0][:, k, :], y[:, k, :]).then_inc(*h_hi.one())
                        act.wait_ge(*ss_ok.at(2))
                        nc.scalar.activation(ss[:], ss[:], ACT.Sqrt, scale=1.0 / HD,
                                             bias=tab("eps", 0, 1)).then_inc(*root_ok.one())
                        for n in range(GH):
                            act.wait_ge(*unit_used.at(n + 1))
                            split_hi(act, n + 2)
                            if n > 1:
                                act.wait_ge(*done.at(n - 1))
                            nc.scalar.activation(zs[:, n % 2, :], ps[:, n % 2, :], ACT.Silu).then_inc(*z_ok.one())
                            act.wait_ge(*done.at(n + 1))
                            nc.scalar.copy(gdn[0][:, n, :], go[:, n % 2, :]).then_inc(*high.one())
                            act.wait_ge(*norm_in[n].at(32))
                            nc.scalar.copy(attn[0][:, n, :], y[:, n, :]).then_inc(*a_hi.one())

                    @block.vector
                    def _(dve):
                        split_lo(dve, 1)
                        for k in range(KD):
                            dve.wait_ge(*h_hi.at(k + 1))
                            nc.vector.tensor_tensor(h[1][:, k, :], y[:, k, :], as_f32(h[0][:, k, :]),
                                                    ALU.subtract).then_inc(*h_lo.one())
                        for c in range(2):
                            half = slice(c * TL * GH // 2, (c + 1) * TL * GH // 2)
                            if c > 0:
                                dve.wait_ge(*ss_ok.at(c))
                            nc.vector.tensor_tensor(sq[:], ov[:, half], ov[:, half], ALU.mult).then_inc(*sq_ok.one())
                            dve.wait_ge(*sq_ok.at(c + 1))
                            nc.vector.reduce_sum(ss[:, half], sq[:], AX_X).then_inc(*ss_ok.one())
                        dve.wait_ge(*root_ok.at(1))
                        nc.vector.reciprocal(ss[:], ss[:]).then_inc(*rs_ok.one())
                        dve.wait_ge(*rs_ok.at(1))
                        nc.vector.tensor_tensor(ov, ov, ss[:].unsqueeze(2).to_broadcast([P, TL * GH, P]),
                                                ALU.mult).then_inc(*on_ok.one())
                        for n in range(GH):
                            split_lo(dve, n + 2)
                            dve.wait_ge(*tr_ok.at(n + 1))
                            dve.wait_ge(*z_ok.at(n + 1))
                            if n > 1:
                                dve.wait_ge(*low.at(n - 1))
                            nc.vector.scalar_tensor_tensor(out=go[:, n % 2, :], in0=ps[:, 2 + n % 2, :],
                                                           scalar=vec("gdn_norm"), in1=zs[:, n % 2, :],
                                                           op0=ALU.mult, op1=ALU.mult).then_inc(*done.one())
                            dve.wait_ge(*high.at(n + 1))
                            nc.vector.tensor_tensor(gdn[1][:, n, :], go[:, n % 2, :], as_f32(gdn[0][:, n, :]),
                                                    ALU.subtract).then_inc(*low.one())
                            dve.wait_ge(*a_hi.at(n + 1))
                            nc.vector.tensor_tensor(attn[1][:, n, :], y[:, n, :], as_f32(attn[0][:, n, :]),
                                                    ALU.subtract).then_inc(*a_lo.one())
            stage_end()

        def stage_merge(h, attn, gdn, y):
            gate_ok, prod_ok, done = sig("merge_gate"), sig("merge_prod"), sig("merged")
            with ExitStack() as s:
                gate = sb(s, "merge_gates", 2, LAT)
                with nc.Block() as block:
                    @block.sync
                    def _(sp):
                        stream_weights(sp, 4 * KD)

                    @block.tensor
                    def _(pe):
                        for n in range(2 * KD):
                            w = unit(pe)
                            if n > 1:
                                pe.wait_ge(*gate_ok.at(n - 1))
                            product(pe, w, h, ps[:, n % 2, :], LAT).then_inc(*unit_used.one())
                            w = unit(pe)
                            if n > 1:
                                pe.wait_ge(*prod_ok.at(n - 1))
                            product(pe, w, (attn, gdn)[n % 2], ps[:, 2 + n % 2, :],
                                    LAT).then_inc(*unit_used.one())

                    @block.scalar
                    def _(act):
                        split_hi(act, 1)
                        for n in range(2 * KD):
                            act.wait_ge(*unit_used.at(2 * n + 1))
                            split_hi(act, 2 * n + 2)
                            if n > 1:
                                act.wait_ge(*prod_ok.at(n - 1))
                            if n % 2:
                                if n // 2 > 0:
                                    act.wait_ge(*done.at(n // 2))
                            nc.scalar.activation(gate[:, n % 2, :], ps[:, n % 2, :],
                                                 ACT.Sigmoid).then_inc(*gate_ok.one())
                            split_hi(act, 2 * n + 3)

                    @block.vector
                    def _(dve):
                        split_lo(dve, 1)
                        for n in range(2 * KD):
                            split_lo(dve, 2 * n + 2)
                            dve.wait_ge(*gate_ok.at(n + 1))
                            split_lo(dve, 2 * n + 3)
                            dve.wait_ge(*unit_used.at(2 * n + 2))
                            dst = y[:, n // 2, :] if n % 2 == 0 else gate[:, 1, :]
                            nc.vector.tensor_tensor(dst, gate[:, n % 2, :], ps[:, 2 + n % 2, :],
                                                    ALU.mult).then_inc(*prod_ok.one())
                            if n % 2:
                                dve.wait_ge(*prod_ok.at(n + 1))
                                nc.vector.tensor_tensor(y[:, n // 2, :], y[:, n // 2, :], gate[:, 1, :],
                                                        ALU.add).then_inc(*done.one())
            stage_end()

        def stage_project(src, x, nk, gain_of=None, load=None, sums=True):
            sq_ok, sum_ok = sig("norm_sq"), sig("norm_sum")
            done, high, low = sig("gemm_evac"), sig("src_hi"), sig("src_lo")
            per = -(-nk // 8)
            given = isinstance(src, tuple)
            with ExitStack() as s:
                sq = sb(s, "project_sq", 2, LAT)
                xs = src if given else (sbr(s, "src_hi_buf", nk, LAT), sbr(s, "src_lo_buf", nk, LAT))
                with nc.Block() as block:
                    @block.sync
                    def _(sp):
                        if load is not None:
                            for k in range(KD):
                                sp.dma_start(x[:, k, :], load[k][:, 0:LAT]).then_inc(*norm_in[k].dma())
                        stream_weights(sp, KD * per)

                    @block.tensor
                    def _(pe):
                        def square_sums(n):
                            pe.wait_ge(*sq_ok.at(n + 1))
                            nc.tensor.matmul(ps[:, 4, :], ones, sq[:, n % 2, :], start=n == 0,
                                             stop=n == KD - 1).then_inc(*sum_ok.one())

                        for n in range(KD):
                            if n > 3:
                                pe.wait_ge(*done.at(n - 3))
                            for u in range(per):
                                w = unit(pe)
                                if given or n:
                                    mm = product(pe, w, xs, ps[:, n % 4, :], LAT, k0=8 * u,
                                                 nk=min(8, nk - 8 * u), start=u == 0, stop=u == per - 1)
                                else:
                                    for k in range(nk):
                                        pe.wait_ge(*low.at(k + 1))
                                        mm = product(pe, tuple(p[:, k * P:(k + 1) * P] for p in w), xs,
                                                     ps[:, 0, :], LAT, k0=k, nk=1, start=k == 0,
                                                     stop=k == nk - 1)
                                mm.then_inc(*unit_used.one())
                            if sums and n > 0:
                                square_sums(n - 1)
                        if sums:
                            square_sums(KD - 1)

                    @block.scalar
                    def _(act):
                        split_hi(act, 1)
                        if not given:
                            for k in range(nk):
                                nc.scalar.copy(xs[0][:, k, :], src[:, k, :]).then_inc(*high.one())
                        def square(n):
                            act.wait_ge(*done.at(n + 1))
                            if n > 1:
                                act.wait_ge(*sum_ok.at(n - 1))
                            nc.scalar.activation(sq[:, n % 2, :], x[:, n, :], ACT.Square).then_inc(*sq_ok.one())

                        for n in range(KD):
                            if sums and n > 0:
                                square(n - 1)
                            for u in range(per):
                                act.wait_ge(*unit_used.at(per * n + u + 1))
                                split_hi(act, per * n + u + 2)
                        if sums:
                            square(KD - 1)

                    @block.vector
                    def _(dve):
                        split_lo(dve, 1)
                        if not given:
                            for k in range(nk):
                                dve.wait_ge(*high.at(k + 1))
                                nc.vector.tensor_tensor(xs[1][:, k, :], src[:, k, :], as_f32(xs[0][:, k, :]),
                                                        ALU.subtract).then_inc(*low.one())
                        for n in range(KD):
                            if load is not None:
                                dve.wait_ge(*norm_in[n].at(16))
                            for u in range(per):
                                split_lo(dve, per * n + u + 2)
                            dve.wait_ge(*unit_used.at(per * (n + 1)))
                            if gain_of is None:
                                nc.vector.tensor_tensor(x[:, n, :], x[:, n, :], ps[:, n % 4, :],
                                                        ALU.add).then_inc(*done.one())
                            else:
                                nc.vector.scalar_tensor_tensor(out=x[:, n, :], in0=ps[:, n % 4, :],
                                                               scalar=gain_of(n), in1=x[:, n, :], op0=ALU.mult,
                                                               op1=ALU.add).then_inc(*done.one())
            stage_end()

        def stage_up(h, mid, norm):
            evac, taps, conv_ok, silu_ok, done = (sig("gemm_evac"), sig("conv_tap"), sig("conv_done"),
                                                  sig("silu_done"), sig("up_done"))
            pad_ok = sig("pad_zero")
            n_items = 2 * KF
            with ExitStack() as s:
                norm_act, norm_pe, norm_dve = norm_steps(s, *norm, summed=True)
                cb = sb(s, "up_in", 2, LAT + 2)
                cv = sb(s, "up_conv", 4, LAT)
                hi_done, lo_done = sig("mid_hi"), sig("mid_lo")
                with nc.Block() as block:
                    @block.sync
                    def _(sp):
                        stream_weights(sp, n_items)

                    @block.gpsimd
                    def _(pool):
                        nc.gpsimd.memset(cb[:], 0.0).then_inc(*pad_ok.one())
                        for j in range(KF):
                            pool.wait_ge(*silu_ok.at(j + 1))
                            pool.wait_ge(*conv_ok.at(2 * j + 2))
                            val = cv[:, (2 * j + 1) % 4, :]
                            nc.gpsimd.tensor_tensor(val, cv[:, (2 * j) % 4, :], val, ALU.mult).then_inc(*done.one())

                    @block.tensor
                    def _(pe):
                        norm_pe(pe)
                        for n in range(n_items):
                            w = unit(pe)
                            if n > 3:
                                pe.wait_ge(*evac.at(n - 3))
                            mm = product(pe, w, h, ps[:, n % 4, :], LAT) if n else \
                                product_of_norm(pe, w, h, ps[:, 0, :])
                            mm.then_inc(*unit_used.one())

                    @block.scalar
                    def _(act):
                        act.wait_ge(*pad_ok.at(1))
                        norm_act(act)
                        split_hi(act, 1)

                        def high(j):
                            act.wait_ge(*done.at(j + 1))
                            nc.scalar.copy(mid[0][:, j, :], cv[:, (2 * j + 1) % 4, :]).then_inc(*hi_done.one())

                        for n in range(n_items):
                            act.wait_ge(*unit_used.at(n + 1))
                            split_hi(act, n + 2)
                            if n > 1:
                                act.wait_ge(*conv_ok.at(n - 1))
                            nc.scalar.copy(cb[:, n % 2, 1:1 + LAT], ps[:, n % 4, :]).then_inc(*evac.one())
                            if n % 2 == 0 and n >= 4:
                                high(n // 2 - 2)
                            if n % 2:
                                act.wait_ge(*conv_ok.at(n))
                                g = cv[:, (n - 1) % 4, :]
                                nc.scalar.activation(g, g, ACT.Silu).then_inc(*silu_ok.one())
                        high(KF - 2)
                        high(KF - 1)

                    @block.vector
                    def _(dve):
                        norm_dve(dve)
                        split_lo(dve, 1)

                        def low(j):
                            dve.wait_ge(*hi_done.at(j + 1))
                            nc.vector.tensor_tensor(mid[1][:, j, :], cv[:, (2 * j + 1) % 4, :], as_f32(mid[0][:, j, :]),
                                                    ALU.subtract).then_inc(*lo_done.one())

                        for n in range(n_items):
                            tile = n // 2 + KF * (n % 2)
                            x, y = cb[:, n % 2, :], cv[:, n % 4, :]
                            c, b = VEC["ffn_w"] + 3 * tile, VEC["ffn_b"] + tile
                            split_lo(dve, n + 2)
                            dve.wait_ge(*evac.at(n + 1))
                            if n > 3:
                                dve.wait_ge(*done.at(n // 2 - 1))
                            if n % 2:
                                if n > 3:
                                    dve.wait_ge(*lo_done.at(n // 2 - 1))
                            nc.vector.tensor_scalar(y, x[:, 0:LAT], vecs[:, c:c + 1], vecs[:, b:b + 1], ALU.mult,
                                                    ALU.add).then_inc(*taps.one())
                            dve.wait_ge(*taps.at(2 * n + 1))
                            nc.vector.scalar_tensor_tensor(out=y, in0=x[:, 1:1 + LAT], scalar=vecs[:, c + 1:c + 2],
                                                           in1=y, op0=ALU.mult, op1=ALU.add).then_inc(*taps.one())
                            dve.wait_ge(*taps.at(2 * n + 2))
                            nc.vector.scalar_tensor_tensor(out=y, in0=x[:, 2:2 + LAT], scalar=vecs[:, c + 2:c + 3],
                                                           in1=y, op0=ALU.mult,
                                                           op1=ALU.add).then_inc(*conv_ok.one())
                            if n % 2 == 0 and n >= 4:
                                low(n // 2 - 2)
                        low(KF - 2)
                        low(KF - 1)
            stage_end()

        def stage_mixer_inputs(u, norm, summed, pin, gq, gk, gr, gg, qz, dk, dv, gv):
            evac, zeroed, dv_ok = sig("gemm_evac"), sig("pad_zero"), sig("dv_evac")
            kinds = [("pin", i) for i in range(2)] + [("gq", 0), ("gk", 0)] + [("gr", i) for i in range(2)] + \
                    [("gg", 0)] + [("dq", i) for i in range(DH2)] + [("dk", i) for i in range(DH2)] + \
                    [("gv", i) for i in range(2)] + [("dv", i) for i in range(4)]
            n_major = [kind for kind, _ in kinds].index("gv")
            with ExitStack() as s:
                norm_act, norm_pe, norm_dve = norm_steps(s, *norm, summed=summed)
                with nc.Block() as block:
                    @block.sync
                    def _(sp):
                        stream_weights(sp, len(kinds))

                    @block.gpsimd
                    def _(pool):
                        nc.gpsimd.memset(qz[:], 0.0).then_inc(*zeroed.one())

                    @block.tensor
                    def _(pe):
                        norm_pe(pe)
                        for n, (kind, i) in enumerate(kinds):
                            w = unit(pe)
                            if 3 < n < n_major:
                                pe.wait_ge(*evac.at(n - 3))
                            if (kind, i) == ("dv", 0):
                                pe.wait_ge(*evac.at(n_major))
                            if kind == "gv":
                                mm = product_tok(pe, w, u, lambda t: ps[:, 4 + t, 0:256], TL, 256, k0=4 * i, nk=4,
                                                 start=i == 0, stop=i == 1)
                            elif kind == "dv":
                                mm = product_tok(pe, w, u, lambda t: ps[:, t, :], TL, 512, k0=2 * i, nk=2,
                                                 start=i == 0, stop=i == 3)
                            elif n == 0:
                                mm = product_of_norm(pe, w, u, ps[:, 0, :])
                            else:
                                mm = product(pe, w, u, ps[:, n % 4, :], LAT)
                            mm.then_inc(*unit_used.one())

                    @block.scalar
                    def _(act):
                        norm_act(act)
                        act.wait_ge(*zeroed.at(1))
                        split_hi(act, 1)
                        for n, (kind, i) in enumerate(kinds):
                            act.wait_ge(*unit_used.at(n + 1))
                            split_hi(act, n + 2)
                            b = ps[:, n % 4, :]
                            if kind == "gr":
                                mm = nc.scalar.activation(gr[:, i, :], b, ACT.Silu)
                            elif kind == "gg":
                                mm = nc.scalar.copy(gg[0:16, :], b[0:16, :])
                            elif kind == "dq":
                                for m in range(2):
                                    mm = nc.scalar.copy(qz[64 * m:64 * m + 64, m, i, :], b[64 * m:64 * m + 64, :])
                            elif kind == "gv":
                                if i == 0:
                                    continue
                                mm = nc.scalar.copy(gv[:], ps[:, 4:8, 0:256])
                            elif kind == "dv":
                                if i < 3:
                                    continue
                                mm = nc.scalar.copy(dv[:, 0:2], ps[:, 0:2, :])
                            else:
                                dst = {"pin": pin, "gq": gq, "gk": gk, "dk": dk}[kind]
                                mm = nc.scalar.copy(dst[:, i, :] if kind in ("pin", "dk") else dst[:], b)
                            mm.then_inc(*evac.one())

                    @block.vector
                    def _(dve):
                        norm_dve(dve)
                        for n in range(len(kinds) + 1):
                            split_lo(dve, n)
                        dve.wait_ge(*unit_used.at(len(kinds)))
                        nc.vector.tensor_copy(dv[:, 2:4], ps[:, 2:4, :]).then_inc(*dv_ok.one())
            stage_end()

        def stage_pool_gla(layer, mats, pin, gq, gk, gr, gg, gv, mix):
            a_ok, d_ok, l_ok, p_ok = sig("gla_act"), sig("gla_dve"), sig("gla_pool"), sig("gla_pe")
            with ExitStack() as s:
                cs_ = sb(s, "pool_csum", 2, 16 + LAT)
                pw = sb(s, "pool_mean", 2, LAT)
                x = sb(s, "gla_x", 3, LAT)
                bc = sb(s, "gla_cum", LAT)
                ex = sb(s, "gla_exp", 3, LAT)
                qd = sb(s, "gla_qdec", LAT)
                ke = x[:, 0, :]
                kp = sb(s, "gla_kinv", 4, LAT)
                vp = sb(s, "gla_vpad", TL, 4, P)
                kt = sb(s, "gla_kend_tok", 2, TL, P)
                at_ = sb(s, "gla_att", TL, 4, P)
                kv = sb(s, "gla_kv", NCH, 256)
                st = sb(s, "gla_state", NCH, 256)
                og = mix[:, 2:4, :]
                rt = mix[:, 4:6, :]
                chunks = lambda a: a.rearrange("p (c i) -> p c i", i=GLA_C)
                with nc.Block() as block:
                    @block.sync
                    def _(sp):
                        stream_weights(sp, 0)

                    @block.gpsimd
                    def _(pool):
                        nc.gpsimd.memset(kp[:], 0.0).then_inc(*l_ok.one())
                        nc.gpsimd.memset(cs_[:], 0.0).then_inc(*l_ok.one())
                        nc.gpsimd.memset(vp[:], 0.0).then_inc(*l_ok.one())
                        nc.gpsimd.memset(st[:, 0, :], 0.0).then_inc(*l_ok.one())
                        pool.wait_ge(*l_ok.at(4))
                        for h in range(4):
                            c = 64 * (h % 2)
                            nc.gpsimd.tensor_copy(vp[:, :, h, c:c + 64],
                                                  gv[:, :, 64 * h:64 * h + 64]).then_inc(*l_ok.one())
                        pool.wait_ge(*d_ok.at(2))
                        for tile in range(2):
                            for half in range(2):
                                w, r = POOL_WINDOWS[2 * tile + half], slice(64 * half, 64 * half + 64)
                                pool.wait_ge(*l_ok.at(8 + 2 * tile + half))
                                nc.gpsimd.tensor_tensor(pw[r, tile, :], cs_[r, tile, 16:16 + LAT],
                                                        cs_[r, tile, 16 - w:16 - w + LAT],
                                                        ALU.subtract).then_inc(*l_ok.one())
                        pool.wait_ge(*l_ok.at(12))
                        nc.gpsimd.tensor_tensor(pw[:].rearrange("p a b -> p (a b)"),
                                                pw[:].rearrange("p a b -> p (a b)"), tab("inv_count", 0, 2 * LAT),
                                                ALU.mult).then_inc(*l_ok.one())
                        pool.wait_ge(*l_ok.at(13))
                        nc.gpsimd.tensor_tensor(pw[:], pw[:], pin[:], ALU.subtract).then_inc(*l_ok.one())

                    @block.scalar
                    def _(act):
                        act.wait_ge(*d_ok.at(4))
                        nc.scalar.activation(x[:, 1, :], x[:, 1, :], ACT.Exp, scale=-1.0).then_inc(*a_ok.one())
                        act.wait_ge(*a_ok.at(1))
                        nc.scalar.activation(x[:, 1, :], x[:, 1, :], ACT.Ln, bias=1.0).then_inc(*a_ok.one())
                        act.wait_ge(*d_ok.at(8))
                        nc.scalar.activation(ex[:, 0, :], bc[:], ACT.Exp).then_inc(*a_ok.one())
                        nc.scalar.activation(ex[:, 1, :], bc[:], ACT.Exp, scale=-1.0).then_inc(*a_ok.one())
                        act.wait_ge(*d_ok.at(9))
                        nc.scalar.activation(ex[:, 2, :], x[:, 2, :], ACT.Exp).then_inc(*a_ok.one())
                        act.wait_ge(*p_ok.at(12))
                        for tile in range(2):
                            nc.scalar.activation(mix[:, tile, :], ps[:, 6 + tile, :], ACT.Copy,
                                                 scale=vec("pool_scale", 2 * layer + tile)).then_inc(*a_ok.one())
                        for p in range(2):
                            act.wait_ge(*p_ok.at(13 + p))
                            nc.scalar.copy(og[:, p, :], ps[:, 4 + p, :]).then_inc(*a_ok.one())
                        act.wait_ge(*a_ok.at(9))
                        for p in range(2):
                            nc.scalar.activation(rt[:, p, :], og[:, p, :], ACT.Square).then_inc(*a_ok.one())
                        for p in range(2):
                            act.wait_ge(*p_ok.at(15 + p))
                            nc.scalar.activation(rt[:, p, :], ps[:, 6 + p, :], ACT.Sqrt, scale=1.0 / 64,
                                                 bias=tab("eps", 0, 1)).then_inc(*a_ok.one())

                    @block.vector
                    def _(dve):
                        dve.wait_ge(*l_ok.at(4))
                        for tile in range(2):
                            nc.vector.tensor_tensor_scan(cs_[:, tile, 16:16 + LAT],
                                                         ones[:, 0:1].to_broadcast([P, LAT]), pin[:, tile, :], 0.0,
                                                         ALU.mult, ALU.add).then_inc(*d_ok.one())
                        dve.wait_ge(*p_ok.at(1))
                        nc.vector.tensor_scalar(x[:, 0, :], ps[:, 0, :], vec("gla_b", layer), None,
                                                ALU.add).then_inc(*d_ok.one())
                        dve.wait_ge(*d_ok.at(3))
                        nc.vector.scalar_tensor_tensor(out=x[:, 1, :], in0=x[:, 0, :], scalar=-1.0,
                                                       in1=x[:, 0, :], op0=ALU.mult,
                                                       op1=ALU.max).then_inc(*d_ok.one())
                        nc.vector.tensor_scalar(x[:, 0, :], x[:, 0, :], 0.0, None, ALU.min).then_inc(*d_ok.one())
                        dve.wait_ge(*d_ok.at(5))
                        dve.wait_ge(*a_ok.at(2))
                        nc.vector.tensor_tensor(x[:, 0, :], x[:, 0, :], x[:, 1, :],
                                                ALU.subtract).then_inc(*d_ok.one())
                        dve.wait_ge(*d_ok.at(6))
                        nc.vector.tensor_scalar(x[:, 0, :], x[:, 0, :], 1.0 / 16, None,
                                                ALU.mult).then_inc(*d_ok.one())
                        dve.wait_ge(*d_ok.at(7))
                        nc.vector.tensor_tensor_scan(bc[:], tab("keep", 0, LAT), x[:, 0, :], 0.0, ALU.mult,
                                                     ALU.add).then_inc(*d_ok.one())
                        dve.wait_ge(*d_ok.at(8))
                        nc.vector.tensor_tensor(chunks(x[:, 2, :]),
                                                chunks(bc[:])[:, :, GLA_C - 1:GLA_C].to_broadcast([P, NCH, GLA_C]),
                                                chunks(bc[:]), ALU.subtract).then_inc(*d_ok.one())
                        dve.wait_ge(*a_ok.at(5))
                        nc.vector.scalar_tensor_tensor(out=qd[:], in0=gq[:], scalar=32 ** -0.5, in1=ex[:, 0, :],
                                                       op0=ALU.mult, op1=ALU.mult).then_inc(*d_ok.one())
                        nc.vector.tensor_tensor(ke, gk[:], ex[:, 2, :], ALU.mult).then_inc(*d_ok.one())
                        for h in range(4):
                            r = slice(32 * h, 32 * h + 32)
                            nc.vector.tensor_tensor(kp[r, h, :], gk[r, :], ex[r, 1, :], ALU.mult).then_inc(*d_ok.one())
                        dve.wait_ge(*p_ok.at(2))
                        for half in range(2):
                            nc.vector.tensor_scalar(kt[:, half, :, :].rearrange("p t c -> p (t c)"), ps[:, 3, :],
                                                    tab("half", half, 1), None, ALU.mult).then_inc(*d_ok.one())
                        for t in range(TL):
                            dve.wait_ge(*p_ok.at(3 + t))
                            nc.vector.tensor_tensor(at_[:, t], ps[:, 4 + t, :].rearrange("p (h c) -> p h c", h=4),
                                                    tab("causal64").unsqueeze(1).to_broadcast([P, 4, P]),
                                                    ALU.mult).then_inc(*d_ok.one())
                        for t in range(TL):
                            dve.wait_ge(*p_ok.at(7 + t))
                            nc.vector.tensor_tensor(kv[:, 2 * t:2 * t + 2, :],
                                                    ps[:, t, :].rearrange("p (c n) -> p c n", c=2),
                                                    tab("blockdiag", 0, 256).unsqueeze(1).to_broadcast([P, 2, 256]),
                                                    ALU.mult).then_inc(*d_ok.one())
                        for c in range(NCH - 1):
                            dve.wait_ge(*d_ok.at(25 + c))
                            e = ex[:, 0, c * GLA_C + GLA_C - 1:c * GLA_C + GLA_C]
                            nc.vector.scalar_tensor_tensor(out=st[:, c + 1, :], in0=st[:, c, :], scalar=e,
                                                           in1=kv[:, c, :], op0=ALU.mult,
                                                           op1=ALU.add).then_inc(*d_ok.one())
                        for p in range(2):
                            dve.wait_ge(*a_ok.at(12 + p))
                            nc.vector.reciprocal(rt[:, p, :], rt[:, p, :]).then_inc(*d_ok.one())
                            dve.wait_ge(*d_ok.at(33 + 3 * p))
                            nc.vector.scalar_tensor_tensor(out=og[:, p, :], in0=og[:, p, :],
                                                           scalar=vec("gla_norm", 2 * layer + p), in1=rt[:, p, :],
                                                           op0=ALU.mult, op1=ALU.mult).then_inc(*d_ok.one())
                            dve.wait_ge(*d_ok.at(34 + 3 * p))
                            nc.vector.tensor_tensor(mix[:, 6 + p, :], og[:, p, :], gr[:, p, :],
                                                    ALU.mult).then_inc(*d_ok.one())

                    @block.tensor
                    def _(pe):
                        nc.tensor.matmul(ps[:, 0, :], mats[0:16, layer * P:(layer + 1) * P], gg[0:16, :],
                                         start=True, stop=True).then_inc(*p_ok.one())
                        pe.wait_ge(*d_ok.at(15))
                        for t in range(TL):
                            mm = nc.tensor.transpose(ps[:, 3, t * P:(t + 1) * P], ke[:, t * P:(t + 1) * P], ident)
                        mm.then_inc(*p_ok.one())
                        for t in range(TL):
                            for h in range(4):
                                mm = nc.tensor.matmul(ps[:, 4 + t, h * P:(h + 1) * P], kp[:, h, t * P:(t + 1) * P],
                                                      qd[:, t * P:(t + 1) * P], start=True, stop=True)
                            mm.then_inc(*p_ok.one())
                        pe.wait_ge(*d_ok.at(17))
                        for t in range(TL):
                            for half in range(2):
                                mm = nc.tensor.matmul(ps[:, t, 256 * half:256 * half + 256], kt[:, half, t, :],
                                                      gv[:, t, :], start=True, stop=True)
                            mm.then_inc(*p_ok.one())
                        pe.wait_ge(*d_ok.at(21))
                        pe.wait_ge(*l_ok.at(14))
                        for tile in range(2):
                            c = (2 + 2 * layer + tile) * P
                            nc.tensor.matmul(ps[:, 6 + tile, :], mats[:, c:c + P], pw[:, tile, :],
                                             start=True, stop=True).then_inc(*p_ok.one())
                        pe.wait_ge(*d_ok.at(32))
                        for p in range(2):
                            for t in range(TL):
                                o = ps[:, 4 + p, t * P:(t + 1) * P]
                                for i in range(2):
                                    nc.tensor.matmul(o, vp[:, t, 2 * p + i, :], at_[:, t, 2 * p + i, :],
                                                     start=i == 0, stop=False)
                                for half in range(2):
                                    c = 2 * t + half
                                    mm = nc.tensor.matmul(o[:, 64 * half:64 * half + 64],
                                                          st[:, c, p * P:(p + 1) * P],
                                                          qd[:, c * GLA_C:(c + 1) * GLA_C], start=False,
                                                          stop=half == 1)
                            mm.then_inc(*p_ok.one())
                        for p in range(2):
                            pe.wait_ge(*a_ok.at(10 + p))
                            nc.tensor.matmul(ps[:, 6 + p, :], tab("ones64"), rt[:, p, :], start=True,
                                             stop=True).then_inc(*p_ok.one())
            stage_end()

        def stage_diff(layer, qz, dk, dv, mix):
            lam0 = 0.8 - 0.6 * float(np.exp(-0.3 * layer))
            scale = 64 ** -0.5
            s_ok, max_ok, nmax_ok, exp_ok, rinv_ok = (sig("score_done"), sig("max_done"), sig("nmax_done"),
                                                      sig("exp_done"), sig("rinv_done"))
            w_ok, t1_ok, p_ok, t_ok, tev = (sig("weight_done"), sig("map1_done"), sig("prob_done"),
                                            sig("probT_done"), sig("probT_evac"))
            pv_ok, o_ok, lam_ok, lame_ok, lams_ok = (sig("pv_done"), sig("pv_evac"), sig("lam_dve"),
                                                     sig("lam_exp"), sig("lam_sum"))
            sq_ok, ss_ok, root_ok, rs_ok, done = (sig("qk_sq"), sig("qk_ss"), sig("qk_root"), sig("qk_rstd"),
                                                  sig("qk_normed"))
            n_items = DH2 * TL
            with ExitStack() as s:
                pr = sb(s, "diff_probs", 2, 2, LAT)
                pt = sb(s, "diff_probsT", 2, TL, LAT)
                mx = sb(s, "diff_max", n_items, 2)
                nmx = sb(s, "diff_nmax", n_items, 2)
                rsum = sb(s, "diff_sum", n_items, 2)
                rinv = sb(s, "diff_inv", n_items, 2)
                lam = sb(s, "diff_lam", 8)
                gain = sb(s, "diff_gain", DH2)
                o = sb(s, "diff_o", DH2, LAT)
                rt = sb(s, "diff_root", DH2, LAT)
                with nc.Block() as block:
                    @block.sync
                    def _(sp):
                        stream_weights(sp, 0)

                    @block.tensor
                    def _(pe):
                        pe.wait_ge(*lam_ok.at(1))
                        nc.tensor.matmul(ps[:, 7, 0:2], ones, lam[:, 0:2], start=True,
                                         stop=True).then_inc(*lams_ok.one())

                        def scores(i):
                            h, t = divmod(i, TL)
                            if i > 1:
                                pe.wait_ge(*exp_ok.at(2 * (i - 1)))
                            for m in range(2):
                                b = ps[:, 2 * (i % 2) + m, :]
                                nc.tensor.matmul(b[:, 0:(t + 1) * P], qz[:, m, h, t * P:(t + 1) * P],
                                                 dk[:, h, 0:(t + 1) * P], start=True, stop=False)
                                mm = nc.tensor.matmul(b[:, t * P:(t + 1) * P], tab("mask_q"), tab("mask_k"),
                                                      start=False, stop=True)
                            mm.then_inc(*s_ok.one())

                        def head_sums(h):
                            pe.wait_ge(*sq_ok.at(h + 1))
                            if h == 0:
                                pe.wait_ge(*lame_ok.at(1))
                            else:
                                pe.wait_ge(*root_ok.at(h))
                            nc.tensor.matmul(ps[:, 7, :], ones, rt[:, h, :], start=True,
                                             stop=True).then_inc(*ss_ok.one())

                        scores(0)
                        scores(1)
                        for i in range(n_items):
                            h, t = divmod(i, TL)
                            if i + 2 < n_items:
                                scores(i + 2)
                            pe.wait_ge(*p_ok.at(i + 1))
                            if i > 1:
                                pe.wait_ge(*tev.at(i - 1))
                            for k in range(t + 1):
                                mm = nc.tensor.transpose(ps[:, 4 + i % 2, k * P:(k + 1) * P],
                                                         pr[:, i % 2, 0, k * P:(k + 1) * P], ident)
                            mm.then_inc(*t_ok.one())
                            if t == TL - 1:
                                pe.wait_ge(*tev.at(i + 1))
                                if h > 0:
                                    pe.wait_ge(*o_ok.at(h))
                                for k in range(TL):
                                    mm = nc.tensor.matmul(ps[:, 6, k * P:LAT],
                                                          dv[:, k, h * P:(h + 1) * P], pt[:, h % 2, k, k * P:LAT],
                                                          start=k == 0, stop=k == TL - 1)
                                mm.then_inc(*pv_ok.one())
                            if i % TL == 1 and h > 0:
                                head_sums(h - 1)
                        head_sums(DH2 - 1)

                    @block.scalar
                    def _(act):
                        def head_root(h):
                            act.wait_ge(*ss_ok.at(h + 1))
                            nc.scalar.activation(rt[:, h, :], ps[:, 7, :], ACT.Sqrt, scale=1.0 / P,
                                                 bias=tab("eps", 0, 1)).then_inc(*root_ok.one())

                        act.wait_ge(*lams_ok.at(1))
                        nc.scalar.activation(lam[:, 2:4], ps[:, 7, 0:2], ACT.Exp).then_inc(*lame_ok.one())

                        def exponentials(i):
                            t = i % TL
                            act.wait_ge(*nmax_ok.at(i + 1))
                            if i > 1:
                                act.wait_ge(*t_ok.at(i - 1))
                            for m in range(2):
                                nc.scalar.activation(pr[:, i % 2, m, 0:(t + 1) * P],
                                                     ps[:, 2 * (i % 2) + m, 0:(t + 1) * P], ACT.Exp, scale=scale,
                                                     bias=nmx[:, i, m:m + 1],
                                                     accum_out=rsum[:, i, m:m + 1]).then_inc(*exp_ok.one())

                        exponentials(0)
                        for i in range(n_items):
                            h, t = divmod(i, TL)
                            if i + 1 < n_items:
                                exponentials(i + 1)
                            act.wait_ge(*t_ok.at(i + 1))
                            if h > 1:
                                act.wait_ge(*pv_ok.at(h - 1))
                            nc.scalar.copy(pt[:, h % 2, 0:t + 1, t * P:(t + 1) * P],
                                           ps[:, 4 + i % 2, 0:(t + 1) * P].rearrange("p (k c) -> p k c", c=P)
                                           ).then_inc(*tev.one())
                            if t == TL - 1:
                                act.wait_ge(*pv_ok.at(h + 1))
                                nc.scalar.copy(o[:, h, :], ps[:, 6, :]).then_inc(*o_ok.one())
                                act.wait_ge(*o_ok.at(h + 1))
                                nc.scalar.activation(rt[:, h, :], o[:, h, :], ACT.Square).then_inc(*sq_ok.one())
                            if t == 2 and h > 0:
                                head_root(h - 1)
                        head_root(DH2 - 1)

                    @block.vector
                    def _(dve):
                        lv = vec("lam", 4 * layer, 4).rearrange("p (m w) -> p w m", w=2)
                        nc.vector.tensor_tensor(lam[:, 0:2], lv[:, 0], lv[:, 1], ALU.mult).then_inc(*lam_ok.one())
                        dve.wait_ge(*lame_ok.at(1))
                        nc.vector.scalar_tensor_tensor(out=lam[:, 4:5], in0=lam[:, 3:4], scalar=lam0,
                                                       in1=lam[:, 2:3], op0=ALU.subtract,
                                                       op1=ALU.subtract).then_inc(*lam_ok.one())
                        nc.vector.tensor_scalar(gain[:], vec("diff_norm", DH2 * layer, DH2), 1.0 - lam0, None,
                                                ALU.mult).then_inc(*lam_ok.one())
                        dve.wait_ge(*lam_ok.at(3))

                        def maximum(i):
                            n = (i % TL + 1) * P
                            b = 2 * (i % 2)
                            dve.wait_ge(*s_ok.at(i + 1))
                            nc.vector.reduce_max(mx[:, i, :], ps[:, b:b + 2, 0:n], AX_X).then_inc(*max_ok.one())
                            dve.wait_ge(*max_ok.at(i + 1))
                            nc.vector.tensor_scalar(nmx[:, i, :], mx[:, i, :], -scale, None,
                                                    ALU.mult).then_inc(*nmax_ok.one())

                        def head_scaled(h):
                            dve.wait_ge(*root_ok.at(h + 1))
                            nc.vector.reciprocal(rt[:, h, :], rt[:, h, :]).then_inc(*rs_ok.one())
                            dve.wait_ge(*rs_ok.at(h + 1))
                            nc.vector.scalar_tensor_tensor(out=mix[:, 2 + h, :], in0=o[:, h, :],
                                                           scalar=gain[:, h:h + 1], in1=rt[:, h, :],
                                                           op0=ALU.mult, op1=ALU.mult).then_inc(*done.one())

                        maximum(0)
                        maximum(1)
                        for i in range(n_items):
                            n = (i % TL + 1) * P
                            dve.wait_ge(*exp_ok.at(2 * i + 2))
                            nc.vector.reciprocal(rinv[:, i, :], rsum[:, i, :]).then_inc(*rinv_ok.one())
                            dve.wait_ge(*rinv_ok.at(i + 1))
                            nc.vector.tensor_tensor(mx[:, i, 1:2], rinv[:, i, 1:2], lam[:, 4:5],
                                                    ALU.mult).then_inc(*w_ok.one())
                            dve.wait_ge(*w_ok.at(i + 1))
                            nc.vector.tensor_scalar(pr[:, i % 2, 1, 0:n], pr[:, i % 2, 1, 0:n], mx[:, i, 1:2], None,
                                                    ALU.mult).then_inc(*t1_ok.one())
                            dve.wait_ge(*t1_ok.at(i + 1))
                            nc.vector.scalar_tensor_tensor(out=pr[:, i % 2, 0, 0:n], in0=pr[:, i % 2, 0, 0:n],
                                                           scalar=rinv[:, i, 0:1], in1=pr[:, i % 2, 1, 0:n],
                                                           op0=ALU.mult, op1=ALU.add).then_inc(*p_ok.one())
                            if i + 2 < n_items:
                                maximum(i + 2)
                            if i % TL == 3 and i > TL:
                                head_scaled(i // TL - 1)
                        head_scaled(DH2 - 1)
            stage_end()

        def stage_mlp1(z, mid, n_tiles, norm=None):
            evac, high, squared, low = sig("gemm_evac"), sig("mid_hi"), sig("mid_sq"), sig("mid_lo")
            with ExitStack() as s:
                r = sb(s, "relu", 2, LAT)
                r2 = sb(s, "relu_sq", 2, LAT)
                if norm is not None:
                    norm_act, norm_pe, norm_dve = norm_steps(s, *norm, summed=True)
                with nc.Block() as block:
                    @block.sync
                    def _(sp):
                        stream_weights(sp, n_tiles)

                    @block.tensor
                    def _(pe):
                        for n in range(n_tiles):
                            w = unit(pe)
                            if n > 3:
                                pe.wait_ge(*evac.at(n - 3))
                            mm = product(pe, w, z, ps[:, n % 4, :], LAT) if n or norm is None else \
                                product_of_norm(pe, w, z, ps[:, 0, :])
                            mm.then_inc(*unit_used.one())

                    @block.scalar
                    def _(act):
                        if norm is not None:
                            norm_act(act)
                        split_hi(act, 1)
                        for n in range(n_tiles):
                            act.wait_ge(*unit_used.at(n + 1))
                            split_hi(act, n + 2)
                            if n > 1:
                                act.wait_ge(*squared.at(n - 1))
                            nc.scalar.activation(r[:, n % 2, :], ps[:, n % 4, :], ACT.Relu).then_inc(*evac.one())
                            act.wait_ge(*evac.at(n + 1))
                            nc.scalar.activation(mid[0][:, n, :], r[:, n % 2, :],
                                                 ACT.Square).then_inc(*high.one())

                    @block.vector
                    def _(dve):
                        if norm is not None:
                            norm_dve(dve)
                        split_lo(dve, 1)
                        for n in range(n_tiles):
                            split_lo(dve, n + 2)
                            dve.wait_ge(*evac.at(n + 1))
                            nc.vector.tensor_tensor(r2[:, n % 2, :], r[:, n % 2, :], r[:, n % 2, :],
                                                    ALU.mult).then_inc(*squared.one())
                            dve.wait_ge(*squared.at(n + 1))
                            dve.wait_ge(*high.at(n + 1))
                            nc.vector.tensor_tensor(mid[1][:, n, :], r2[:, n % 2, :], as_f32(mid[0][:, n, :]),
                                                    ALU.subtract).then_inc(*low.one())
            stage_end()

        def lat_mod(j):
            return lambda k, part: mod[:, j * KD + k, part:part + 1]

        def spill(name):
            return nc.dram_tensor(name, (KD, P, LAT), F32, kind="Internal").ap()

        def split_pair(ctx, name, *shape):
            return sbr(ctx, name + "_hi", *shape), sbr(ctx, name + "_lo", *shape)

        spill_h, spill_attn = spill("spill_h"), spill("spill_attn")
        with ExitStack() as s:
            o_tok = sb(s, "o_tok", TL, GH * P)
            with ExitStack() as s2:
                gk_ = sb(s2, "gdn_k", GH, TOK)
                gv_ = sb(s2, "gdn_v", GH, TOK)
                gq_ = sb(s2, "gdn_q", GH, LAT)
                beta = sb(s2, "gdn_beta", 2, TT, GH)
                log_a = sb(s2, "gdn_log_a", 2, TT, GH)
                with ExitStack() as s3:
                    h = split_pair(s3, "h", KD, TOK)
                    cs = sb(s3, "silu_c_buf", 16)
                    stage_modulation(gk_, gv_, gq_)
                    vtok = gv_[:, 0:2, :].rearrange("p a n -> p (a n)").rearrange("p (t c) -> p t c", t=TT)
                    stage_attn_inputs(h, (gk_, h, TOK, lat_mod(1), lat_mod(0)), gq_, gk_, vtok, o_tok)
                    probs_t = o_tok[:].rearrange("p t n -> p (t n)")[:, 0:TT * LAT].rearrange("p (t n) -> p t n", t=TT)
                    stage_attention(gq_, gk_, vtok, probs_t, spill_attn)
                    stage_gdn_inputs(h, gq_, gk_, gv_, beta, log_a, o_tok, spill_h)
                stage_gdn(gq_, gk_, gv_, beta, log_a, o_tok)
            mats = sb(s, "mats", 6 * P)
            with ExitStack() as s2:
                y = sb(s2, "y", KD, LAT)
                with ExitStack() as s3:
                    h = split_pair(s3, "h_lat", KD, LAT)
                    attn = split_pair(s3, "attn_back", KD, LAT)
                    gdn = split_pair(s3, "gdn_o", GH, LAT)
                    stage_gdn_out(h, o_tok, gdn, attn, y, mats, spill_h, spill_attn)
                    stage_merge(h, attn, gdn, y)
                x = o_tok[:].rearrange("p t n -> p (t n)").rearrange("p (k n) -> p k n", k=KD)
                stage_project(y, x, KD, gain_of=lambda n: mod[:, 2 * KD + n, 0:1], load=t_x)
            with ExitStack() as s2:
                mid = split_pair(s2, "mid", KF, LAT)
                with ExitStack() as s3:
                    h = split_pair(s3, "h_ffn", KD, LAT)
                    stage_up(h, mid, (x, h, LAT, lat_mod(4), lat_mod(3)))
                stage_project(mid, x, KF, gain_of=lambda n: mod[:, 5 * KD + n, 0:1])
            stage_norm(x, x, LAT, lambda k, part: vec("final", k), summed=True)

            for layer in range(DEPTH2):
                with ExitStack() as s2:
                    mix = sb(s2, "mix", KD, LAT)
                    pin = sb(s2, "pool_in", 2, LAT)
                    gq, gk = sb(s2, "gla_q", LAT), sb(s2, "gla_k", LAT)
                    gr, gg = sb(s2, "gla_r", 2, LAT), sb(s2, "gla_g", LAT)
                    gv = sb(s2, "gla_v", TL, 256)
                    qz, dk = sb(s2, "diff_q", 2, DH2, LAT), sb(s2, "diff_k", DH2, LAT)
                    dv = sb(s2, "diff_v", TL, DH2 * P)
                    with ExitStack() as s3:
                        u = split_pair(s3, "u", KD, LAT)
                        norm1 = (x, u, LAT, lambda k, part: vec("norm1", KD * layer + k))
                        stage_mixer_inputs(u, norm1, layer > 0, pin, gq, gk, gr, gg, qz, dk, dv, gv)
                    stage_pool_gla(layer, mats, pin, gq, gk, gr, gg, gv, mix)
                    stage_diff(layer, qz, dk, dv, mix)
                    stage_project(mix, x, KD)
                with ExitStack() as s2:
                    z = split_pair(s2, "z_mlp", KD, LAT)
                    mid = split_pair(s2, "mid2", KF2 // 2, LAT)
                    norm2 = (x, z, LAT, lambda k, part: vec("norm2", KD * layer + k))
                    for half in range(2):
                        stage_mlp1(z, mid, KF2 // 2, norm=None if half else norm2)
                        stage_project(mid, x, KF2 // 2, sums=half == 1)
            stage_norm(x, x, LAT, lambda k, part: vec("final2", k), summed=True, store=out)
        assert at["used"] == len(units)


def _units(w, cols=P, kt=8):
    k, n = w.shape
    out = []
    for j in range(n // cols):
        for a in range(0, k // P, kt):
            b = min(kt, k // P - a)
            t = w[a * P:(a + b) * P, j * cols:(j + 1) * cols].reshape(b, P, cols).transpose(1, 0, 2)
            out.append(t.reshape(P, b * cols))
    return out


def _columns(a):
    return np.asarray(a).reshape(-1, P).T


def kernel(**inputs):
    import concourse.bacc as bacc
    from concourse.bass_utils import run_bass_kernel_spmd

    i = {k: np.asarray(v) for k, v in inputs.items()}
    f32 = np.float32
    xt = np.concatenate([i["x"][0].T, i["ctx"][0].T], 1).reshape(KD, P, TOK)

    vecs = np.zeros((P, NVEC), f32)

    def put(name, a, at=0):
        c = VEC[name] + at
        vecs[:a.shape[0], c:c + a.shape[1]] = a

    put("c", np.stack([_columns(i["c"][0]), _columns(i["c_ctx"])], 2).reshape(P, 16))
    put("b_mod", _columns(i["b_mod"][0]))
    put("q_norm", _columns(i["q_norm_w"][0]))
    put("k_norm", _columns(i["k_norm_w"][0]))
    put("conv_qkv", i["conv_qkv_w"][0].reshape(3, 24, P).transpose(2, 1, 0).reshape(P, 72))
    put("gdn_norm", _columns(i["gdn_norm_w"][0]))
    put("ffn_w", i["ffn_conv_w"][0].reshape(3, 44, P).transpose(2, 1, 0).reshape(P, 132))
    put("ffn_b", _columns(i["ffn_conv_b"][0]))
    put("final", _columns(i["final_norm_w"]))
    put("a_log", np.broadcast_to(i["a_log"].reshape(1, 16), (P, 16)))
    put("dt_bias", np.broadcast_to(i["dt_bias"].reshape(1, 16), (P, 16)))
    put("final2", _columns(i["final_norm_g_2"]))
    mats = np.zeros((P, 6 * P), f32)
    for l in range(DEPTH2):
        put("norm1", _columns(i["norm1_g_2"][l]), KD * l)
        put("norm2", _columns(i["norm2_g_2"][l]), KD * l)
        put("diff_norm", _columns(i["diff_norm_g_2"][l]), DH2 * l)
        put("gla_norm", _columns(i["gla_norm_g_2"][l]), 2 * l)
        put("gla_b", _columns(i["gla_b_gate_2"][l]), l)
        put("pool_scale", _columns(i["pool_scale_2"][l]), 2 * l)
        put("lam", np.stack([i[f"diff_{n}_2"][l] for n in ("lq1", "lk1", "lq2", "lk2")], 1), 4 * l)
        mats[0:16, l * P:(l + 1) * P] = i["gla_w_gate2_2"][l]
        for g in range(4):
            r, c = 64 * (g % 2), (2 + 2 * l + g // 2) * P + 64 * (g % 2)
            mats[r:r + 64, c:c + 64] = i["pool_w_2"][l, g]
    tabs, rope = shape_tables()

    w = i["w_in"][0]
    o = np.cumsum([0, 256, 256, 3072, 16, 16, 1024, 1024, 2048])
    ak, av, qkv, db, da, aq, z, gates = [w[:, o[n]:o[n + 1]] for n in range(8)]
    ga, gd = _units(gates[:, :D]), _units(gates[:, D:])
    pa, pd = _units(i["w_pa"][0]), _units(i["w_pd"][0])
    up = _units(i["w_up"][0])
    mod = _units(i["w_mod"][0], 2 * P, 4)
    weights = {
        "mod_first": mod[:MOD_FIRST],
        "mod_rest": mod[MOD_FIRST:],
        "attn_in": _units(av, KV_HEADS * P, 4) + _units(ak) + _units(aq),
        "gates": _units(np.concatenate([db, da], 1), 32),
        "gdn_in": _units(qkv),
        "z": _units(z),
        "merge": [u for j in range(KD) for u in (ga[j], pa[j], gd[j], pd[j])],
        "out": _units(i["w_out"][0]),
        "up": [up[j + KF * s] for j in range(KF) for s in range(2)],
        "down": _units(i["w_down"][0]),
    }
    for l in range(DEPTH2):
        w = i["w_in_2"][l]
        o = np.cumsum([0, 256, 512, 512, 512, 128, 128, 256, 256, 16])
        p_in, dq, dk, dv, gq, gk, gv, gr, gg = [w[:, o[n]:o[n + 1]] for n in range(9)]
        gg = np.pad(gg, ((0, 0), (0, P - gg.shape[1])))
        weights[f"in2_{l}"] = [u for m in (p_in, gq, gk, gr, gg, dq, dk) for u in _units(m)] + \
            _units(gv, 256, 4) + _units(dv, 512, 2)
        weights[f"out2_{l}"] = _units(i["w_out_2"][l])
        up, down = _units(i["w_mlp1_2"][l]), _units(i["w_mlp2_2"][l])
        for s, half in enumerate("ab"):
            weights[f"mlp1{half}_{l}"] = up[s * KF2 // 2:(s + 1) * KF2 // 2]
            weights[f"mlp2{half}_{l}"] = [u for j in range(KD) for u in down[4 * j + 2 * s:4 * j + 2 * s + 2]]

    nc = bacc.Bacc("TRN2", target_bir_lowering=False, num_devices=1)
    arrays = {}

    def dram(name, a):
        a = arrays[f"in_{name}"] = np.ascontiguousarray(a)
        return nc.dram_tensor(f"in_{name}", a.shape, F32, kind="ExternalInput").ap()

    t_w = {}
    for name, us in weights.items():
        widths = sorted({u.shape[1] for u in us})
        if len(widths) == 1:
            t = dram(f"w_{name}", np.stack(us))
            t_w[name] = [t[n] for n in range(len(us))]
        else:
            t = {c: dram(f"w_{name}_{c}", np.stack([u for u in us if u.shape[1] == c])) for c in widths}
            at = dict.fromkeys(widths, 0)
            t_w[name] = []
            for u in us:
                c = u.shape[1]
                t_w[name].append(t[c][at[c]])
                at[c] += 1
    out = nc.dram_tensor("out", (KD, P, LAT), F32, kind="ExternalOutput").ap()
    build(nc, dram("vecs", vecs), dram("mats", mats), dram("tabs", tabs), dram("rope", rope),
          dram("xt", xt), t_w, out)
    r = run_bass_kernel_spmd(nc, [arrays], core_ids=[0])
    got = np.asarray(r.results[0]["out"])
    return np.ascontiguousarray(got.reshape(D, LAT).T)[None]
```
